# Optimizing a Trainium2 kernel written in Bass

```python
import math
import jax, jax.numpy as jnp
from jax import lax
import numpy as np

D_MODEL = 1024
BATCH = 1
SEQ = 512
DEPTH = 2

CHUNK = 64
HEAD_DIM = 64
ATT_HEADS = 8
ATT_KV_HEADS = 2
ATT_GROUP = ATT_HEADS // ATT_KV_HEADS
WINDOW = 128
WINDOW_CHUNKS = WINDOW // CHUNK
ROT_DIM = HEAD_DIM // 4
ROPE_THETA = 500000.0
ATT_WIDTH = ATT_HEADS * HEAD_DIM
KV_WIDTH = ATT_KV_HEADS * HEAD_DIM
SSM_WIDTH = D_MODEL // 4
SSM_GROUP_CH = 16
SSM_GROUPS = SSM_WIDTH // SSM_GROUP_CH
SSM_STATE = 64
DT_MIN = 0.001
DT_MAX = 0.1
SGU_WIDTH = D_MODEL // 4
SGU_BLOCK = 128
SGU_GROUPS = SGU_WIDTH // HEAD_DIM
CONV_WIDTH = D_MODEL // 4
CONV_K = 3
IN_SPLITS = (ATT_WIDTH, KV_WIDTH, KV_WIDTH, SSM_WIDTH, SGU_WIDTH, SGU_WIDTH, CONV_WIDTH, CONV_WIDTH, CONV_WIDTH)
IN_WIDTH = sum(IN_SPLITS)
BRANCH_WIDTHS = (ATT_WIDTH, SSM_WIDTH, SGU_WIDTH, CONV_WIDTH)
MIX_WIDTH = sum(BRANCH_WIDTHS)
N_BRANCHES = 4
D_FF = 2816
RMS_EPS = 1e-6
LN_EPS = 1e-5

kernel_name = "hybrid_gated_streaming_encoder"

def _split(t, sizes, axis=-1):
    return jnp.split(t, np.cumsum(sizes)[:-1].tolist(), axis=axis)

def rms_norm(x, g):
    xf = x.astype(jnp.float32)
    y = xf * lax.rsqrt(jnp.mean(xf * xf, axis=-1, keepdims=True) + RMS_EPS)
    return (y * g.astype(jnp.float32)).astype(x.dtype)

def swiglu(x, w1, w3, w2):
    return (jax.nn.silu(x @ w1) * (x @ w3)) @ w2

def partial_rope(x, positions):
    xf = x.astype(jnp.float32)
    rot, rest = xf[..., :ROT_DIM], xf[..., ROT_DIM:]
    inv_freq = ROPE_THETA ** (-jnp.arange(0, ROT_DIM, 2, dtype=jnp.float32) / ROT_DIM)
    ang = positions.astype(jnp.float32)[..., None] * inv_freq
    cos, sin = jnp.cos(ang)[:, :, None, :], jnp.sin(ang)[:, :, None, :]
    x1, x2 = rot[..., :ROT_DIM // 2], rot[..., ROT_DIM // 2:]
    out = jnp.concatenate([x1 * cos - x2 * sin, x2 * cos + x1 * sin, rest], axis=-1)
    return out.astype(x.dtype)

def _shift_chunks(t, j):
    if j == 0:
        return t
    pad = [(0, 0)] * t.ndim
    pad[1] = (j, 0)
    return jnp.pad(t, pad)[:, :-j]

def sliding_window_attention(q, k, v, sinks):
    bsz, seq = q.shape[0], q.shape[1]
    n_chunks = seq // CHUNK
    qc = q.reshape(bsz, n_chunks, CHUNK, ATT_KV_HEADS, ATT_GROUP, HEAD_DIM)
    kc = k.reshape(bsz, n_chunks, CHUNK, ATT_KV_HEADS, HEAD_DIM)
    vc = v.reshape(bsz, n_chunks, CHUNK, ATT_KV_HEADS, HEAD_DIM)
    back = range(WINDOW_CHUNKS - 1, -1, -1)
    kb = jnp.concatenate([_shift_chunks(kc, j) for j in back], axis=2)
    vb = jnp.concatenate([_shift_chunks(vc, j) for j in back], axis=2)
    key_back = jnp.repeat(jnp.arange(WINDOW_CHUNKS - 1, -1, -1), CHUNK)
    valid = jnp.arange(n_chunks)[:, None] >= key_back[None, :]
    scores = jnp.einsum('bcqkgd,bcskd->bckgqs', qc, kb).astype(jnp.float32) * (HEAD_DIM ** -0.5)
    scores = jnp.where(valid[None, :, None, None, None, :], scores, -jnp.inf)
    sink = sinks.astype(jnp.float32).reshape(ATT_KV_HEADS, ATT_GROUP)[None, None, :, :, None, None]
    sink = jnp.broadcast_to(sink, scores.shape[:-1] + (1,))
    probs = jax.nn.softmax(jnp.concatenate([scores, sink], axis=-1), axis=-1)[..., :-1]
    out = jnp.einsum('bckgqs,bcskd->bcqkgd', probs.astype(v.dtype), vb)
    return out.reshape(bsz, seq, ATT_WIDTH)

def s5_branch(u, a_re, a_im, log_dt, b_re, b_im, c_re, c_im, d, w_glu):
    bsz, seq = u.shape[0], u.shape[1]
    uf = u.astype(jnp.float32).reshape(bsz, seq, SSM_GROUPS, SSM_GROUP_CH)
    a = lax.complex(a_re.astype(jnp.float32), a_im.astype(jnp.float32))
    dt = jnp.exp(log_dt.astype(jnp.float32))[:, None]
    a_bar = jnp.exp(a * dt)
    b = lax.complex(b_re.astype(jnp.float32), b_im.astype(jnp.float32))
    b_bar = ((a_bar - 1.0) / a)[:, :, None] * b
    c = lax.complex(c_re.astype(jnp.float32), c_im.astype(jnp.float32))
    bu = jnp.einsum('bsgc,gpc->bsgp', uf.astype(jnp.complex64), b_bar)
    decay = jnp.broadcast_to(a_bar, bu.shape)

    def combine(left, right):
        a_l, h_l = left
        a_r, h_r = right
        return a_l * a_r, a_r * h_l + h_r

    _, h = lax.associative_scan(combine, (decay, bu), axis=1)
    y = jnp.real(jnp.einsum('bsgp,gcp->bsgc', h, c)) + d.astype(jnp.float32).reshape(SSM_GROUPS, SSM_GROUP_CH) * uf
    y = jax.nn.gelu(y.reshape(bsz, seq, SSM_WIDTH)).astype(u.dtype)
    return y * jax.nn.sigmoid(y @ w_glu)

def spatial_gating(u, v, ln_g, ln_b, w_s, b_s):
    bsz, seq = u.shape[0], u.shape[1]
    u = jax.nn.gelu(u)
    vf = jax.nn.gelu(v).astype(jnp.float32)
    mu = jnp.mean(vf, axis=-1, keepdims=True)
    var = jnp.mean(jnp.square(vf - mu), axis=-1, keepdims=True)
    vn = ((vf - mu) * lax.rsqrt(var + LN_EPS) * ln_g.astype(jnp.float32) + ln_b.astype(jnp.float32)).astype(v.dtype)
    vb = vn.reshape(bsz, seq // SGU_BLOCK, SGU_BLOCK, SGU_GROUPS, HEAD_DIM)
    pos_chunk = jnp.arange(SGU_BLOCK) // CHUNK
    mask = pos_chunk[:, None] >= pos_chunk[None, :]
    w = jnp.where(mask[None], w_s, jnp.zeros_like(w_s))
    mixed = jnp.einsum('gij,bnjgd->bnigd', w, vb) + b_s.T[None, None, :, :, None]
    return u * mixed.reshape(bsz, seq, SGU_WIDTH)

def short_conv(xin, gate_b, gate_c, conv_w):
    h = gate_c * xin
    h = lax.conv_general_dilated(h, conv_w[:, None, :], window_strides=(1,), padding=[(CONV_K - 1, 0)],
                                 dimension_numbers=('NWC', 'WIO', 'NWC'), feature_group_count=CONV_WIDTH)
    return gate_b * h

def hybrid_mixer(xn, positions, w_in, sinks, a_re, a_im, log_dt, b_re, b_im, c_re, c_im, d, w_glu,
                 ln_g, ln_b, w_s, b_s, conv_w, w_branch, w_gate, b_gate, w_out):
    bsz, seq = xn.shape[0], xn.shape[1]
    q, k, v, u_ssm, sgu_u, sgu_v, c_x, c_b, c_c = _split(xn @ w_in, IN_SPLITS)
    q = partial_rope(q.reshape(bsz, seq, ATT_HEADS, HEAD_DIM), positions)
    k = partial_rope(k.reshape(bsz, seq, ATT_KV_HEADS, HEAD_DIM), positions)
    v = v.reshape(bsz, seq, ATT_KV_HEADS, HEAD_DIM)
    branches = (
        sliding_window_attention(q, k, v, sinks),
        s5_branch(u_ssm, a_re, a_im, log_dt, b_re, b_im, c_re, c_im, d, w_glu),
        spatial_gating(sgu_u, sgu_v, ln_g, ln_b, w_s, b_s),
        short_conv(c_x, c_b, c_c, conv_w),
    )
    w_rows = _split(w_branch, BRANCH_WIDTHS, axis=0)
    merged = jnp.zeros_like(xn)
    for i in range(N_BRANCHES):
        gate = jax.nn.sigmoid(xn @ w_gate[:, i] + b_gate[i])
        merged = merged + gate * (branches[i] @ w_rows[i])
    return merged @ w_out

def setup_inputs(seed: int = 0) -> dict:
    key = jax.random.key(seed)
    ks = jax.random.split(key, 32)
    f32 = jnp.float32

    def normal(k, shape, scale):
        return jax.random.normal(k, shape, f32) * scale

    x = normal(ks[0], (BATCH, SEQ, D_MODEL), 1.0)
    offset = jax.random.randint(ks[1], (BATCH, 1), 0, 16, dtype=jnp.int32) * CHUNK
    positions = (offset + jnp.arange(SEQ, dtype=jnp.int32)[None, :]).astype(jnp.int32)
    n = jnp.arange(SSM_STATE, dtype=f32)
    return {
        "x": x,
        "positions": positions,
        "norm_gains": 1.0 + normal(ks[2], (DEPTH, 6, D_MODEL), 0.05),
        "ffn_w1": normal(ks[3], (DEPTH, 2, D_MODEL, D_FF), D_MODEL ** -0.5),
        "ffn_w3": normal(ks[4], (DEPTH, 2, D_MODEL, D_FF), D_MODEL ** -0.5),
        "ffn_w2": normal(ks[5], (DEPTH, 2, D_FF, D_MODEL), D_FF ** -0.5),
        "w_in": normal(ks[6], (DEPTH, D_MODEL, IN_WIDTH), D_MODEL ** -0.5),
        "attn_sinks": normal(ks[7], (DEPTH, ATT_HEADS), 0.5),
        "ssm_a_re": -0.5 + normal(ks[8], (DEPTH, SSM_GROUPS, SSM_STATE), 0.01),
        "ssm_a_im": math.pi * n + normal(ks[9], (DEPTH, SSM_GROUPS, SSM_STATE), 0.01),
        "ssm_log_dt": jax.random.uniform(ks[10], (DEPTH, SSM_GROUPS), f32, math.log(DT_MIN), math.log(DT_MAX)),
        "ssm_b_re": normal(ks[11], (DEPTH, SSM_GROUPS, SSM_STATE, SSM_GROUP_CH), (2 * SSM_GROUP_CH) ** -0.5),
        "ssm_b_im": normal(ks[12], (DEPTH, SSM_GROUPS, SSM_STATE, SSM_GROUP_CH), (2 * SSM_GROUP_CH) ** -0.5),
        "ssm_c_re": normal(ks[13], (DEPTH, SSM_GROUPS, SSM_GROUP_CH, SSM_STATE), SSM_STATE ** -0.5),
        "ssm_c_im": normal(ks[14], (DEPTH, SSM_GROUPS, SSM_GROUP_CH, SSM_STATE), SSM_STATE ** -0.5),
        "ssm_d": normal(ks[15], (DEPTH, SSM_WIDTH), 0.5),
        "ssm_glu_w": normal(ks[16], (DEPTH, SSM_WIDTH, SSM_WIDTH), SSM_WIDTH ** -0.5),
        "sgu_ln_g": 1.0 + normal(ks[17], (DEPTH, SGU_WIDTH), 0.05),
        "sgu_ln_b": normal(ks[18], (DEPTH, SGU_WIDTH), 0.02),
        "sgu_w": normal(ks[19], (DEPTH, SGU_GROUPS, SGU_BLOCK, SGU_BLOCK), SGU_BLOCK ** -0.5),
        "sgu_b": 1.0 + normal(ks[20], (DEPTH, SGU_GROUPS, SGU_BLOCK), 0.05),
        "conv_w": normal(ks[21], (DEPTH, CONV_K, CONV_WIDTH), CONV_K ** -0.5),
        "w_branch": normal(ks[22], (DEPTH, MIX_WIDTH, D_MODEL), MIX_WIDTH ** -0.5),
        "w_gate": normal(ks[23], (DEPTH, D_MODEL, N_BRANCHES, D_MODEL), D_MODEL ** -0.5),
        "b_gate": normal(ks[24], (DEPTH, N_BRANCHES, D_MODEL), 0.02),
        "w_out": normal(ks[25], (DEPTH, D_MODEL, D_MODEL), D_MODEL ** -0.5),
    }

def reference(x, positions, norm_gains, ffn_w1, ffn_w3, ffn_w2, w_in, attn_sinks,
              ssm_a_re, ssm_a_im, ssm_log_dt, ssm_b_re, ssm_b_im, ssm_c_re, ssm_c_im, ssm_d, ssm_glu_w,
              sgu_ln_g, sgu_ln_b, sgu_w, sgu_b, conv_w, w_branch, w_gate, b_gate, w_out):
    for l in range(DEPTH):
        g = norm_gains[l]
        h = swiglu(rms_norm(x, g[0]), ffn_w1[l, 0], ffn_w3[l, 0], ffn_w2[l, 0])
        x = x + 0.5 * rms_norm(h, g[1])
        h = hybrid_mixer(rms_norm(x, g[2]), positions, w_in[l], attn_sinks[l],
                         ssm_a_re[l], ssm_a_im[l], ssm_log_dt[l], ssm_b_re[l], ssm_b_im[l],
                         ssm_c_re[l], ssm_c_im[l], ssm_d[l], ssm_glu_w[l],
                         sgu_ln_g[l], sgu_ln_b[l], sgu_w[l], sgu_b[l], conv_w[l],
                         w_branch[l], w_gate[l], b_gate[l], w_out[l])
        x = x + rms_norm(h, g[3])
        h = swiglu(rms_norm(x, g[4]), ffn_w1[l, 1], ffn_w3[l, 1], ffn_w2[l, 1])
        x = x + 0.5 * rms_norm(h, g[5])
    return x


_drawn_inputs = setup_inputs


def setup_inputs(seed=0):
    import zlib

    import numpy as np

    out = dict(_drawn_inputs(seed))
    spreads = {}
    factors = {'attn_sinks': 47.052,
     'ssm_a_re': 64.0,
     'ssm_a_im': 23.392,
     'ssm_log_dt': 25.032,
     'ssm_b_re': 32.48,
     'ssm_b_im': 32.832,
     'ssm_c_re': 32.208,
     'ssm_c_im': 32.464,
     'sgu_ln_g': 2.683,
     'sgu_ln_b': 6.942,
     'b_gate': 6.86,
     'ssm_glu_w': 3.551,
     'sgu_b': 3.28}
    for name, (base, spread) in spreads.items():
        noise = np.random.default_rng([zlib.crc32(name.encode()), seed]).standard_normal(out[name].shape)
        drawn = base * np.exp(spread * noise) if base else spread * noise
        out[name] = __import__('jax').numpy.asarray(drawn.astype(out[name].dtype))
    for name, factor in factors.items():
        out[name] = (out[name] * factor).astype(out[name].dtype)
    return out
```

```python
from contextlib import ExitStack

import numpy as np

import concourse.bass as bass
from concourse import mybir

F32 = mybir.dt.float32
F32R = mybir.dt.float32r
I32 = mybir.dt.int32
ALU = mybir.AluOpType
ACT = mybir.ActivationFunctionType
AX = mybir.AxisListType

P = 128
DEPTH, SEQ, D_MODEL, D_FF = 2, 512, 1024, 2816
KD = D_MODEL // P
KF = D_FF // P
KF2 = KF // 2
TB = SEQ // P
CHUNK, HEAD_DIM, N_WIN = 64, 64, SEQ // 64
ROT_DIM, ROPE_THETA = 16, 500000.0
RMS_EPS, LN_EPS = 1e-6, 1e-5
N_STATE_TILES = 8

CONV, SGU, ATT, SSM = range(4)
REF_BRANCH = (3, 2, 0, 1)
BRANCH_K = (2, 2, 4, 2)
BRANCH_ROW0 = (1024, 768, 0, 512)

W_IN_COLS = {"ssm": 768, "sgu_v": 1280, "sgu_u": 1024, "k": 512, "v": 640, "q": 0,
             "cx": 1536, "cb": 1792, "cc": 2048}
W_IN_TILES = [("ssm", 0), ("ssm", 1), ("sgu_v", 0), ("sgu_v", 1), ("sgu_u", 0), ("sgu_u", 1), ("k", 0), ("v", 0),
              ("q", 0), ("q", 1), ("q", 2), ("q", 3),
              ("cx", 0), ("cc", 0), ("cb", 0), ("cx", 1), ("cc", 1), ("cb", 1)]
N_IN = len(W_IN_TILES)

SLOT = 12 * P
UP_CH, DOWN_CH, IN_CH, MIX_CH, OUT_CH = 2 * KF, 2 * KD, N_IN, 4 * KD, KD
C_UP = (0, UP_CH + DOWN_CH + IN_CH + MIX_CH + OUT_CH)
C_DOWN = (UP_CH, C_UP[1] + UP_CH)
C_IN = UP_CH + DOWN_CH
C_MIX = C_IN + IN_CH
C_OUT = C_MIX + MIX_CH
CHUNKS = C_DOWN[1] + DOWN_CH
A_UP = (0, KF + KD + N_IN + 4 * KD + KD)
A_DOWN = (KF, A_UP[1] + KF)
A_IN = KF + KD
A_MIX = A_IN + N_IN
A_OUT = A_MIX + 4 * KD
STEPS = A_DOWN[1] + KD
N_NORMS = 6
W8, W11 = KD * P, KF2 * P
MIX_W = [(KD + k) * P for k in BRANCH_K]

T_SGU_TURN, T_SGU_MIX, T_ROPE, T_WINDOWS, T_ATT, T_GLU = 6, 9, 12, 16, 17, 37


def ssm_start(j):
    return 3 + 4 * j


def att_group(t):
    return (t - T_ATT) // 2 if t >= T_ATT and (t - T_ATT) % 2 == 0 and (t - T_ATT) // 2 < N_WIN else None


PC_GAIN, PC_BGATE, PC_ARE, PC_AIM, PC_LDT, PC_D, PC_CONV, PC_SINK, PC_N = 0, 48, 80, 88, 96, 104, 106, 112, 116

TWO_PI = 2 * np.pi
C1 = 6.28125
C2 = float(np.float32(np.round((TWO_PI - C1) * 2**20) / 2**20))
C3 = float(np.float32(TWO_PI - C1 - C2))
C23 = float(np.float32(TWO_PI - C1))
PI_F = 3.1415925
MAGIC = 1.5 * 2**23
LN2_HI = 0.693359375
LN2_LO = float(np.float32(np.log(2.0) - LN2_HI))


def build_encoder(nc, x_in, pos_in, params_in, w_up, w_down, w_in, w_conv, w_sgu, w_att, w_ssm, w_out,
                  ssm_b, ssm_c, glu_w, sgu_w, sgu_bias, ln_rows, ident_in, rot_in, invf_in, time_in, out):
    mix_dram = (w_conv, w_sgu, w_att, w_ssm)
    base = (nc.sbuf_base + 63) // 64 * 64

    with ExitStack() as ctx:
        def sem(name):
            return ctx.enter_context(nc.semaphore(name))

        def bank(name):
            return ctx.enter_context(nc.psum_tensor(name, [P, SEQ], F32))

        top = [base]

        def place(name, shape, dt=F32, at=None):
            size = 4 * int(np.prod(shape[1:]))
            off = at
            if at is None:
                off = top[0]
                top[0] += (size + 31) // 32 * 32
            return nc.alloc_sbuf_tensor_at(name, shape, dt, offset=off)

        x = place("x", [P, KD, SEQ])
        w_raw = place("w_raw", [P, 2, SLOT])
        w_hi = place("w_hi", [P, 2, SLOT], F32R)
        w_lo = place("w_lo", [P, 2, SLOT], F32R)
        at_xhi = top[0]
        x_hi = place("x_hi", [P, KD, SEQ], F32R)
        x_lo = place("x_lo", [P, KD, SEQ], F32R)
        h_out = place("h_out", [P, KD, SEQ], at=at_xhi)
        rstd = place("rstd", [P, SEQ])
        sq_sum = place("sq_sum", [P, SEQ])
        at_sq = top[0]
        sq = place("sq", [P, 2, SEQ])
        gate_in = place("gate_in", [P, 2, SEQ], at=at_sq)
        ident = place("ident", [P, P])
        rot = place("rot", [P, P])
        ones = place("ones", [P, P])
        at_diag = top[0]
        diag = place("diag", [P, TB, P])
        time_f = place("time_f", [P, SEQ], at=at_diag)
        params_all = place("params_all", [P, DEPTH, PC_N])
        prm = place("prm", [P, PC_N])
        invf = place("invf", [P, 1])
        mean_sq = place("mean_sq", [P, TB])
        rs = place("rs", [P, TB])
        minus_half = place("minus_half", [P, TB])
        region = top[0]

        hid_hi = place("hid_hi", [P, KF, SEQ], F32R)
        hid_lo = place("hid_lo", [P, KF, SEQ], F32R)
        up_a = place("up_a", [P, 2, SEQ])
        up_b = place("up_b", [P, 2, SEQ])
        up_s = place("up_s", [P, 2, SEQ])
        up_h = place("up_h", [P, 2, SEQ])
        assert top[0] <= nc.sbuf_usable_end
        top[0] = region
        at_merged = top[0]
        conv3 = place("conv3", [P, 3, SEQ])
        conv_pad = place("conv_pad", [P, SEQ + 8])
        rope_c = place("rope_c", [P, SEQ])
        rope_s = place("rope_s", [P, SEQ])
        rope_pos = nc.alloc_sbuf_tensor_at("rope_pos", [P, SEQ], I32, offset=top[0] - 4 * SEQ)
        sgu_v = place("sgu_v", [P, 2, SEQ])
        merged = place("merged", [P, KD, SEQ], at=at_merged)
        at_z = top[0]
        q = place("q", [P, N_WIN, 4, CHUNK])
        att_hi = place("att_hi", [P, N_WIN, 4, CHUNK], F32R, at=at_z)
        k_pad = place("k_pad", [P, CHUNK + SEQ])
        v_pad = place("v_pad", [P, CHUNK + SEQ])
        u_ssm = place("u_ssm", [P, 2, SEQ])
        sgu_u = place("sgu_u", [P, 2, SEQ])
        sgu_hi = place("sgu_hi", [P, 2, SEQ], F32R)
        sgu_lo = place("sgu_lo", [P, 2, SEQ], F32R)
        v_win = place("v_win", [P, N_WIN, P])
        assert top[0] - at_z >= 2 * 4 * KD * SEQ
        mrg_hi = place("mrg_hi", [P, KD, SEQ], F32R, at=at_z)
        mrg_lo = place("mrg_lo", [P, KD, SEQ], F32R, at=at_z + 4 * KD * SEQ)
        at_conv = top[0]
        conv_hi = place("conv_hi", [P, 2, SEQ], F32R)
        conv_lo = place("conv_lo", [P, 2, SEQ], F32R)
        ssm_hi = place("ssm_hi", [P, 2, SEQ], F32R, at=at_conv)
        ssm_lo = place("ssm_lo", [P, 2, SEQ], F32R, at=at_conv + 8 * SEQ)
        att_lo = place("att_lo", [P, N_WIN, 4, CHUNK], F32R)
        v_tok = place("v_tok", [P, TB, 2 * P])
        att_e = place("att_e", [P, 4, P])
        att_pt = place("att_pt", [P, 4, P])
        tab_c = place("tab_c", [P, SEQ])
        tab_s = place("tab_s", [P, SEQ])
        tab_w = place("tab_w", [P, SEQ])
        tab_k = place("tab_k", [P, SEQ])
        st_re = place("st_re", [P, SEQ])
        st_im = place("st_im", [P, SEQ])
        rt_re = place("rt_re", [P, SEQ])
        rt_im = place("rt_im", [P, SEQ])
        prod = place("prod", [P, SEQ])
        gate = place("gate", [P, 2, SEQ])
        wb = place("wb", [P, 2, 2, P])
        wc = place("wc", [P, 2, N_STATE_TILES, 32])
        wc2 = place("wc2", [P, 2, N_STATE_TILES, 32])
        wglu = place("wglu", [P, 2, 2 * P])
        wsgu = place("wsgu", [P, 4, P])
        bsgu = place("bsgu", [P, 2, P])
        lnr = place("lnr", [P, 2, 2 * P])
        sm = place("sm", [P, 12, N_STATE_TILES])
        y_hi = place("y_hi", [P, N_STATE_TILES], F32R)
        smi = nc.alloc_sbuf_tensor_at("smi", [P, N_STATE_TILES], I32, offset=top[0])
        top[0] += 32
        lnst = place("lnst", [P, TB, 6])
        lnmv = place("lnmv", [P, TB, 2])
        lnrs = place("lnrs", [P, TB])
        asm = place("asm", [P, 6, 4])
        assert top[0] <= nc.sbuf_usable_end, (top[0], nc.sbuf_usable_end)
        SM_DT, SM_ER, SM_Y, SM_YLO, SM_KR, SM_KI, SM_T0, SM_T1, SM_T2, SM_T3, SM_T4, SM_T5 = range(12)

        acc = [[bank("acc00"), bank("acc01")], [bank("acc10"), bank("acc11")]]
        ps_y, ps_v, ps6, ps7 = bank("ps_y"), bank("ps_v"), bank("ps6"), bank("ps7")

        raw_landed = [sem("raw_landed0"), sem("raw_landed1")]
        hi_made = sem("hi_made")
        lo_made = sem("lo_made")
        chunk_done = sem("chunk_done")
        acc_free = sem("acc_free")
        consts_landed = sem("consts_landed")
        small_landed = sem("small_landed")
        time_landed = sem("time_landed")
        x_landed = sem("x_landed")
        set_up = sem("set_up")
        x_new = sem("x_new")
        xhi_made = sem("xhi_made")
        xlo_made = sem("xlo_made")
        tmp_made = sem("tmp_made")
        sq_made = sem("sq_made")
        sq_added = sem("sq_added")
        sums_made = sem("sums_made")
        mean_made = sem("mean_made")
        rs_made = sem("rs_made")
        diag_made = sem("diag_made")
        rstd_spread = sem("rstd_spread")
        rstd_made = sem("rstd_made")
        prm_ready = sem("prm_ready")
        a_made = sem("a_made")
        b_made = acc_free
        silu_made = sem("silu_made")
        hid_made = sem("hid_made")
        hid_hi_made = sem("hid_hi_made")
        hid_lo_made = sem("hid_lo_made")
        h_made = sem("h_made")
        gate_scaled = sem("gate_scaled")
        gate_made = sem("gate_made")
        gated = sem("gated")
        merged_added = sem("merged_added")
        mrg_hi_made = sem("mrg_hi_made")
        mrg_lo_made = sem("mrg_lo_made")
        u_ready = sem("u_ready")
        sgu_z = sem("sgu_z")
        sgu_g = sem("sgu_g")
        sgu_turned = sem("sgu_turned")
        sgu_var = sem("sgu_var")
        sgu_rs = sem("sgu_rs")
        sgu_normed = sem("sgu_normed")
        sgu_mixed = sem("sgu_mixed")
        sgu_done = sem("sgu_done")
        sgu_hi_made = sem("sgu_hi_made")
        sgu_lo_made = sem("sgu_lo_made")
        rope_ang = sem("rope_ang")
        rope_sin = sem("rope_sin")
        qk_ready = sem("qk_ready")
        rotated = sem("rotated")
        roped = sem("roped")
        win_turned = sem("win_turned")
        win_ready = sem("win_ready")
        conv_done = sem("conv_done")
        conv_hi_made = sem("conv_hi_made")
        conv_lo_made = sem("conv_lo_made")
        scored = sem("scored")
        shifted = sem("shifted")
        exped = sem("exped")
        probs_made = sem("probs_made")
        turned = sem("turned")
        pt_made = sem("pt_made")
        att_out = sem("att_out")
        att_hi_made = sem("att_hi_made")
        att_lo_made = sem("att_lo_made")
        dt_arg = sem("dt_arg")
        dt_sin = sem("dt_sin")
        ssm_prep = sem("ssm_prep")
        tab_arg = sem("tab_arg")
        tab_sin = sem("tab_sin")
        tab_made = sem("tab_made")
        v_mul = sem("v_mul")
        v_out = sem("v_out")
        rt_made = sem("rt_made")
        scanned = sem("scanned")
        st_made = sem("st_made")
        y_mul = sem("y_mul")
        y_out = sem("y_out")
        y_gelu = sem("y_gelu")
        glu_mul = sem("glu_mul")
        glu_sig = sem("glu_sig")
        ssm_out = sem("ssm_out")
        ssm_hi_made = sem("ssm_hi_made")
        ssm_lo_made = sem("ssm_lo_made")
        stored = sem("stored")

        block = ctx.enter_context(nc.Block())

        @block.sync
        def _(sp):
            sp.dma_start(x[:], x_in).then_inc(x_landed, 16)
            for dst, src in ((ident, ident_in), (rot, rot_in), (invf, invf_in), (params_all, params_in)):
                sp.dma_start(dst[:], src).then_inc(consts_landed, 16)

            def load(c, u, width, src):
                sp.wait_ge(lo_made, c + 1)
                sp.dma_start(w_raw[:, u, 0:width], src).then_inc(raw_landed[u], 16)

            def load_phase(c0, n, width, dram, row0):
                with sp.Fori(0, n // 2) as i:
                    for u in range(2):
                        load(c0 + 2 * i + u, u, width, dram[row0 + 2 * i + u])

            with sp.Fori(0, DEPTH) as l:
                c = l * CHUNKS
                load_phase(c + C_UP[0], UP_CH, W8, w_up, l * 2 * UP_CH)
                load_phase(c + C_DOWN[0], DOWN_CH, W11, w_down, l * 2 * DOWN_CH)
                sp.wait_ge(chunk_done, c + C_IN + 2)
                for dst, dram in ((wb, ssm_b), (wc, ssm_c), (wglu, glu_w), (wsgu, sgu_w), (bsgu, sgu_bias)):
                    sp.dma_start(dst[:], dram[l]).then_inc(small_landed, 16)
                for r in range(2):
                    sp.dma_start(lnr[:, r, :], ln_rows[l, r:r + 1, :].partition_broadcast(P)).then_inc(small_landed, 16)
                sp.dma_start(rope_pos[:], pos_in.partition_broadcast(P)).then_inc(small_landed, 16)
                load_phase(c + C_IN, IN_CH, W8, w_in, l * IN_CH)
                for b in range(4):
                    load_phase(c + C_MIX + KD * b, KD, MIX_W[b], mix_dram[b], l * KD)
                load_phase(c + C_OUT, OUT_CH, W8, w_out, l * OUT_CH)
                load_phase(c + C_UP[1], UP_CH, W8, w_up, l * 2 * UP_CH + UP_CH)
                load_phase(c + C_DOWN[1], DOWN_CH, W11, w_down, l * 2 * DOWN_CH + DOWN_CH)
            for k in range(KD):
                sp.wait_ge(x_new, 3 * KD * DEPTH + k + 1)
                sp.dma_start(out[:, k, :], x[:, k, :]).then_inc(stored, 16)
            sp.wait_ge(stored, 16 * KD)

        @block.tensor
        def _(pe):
            def product(ps, slot, blk, hi, lo, start, stop):
                wh = w_hi[:, slot, blk * P:(blk + 1) * P]
                pe.matmul(ps[:], wh, hi, start=start, stop=False)
                pe.matmul(ps[:], wh, lo, start=False, stop=False)
                return pe.matmul(ps[:], w_lo[:, slot, blk * P:(blk + 1) * P], hi, start=False, stop=stop)

            def chunk_ready(c):
                pe.wait_ge(lo_made, c + 3)

            def norm_sums(n):
                pe.wait_ge(sq_added, 7 * (n + 1))
                for b in range(TB):
                    mm = pe.matmul(ps6[:, b:b + 1], sq_sum[:, b * P:(b + 1) * P], ones[:, 0:1], start=True, stop=True)
                mm.then_inc(sums_made, 1)

            def norm_spread(n):
                pe.wait_ge(diag_made, n + 1)
                pe.matmul(ps7[:], ones[:], diag[:].rearrange("p b n -> p (b n)"), start=True, stop=True)\
                  .then_inc(rstd_spread, 1)

            def up_step(c, a, u, xr, extra=None):
                pe.wait_ge(acc_free, a + 1)
                for part in range(2):
                    chunk_ready(c + part)
                    for k in range(KD):
                        if xr is not None and part == 0:
                            pe.wait_ge(xlo_made, xr + k + 1)
                        mm = product(acc[u][part], part, k, x_hi[:, k, :], x_lo[:, k, :], k == 0, k == KD - 1)
                    mm.then_inc(chunk_done, 1)
                    if extra is not None:
                        extra(part)

            def ffn(l, f):
                c, a = l * CHUNKS + C_UP[f], l * STEPS + A_UP[f]
                xr = l * 3 * KD + 2 * KD * f
                n = l * N_NORMS + 4 * f
                up_step(c, a, 0, xr)
                norm_sums(n)
                up_step(c + 2, a + 1, 1, None, lambda part: norm_spread(n) if part == 0 else None)
                with pe.Fori(1, KF // 2) as i:
                    for u in range(2):
                        up_step(c + 4 * i + 2 * u, a + 2 * i + u, u, None)
                c, a = l * CHUNKS + C_DOWN[f], l * STEPS + A_DOWN[f]
                hid = (2 * l + f) * KF
                with pe.Fori(0, KD // 2) as i:
                    for u in range(2):
                        pe.wait_ge(acc_free, a + 2 * i + u + 1)
                        for part in range(2):
                            chunk_ready(c + 4 * i + 2 * u + part)
                            pe.wait_ge(hid_lo_made, hid + KF2 * (part + 1))
                            for b in range(KF2):
                                k = KF2 * part + b
                                mm = product(acc[u][0], part, b, hid_hi[:, k, :], hid_lo[:, k, :], k == 0, k == KF - 1)
                            mm.then_inc(chunk_done, 1)
                norm_sums(n + 1)
                norm_spread(n + 1)

            with pe.Fori(0, DEPTH) as l:
                ffn(l, 0)

                def sgu_turn():
                    pe.wait_ge(sgu_g, 4 * l + 2)
                    for b in range(TB):
                        for t in range(2):
                            mm = pe.transpose((ps6, ps7)[b // 2][:, (b % 2 * 2 + t) * P:(b % 2 * 2 + t + 1) * P],
                                              sgu_v[:, t, b * P:(b + 1) * P], ident[:])
                    mm.then_inc(sgu_turned, 1)

                def sgu_mix():
                    pe.wait_ge(sgu_normed, l + 1)
                    for t in range(2):
                        for b in range(TB):
                            for g in range(2):
                                h = 2 * t + g
                                mm = pe.matmul((ps6, ps7)[t][64 * g:64 * g + 64, b * P:(b + 1) * P],
                                               v_tok[:, b, 64 * h:64 * h + 64], wsgu[:, h, :], start=True, stop=True)
                    mm.then_inc(sgu_mixed, 1)

                def rotate(i):
                    pe.wait_ge(qk_ready, 6 * l + (1 if i == 0 else 2 + i))
                    pe.wait_ge(sgu_done, 2 * l + 2)
                    if i >= 2:
                        pe.wait_ge(roped, 5 * l + i - 1)
                    src = k_pad[:, CHUNK:] if i == 0 else q[:, :, i - 1, :]
                    pe.matmul((ps6, ps7)[i % 2][:], rot[:], src, start=True, stop=True).then_inc(rotated, 1)

                def windows():
                    pe.wait_ge(roped, 5 * l + 5)
                    for half in range(2):
                        for w in range(4):
                            c = 4 * half + w
                            mm = pe.transpose((ps6, ps7)[half][:, w * P:(w + 1) * P],
                                              v_pad[:, CHUNK * c:CHUNK * c + P], ident[:])
                        mm.then_inc(win_turned, 1)

                def scores(c):
                    if c == 0:
                        pe.wait_ge(win_ready, 2 * l + 2)
                    else:
                        pe.wait_ge(shifted, N_WIN * l + c)
                    for kv in range(2):
                        if kv:
                            pe.drain()
                        for pair in range(2):
                            j = 2 * kv + pair
                            mm = pe.matmul(ps6[:, j * P:(j + 1) * P],
                                           q[64 * kv:64 * kv + 64, c, 2 * pair:2 * pair + 2, :].rearrange("p a b -> p (a b)"),
                                           k_pad[64 * kv:64 * kv + 64, CHUNK * c:CHUNK * c + P], start=True, stop=True)
                    mm.then_inc(scored, 1)

                def turn_probs(c):
                    pe.wait_ge(probs_made, N_WIN * l + c + 1)
                    if c:
                        pe.wait_ge(att_lo_made, N_WIN * l + c)
                    for j in range(4):
                        mm = pe.transpose(ps7[:, j * P:(j + 1) * P], att_e[:, j, :], ident[:])
                    mm.then_inc(turned, 1)

                def attend(c):
                    pe.wait_ge(pt_made, N_WIN * l + c + 1)
                    for kv in range(2):
                        mm = pe.matmul(ps7[64 * kv:64 * kv + 64, 0:2 * P], v_win[:, c, 64 * kv:64 * kv + 64],
                                       att_pt[:, 2 * kv:2 * kv + 2, :].rearrange("p a b -> p (a b)"),
                                       start=True, stop=True)
                    mm.then_inc(att_out, 1)

                def ssm_in(j, part):
                    if j == 0 and part == 0:
                        pe.wait_ge(small_landed, 128 * l + 128)
                        pe.wait_ge(u_ready, 2 * l + 2)
                    if j or part:
                        pe.wait_ge(v_out, 16 * l + 2 * j + part)
                    r = 32 * (j % 4)
                    pe.matmul(ps_v[:], wb[r:r + 32, j // 4, part, :], u_ssm[r:r + 32, j // 4, :],
                              start=True, stop=True).then_inc(v_mul, 1)

                def ssm_y(j):
                    pe.wait_ge(st_made, N_STATE_TILES * l + j + 1)
                    if j == 4:
                        pe.wait_ge(y_out, 2 * l + 1)
                    r = 32 * (j % 4)
                    pe.matmul(ps_y[r:r + 32, :], wc2[:, 0, j, :], rt_re[:], start=True, stop=False)
                    pe.matmul(ps_y[r:r + 32, :], wc2[:, 1, j, :], rt_im[:], start=False, stop=True).then_inc(y_mul, 1)

                def glu():
                    pe.wait_ge(y_gelu, 2 * l + 2)
                    pe.wait_ge(att_lo_made, N_WIN * (l + 1))
                    for m in range(2):
                        for k in range(2):
                            mm = pe.matmul((ps6, ps7)[m][:], wglu[:, k, m * P:(m + 1) * P], u_ssm[:, k, :],
                                           start=(k == 0), stop=(k == 1))
                        mm.then_inc(glu_mul, 1)

                def side_work(t):
                    for j in range(N_STATE_TILES):
                        if t == ssm_start(j) + 4:
                            ssm_y(j)
                    for j in range(N_STATE_TILES):
                        if t in (ssm_start(j), ssm_start(j) + 1):
                            ssm_in(j, t - ssm_start(j))
                    if t == T_SGU_TURN:
                        sgu_turn()
                    if t == T_SGU_MIX:
                        sgu_mix()
                    if T_ROPE <= t < T_ROPE + 3:
                        for i in range(2 * (t - T_ROPE), min(2 * (t - T_ROPE) + 2, 5)):
                            rotate(i)
                    if t == T_WINDOWS:
                        windows()
                    if att_group(t - 2) is not None:
                        attend(att_group(t - 2))
                    if att_group(t) is not None:
                        scores(att_group(t))
                    if att_group(t - 1) is not None:
                        turn_probs(att_group(t - 1))
                    if t == T_GLU:
                        glu()

                n = l * N_NORMS + 2
                for s in range(N_IN):
                    if s >= 2:
                        side_work(s)
                    c, a = l * CHUNKS + C_IN + s, l * STEPS + A_IN + s
                    pe.wait_ge(acc_free, a + 1)
                    chunk_ready(c)
                    for k in range(KD):
                        if s == 0:
                            pe.wait_ge(xlo_made, l * 3 * KD + KD + k + 1)
                        mm = product(acc[s % 2][0], s % 2, k, x_hi[:, k, :], x_lo[:, k, :], k == 0, k == KD - 1)
                    mm.then_inc(chunk_done, 1)
                    if s == 1:
                        norm_sums(n)
                        norm_spread(n)

                parts = ((conv_hi, conv_lo), (sgu_hi, sgu_lo), (att_hi, att_lo), (ssm_hi, ssm_lo))

                def mix_step(b, c, a, u):
                    pe.wait_ge(acc_free, a + 1)
                    chunk_ready(c)
                    for k in range(KD):
                        product(acc[u][0], u, k, x_hi[:, k, :], x_lo[:, k, :], k == 0, k == KD - 1)
                    for s, count in ((conv_lo_made, 2), (sgu_lo_made, 2), (att_lo_made, N_WIN), (ssm_lo_made, 2))[b:b + 1]:
                        pe.wait_ge(s, count * l + count)
                    hi, lo = parts[b]
                    for k in range(BRANCH_K[b]):
                        at = (slice(None), slice(None), k) if b == ATT else (slice(None), k)
                        mm = product(acc[u][1], u, KD + k, hi[at], lo[at], k == 0, k == BRANCH_K[b] - 1)
                    mm.then_inc(chunk_done, 1)

                for b in range(3):
                    for s in range(KD):
                        t = N_IN + KD * b + s
                        side_work(t)
                        mix_step(b, l * CHUNKS + C_MIX + KD * b + s, l * STEPS + A_MIX + KD * b + s, s % 2)
                with pe.Fori(0, KD // 2) as i:
                    for u in range(2):
                        s = 3 * KD + 2 * i + u
                        mix_step(SSM, l * CHUNKS + C_MIX + s, l * STEPS + A_MIX + s, u)

                with pe.Fori(0, KD // 2) as i:
                    for u in range(2):
                        pe.wait_ge(mrg_lo_made, KD * l + KD)
                        pe.wait_ge(acc_free, l * STEPS + A_OUT + 2 * i + u + 1)
                        chunk_ready(l * CHUNKS + C_OUT + 2 * i + u)
                        for k in range(KD):
                            mm = product(acc[u][0], u, k, mrg_hi[:, k, :], mrg_lo[:, k, :], k == 0, k == KD - 1)
                        mm.then_inc(chunk_done, 1)
                norm_sums(l * N_NORMS + 3)
                norm_spread(l * N_NORMS + 3)
                ffn(l, 1)

        @block.scalar
        def _(act):
            def upper(c, c0, u, width):
                act.wait_ge(raw_landed[u], 8 * (c - u) + 16)
                act.wait_ge(chunk_done, c + 1)
                act.activation(w_hi[:, u, 0:width], w_raw[:, u, 0:width], ACT.Copy).then_inc(hi_made, 1)

            def square(n, k, src):
                if k == 0:
                    act.activation(sq_sum[:], src, ACT.Square).then_inc(sq_made, 1)
                    return
                if k >= 3:
                    act.wait_ge(sq_added, 7 * n + k - 2)
                act.activation(sq[:, k % 2, :], src, ACT.Square).then_inc(sq_made, 1)

            def x_upper(l, r):
                for k in range(KD):
                    g = PC_GAIN + 2 * KD * r + k
                    act.wait_ge(x_new, 3 * KD * l + KD * r + k + 1)
                    act.activation(x_hi[:, k, :], x[:, k, :], ACT.Copy, scale=prm[:, g:g + 1]).then_inc(xhi_made, 1)
                    square(l * N_NORMS + 2 * r, k, x[:, k, :])

            def up_step(l, f, m, u, next_w):
                c, h = l * CHUNKS + C_UP[f] + 2 * m, (2 * l + f) * KF + m
                upper(c + 2, 0, 0, next_w)
                act.wait_ge(a_made, h + 1)
                act.activation(up_s[:, u, :], up_a[:, u, :], ACT.Silu).then_inc(silu_made, 1)
                upper(c + 3, 0, 1, next_w)
                act.wait_ge(hid_made, h + 1)
                act.activation(hid_hi[:, bass.ds(m, 1), :], up_h[:, u:u + 1, :], ACT.Copy).then_inc(hid_hi_made, 1)

            def ffn(l, f):
                with act.Fori(0, KF // 2 - 1) as i:
                    for u in range(2):
                        up_step(l, f, 2 * i + u, u, W8)
                up_step(l, f, KF - 2, 0, W8)
                up_step(l, f, KF - 1, 1, W11)
                for n in range(KD):
                    c = l * CHUNKS + C_DOWN[f] + 2 * n
                    next_w = W11 if n < KD - 1 else (W8 if f == 0 else 0)
                    if next_w:
                        upper(c + 2, 0, 0, next_w)
                    act.wait_ge(h_made, 3 * KD * l + 2 * KD * f + n + 1)
                    square(l * N_NORMS + 4 * f + 1, n, h_out[:, n, :])
                    if next_w:
                        upper(c + 3, 0, 1, next_w)

            with act.Fori(0, DEPTH) as l:
                act.wait_ge(prm_ready, l + 1)
                for u in range(2):
                    upper(l * CHUNKS + u, 0, u, W8)
                x_upper(l, 0)
                ffn(l, 0)
                x_upper(l, 1)

                def side_work(t):
                    if t == 2:
                        act.wait_ge(rstd_made, l * N_NORMS + 3)
                        act.dma_start(time_f[:], time_in).then_inc(time_landed, 16)
                        act.wait_ge(dt_arg, l + 1)
                        act.activation(sm[:, SM_T0, :], sm[:, SM_Y, :], ACT.Sin)
                        act.activation(sm[:, SM_T1, :], sm[:, SM_Y, :], ACT.Sin, scale=0.5).then_inc(dt_sin, 1)
                    for j in range(N_STATE_TILES):
                        g = N_STATE_TILES * l + j
                        t0 = ssm_start(j)
                        if t in (t0, t0 + 1):
                            part = t - t0
                            if j:
                                act.wait_ge(y_mul, g)
                            act.wait_ge(v_mul, 2 * g + part + 1)
                            act.activation((st_re, st_im)[part][:], ps_v[:], ACT.Copy).then_inc(v_out, 1)
                        if t == t0:
                            act.wait_ge(tab_arg, g + 1)
                            act.activation(tab_s[:], tab_w[:], ACT.Sin)
                            act.activation(tab_c[:], tab_w[:], ACT.Sin, scale=0.5)
                            act.drain()
                            act.activation(tab_c[:], tab_c[:], ACT.Square).then_inc(tab_sin, 1)
                    for i, at in enumerate((2, 3, 4, 5)):
                        if t == at:
                            z = (sgu_v if i < 2 else sgu_u)[:, i % 2, :]
                            act.wait_ge(sgu_z, 4 * l + i + 1)
                            act.activation(z, z, ACT.Gelu_apprx_tanh).then_inc(sgu_g, 1)
                    if t == T_SGU_MIX + 1:
                        for i in range(2):
                            act.wait_ge(sgu_done, 2 * l + i + 1)
                            act.activation(sgu_hi[:, i, :], sgu_u[:, i, :], ACT.Copy).then_inc(sgu_hi_made, 1)
                    if t == 8:
                        act.wait_ge(rope_ang, l + 1)
                        act.activation(rope_s[:], rope_c[:], ACT.Sin)
                        act.drain()
                        act.activation(rope_c[:], rope_c[:], ACT.Sin, scale=0.5)
                        act.drain()
                        act.activation(rope_c[:], rope_c[:], ACT.Square).then_inc(rope_sin, 1)
                    if t in (14, 17):
                        i = (t - 14) // 3
                        act.wait_ge(conv_done, 2 * l + i + 1)
                        act.activation(conv_hi[:, i, :], conv3[:, 0, :], ACT.Copy).then_inc(conv_hi_made, 1)
                    if t == T_WINDOWS:
                        for half in range(2):
                            act.wait_ge(win_turned, 2 * l + half + 1)
                            act.activation(v_win[:, 4 * half:4 * half + 4, :].rearrange("p a b -> p (a b)"),
                                           (ps6, ps7)[half][:], ACT.Copy).then_inc(win_ready, 1)
                    c = att_group(t)
                    if c is not None:
                        g = N_WIN * l + c
                        act.wait_ge(shifted, g + 1)
                        keys = att_e[:, :, CHUNK:] if c == 0 else att_e[:]
                        act.activation(keys, keys, ACT.Exp)
                        act.activation(asm[:, 3, :], asm[:, 2, :], ACT.Exp).then_inc(exped, 1)
                    c = att_group(t - 1)
                    if c is not None:
                        g = N_WIN * l + c
                        act.wait_ge(turned, g + 1)
                        act.activation(att_pt[:].rearrange("p a b -> p (a b)"), ps7[:], ACT.Copy).then_inc(pt_made, 1)
                    c = att_group(t - 2)
                    if c is not None:
                        g = N_WIN * l + c
                        act.wait_ge(att_out, g + 1)
                        act.activation(att_hi[:, c],
                                       ps7[:, 0:2 * P].rearrange("p (t q) -> p t q", t=4), ACT.Copy)\
                           .then_inc(att_hi_made, 1)
                    for i in range(2):
                        if t == ssm_start(4 * i + 3) + 4:
                            act.wait_ge(y_out, 2 * l + i + 1)
                            act.activation(u_ssm[:, i, :], u_ssm[:, i, :], ACT.Gelu_apprx_tanh).then_inc(y_gelu, 1)
                    if t == T_GLU:
                        for i in range(2):
                            act.wait_ge(glu_mul, 2 * l + i + 1)
                            act.activation((st_re, st_im)[i][:], (ps6, ps7)[i][:], ACT.Sigmoid).then_inc(glu_sig, 1)
                        for i in range(2):
                            act.wait_ge(ssm_out, 2 * l + i + 1)
                            act.activation(ssm_hi[:, i, :], u_ssm[:, i, :], ACT.Copy).then_inc(ssm_hi_made, 1)

                for s in range(N_IN):
                    upper(l * CHUNKS + C_IN + s + 2, 0, s % 2, W8 if s < N_IN - 2 else MIX_W[0])
                    side_work(s)

                for s in range(4 * KD):
                    b, n, u = s // KD, s % KD, s % 2
                    nb = (s + 2) // KD
                    upper(l * CHUNKS + C_MIX + s + 2, 0, u, MIX_W[nb] if nb < 4 else W8)
                    if s > KD + 1:
                        act.wait_ge(merged_added, 3 * KD * l + s - KD - 1)
                    bg = PC_BGATE + s
                    act.wait_ge(gate_scaled, 4 * KD * l + s + 1)
                    act.activation(gate[:, u, :], gate_in[:, u, :], ACT.Sigmoid, bias=prm[:, bg:bg + 1])\
                       .then_inc(gate_made, 1)
                    if b == SSM:
                        act.wait_ge(merged_added, 3 * KD * l + s - KD + 1)
                        act.activation(mrg_hi[:, n, :], merged[:, n, :], ACT.Copy).then_inc(mrg_hi_made, 1)
                    side_work(N_IN + s)
                for n in range(KD):
                    upper(l * CHUNKS + C_OUT + n + 2, 0, n % 2, W8)
                    act.wait_ge(h_made, 3 * KD * l + KD + n + 1)
                    square(l * N_NORMS + 3, n, h_out[:, n, :])
                x_upper(l, 2)
                ffn(l, 1)

        @block.gpsimd
        def _(pool):
            pool.wait_ge(set_up, 1)

            def add_squares(n, k):
                pool.wait_ge(sq_made, 8 * n + k + 1)
                pool.tensor_tensor(sq_sum[:], sq_sum[:], sq[:, k % 2, :], ALU.add).then_inc(sq_added, 1)
                pool.drain()

            def inverse_root(n):
                pool.wait_ge(mean_made, n + 1)
                pool.tensor_tensor(rs[:], mean_sq[:], minus_half[:], ALU.pow).then_inc(rs_made, 1)

            def norm(n):
                for k in range(1, KD):
                    add_squares(n, k)
                inverse_root(n)

            def ffn(l, f):
                norm(l * N_NORMS + 4 * f)
                with pool.Fori(0, KF // 2) as i:
                    for u in range(2):
                        h = (2 * l + f) * KF + 2 * i + u
                        pool.wait_ge(silu_made, h + 1)
                        pool.wait_ge(b_made, l * STEPS + A_UP[f] + 2 * i + u + 3)
                        pool.tensor_tensor(up_h[:, u, :], up_s[:, u, :], up_b[:, u, :], ALU.mult).then_inc(hid_made, 1)
                norm(l * N_NORMS + 4 * f + 1)

            with pool.Fori(0, DEPTH) as l:
                ffn(l, 0)
                norm(l * N_NORMS + 2)

                def turn(out_re, out_im, re, im, sign):
                    pool.tensor_tensor(out_re[:], tab_c[:], re[:], ALU.mult)
                    pool.tensor_tensor(prod[:], tab_s[:], im[:], ALU.mult)
                    pool.drain()
                    pool.tensor_tensor(out_re[:], out_re[:], prod[:], ALU.subtract if sign > 0 else ALU.add)
                    pool.drain()
                    pool.tensor_tensor(out_im[:], tab_c[:], im[:], ALU.mult)
                    pool.tensor_tensor(prod[:], tab_s[:], re[:], ALU.mult)
                    pool.drain()
                    return pool.tensor_tensor(out_im[:], out_im[:], prod[:], ALU.add if sign > 0 else ALU.subtract)

                for t in range(N_IN + 4 * KD):
                    for j in range(N_STATE_TILES):
                        g = N_STATE_TILES * l + j
                        if t == ssm_start(j) + 1:
                            pool.wait_ge(tab_made, g + 1)
                            pool.wait_ge(v_out, 2 * g + 2)
                            turn(rt_re, rt_im, st_re, st_im, -1).then_inc(rt_made, 1)
                        if t == ssm_start(j) + 2:
                            pool.wait_ge(scanned, g + 1)
                            turn(rt_re, rt_im, st_re, st_im, 1).then_inc(st_made, 1)
                    if t == T_SGU_TURN:
                        pool.wait_ge(sgu_var, l + 1)
                        pool.tensor_tensor(lnrs[:], lnrs[:], minus_half[:], ALU.pow).then_inc(sgu_rs, 1)
                    if t == T_GLU:
                        for i in range(2):
                            pool.wait_ge(glu_sig, 2 * l + i + 1)
                            pool.tensor_tensor(u_ssm[:, i, :], u_ssm[:, i, :], (st_re, st_im)[i][:], ALU.mult)\
                                .then_inc(ssm_out, 1)
                    if t >= N_IN + KD:
                        s = t - N_IN
                        pool.wait_ge(gated, 4 * KD * l + s + 1)
                        pool.tensor_tensor(merged[:, s % KD, :], merged[:, s % KD, :], gate[:, s % 2, :], ALU.add)\
                            .then_inc(merged_added, 1)
                norm(l * N_NORMS + 3)
                ffn(l, 1)

        @block.vector
        def _(dve):
            dve.memset(ones[:], 1.0)
            dve.memset(minus_half[:], -0.5).then_inc(set_up, 1)
            dve.memset(mean_sq[:], 0.0).then_inc(lo_made, 2)
            dve.memset(rs[:], 0.0).then_inc(chunk_done, 2)
            dve.memset(diag[:, 0, 0:8], 0.0).then_inc(acc_free, 2)
            dve.wait_ge(x_landed, 16)
            dve.memset(lnrs[:], 1.0).then_inc(x_new, KD)
            dve.wait_ge(consts_landed, 64)
            dve.drain()

            def lower(c, u, width):
                dve.wait_ge(hi_made, c + 1)
                dve.tensor_tensor(w_lo[:, u, 0:width], w_raw[:, u, 0:width], w_hi[:, u, 0:width].bitcast(F32),
                                  ALU.subtract).then_inc(lo_made, 1)

            def norm_scale(n):
                dve.wait_ge(sums_made, n + 1)
                dve.tensor_scalar(mean_sq[:], ps6[:, 0:TB], 1.0 / D_MODEL, RMS_EPS, ALU.mult, ALU.add)\
                   .then_inc(mean_made, 1)
                dve.wait_ge(rs_made, n + 1)
                dve.tensor_tensor(diag[:], ident[:].unsqueeze(1).to_broadcast([P, TB, P]),
                                  rs[:].unsqueeze(2).to_broadcast([P, TB, P]), ALU.mult).then_inc(diag_made, 1)
                dve.wait_ge(rstd_spread, n + 1)
                dve.tensor_copy(rstd[:], ps7[:]).then_inc(rstd_made, 1)
                dve.drain()

            def x_lower(l, r, k):
                g = PC_GAIN + 2 * KD * r + k
                dve.wait_ge(xhi_made, 3 * KD * l + KD * r + k + 1)
                dve.scalar_tensor_tensor(x_lo[:, k, :], x[:, k, :], prm[:, g:g + 1], x_hi[:, k, :].bitcast(F32),
                                         ALU.mult, ALU.subtract).then_inc(xlo_made, 1)

            def residual(l, p, split):
                def scale(k):
                    g = PC_GAIN + KD * (2 * p + 1) + k
                    dve.scalar_tensor_tensor(h_out[:, k, :], h_out[:, k, :], prm[:, g:g + 1], rstd[:],
                                             ALU.mult, ALU.mult).then_inc(tmp_made, 1)
                scale(0)
                for k in range(KD):
                    if k + 1 < KD:
                        scale(k + 1)
                    dve.wait_ge(tmp_made, 3 * KD * l + KD * p + k + 1)
                    dve.tensor_tensor(x[:, k, :], x[:, k, :], h_out[:, k, :], ALU.add).then_inc(x_new, 1)
                    if split and k:
                        x_lower(l, p + 1, k - 1)
                if split:
                    x_lower(l, p + 1, KD - 1)

            def up_out(l, f, m, u, part):
                src = acc[u][part]
                dve.wait_ge(chunk_done, l * CHUNKS + C_UP[f] + 2 * m + part + 3)
                ins = dve.tensor_tensor((up_a, up_b)[part][:, u, :], src[:], rstd[:], ALU.mult)
                ins.then_inc((a_made, acc_free)[part], 1)

            def up_step(l, f, m, u, next_w, norm=None):
                c, h = l * CHUNKS + C_UP[f] + 2 * m, (2 * l + f) * KF + m
                if norm is not None:
                    lower(c + 2, 0, next_w)
                    norm_scale(norm)
                up_out(l, f, m, u, 0)
                if norm is None:
                    lower(c + 2, 0, next_w)
                up_out(l, f, m, u, 1)
                lower(c + 3, 1, next_w)
                dve.wait_ge(hid_hi_made, h + 1)
                dve.tensor_tensor(hid_lo[:, bass.ds(m, 1), :], up_h[:, u:u + 1, :],
                                  hid_hi[:, bass.ds(m, 1), :].bitcast(F32), ALU.subtract).then_inc(hid_lo_made, 1)

            def out_tile(l, p, n, c_last, u):
                dve.wait_ge(chunk_done, c_last + 3)
                dve.tensor_copy(h_out[:, n, :], acc[u][0][:]).then_inc(h_made, 1)
                dve.wait_ge(h_made, 3 * KD * l + KD * p + n + 1)
                dve.sem_inc(acc_free, 1)

            def ffn(l, f):
                up_step(l, f, 0, 0, W8, l * N_NORMS + 4 * f)
                up_step(l, f, 1, 1, W8)
                with dve.Fori(1, KF // 2 - 1) as i:
                    for u in range(2):
                        up_step(l, f, 2 * i + u, u, W8)
                up_step(l, f, KF - 2, 0, W8)
                up_step(l, f, KF - 1, 1, W11)
                for n in range(KD):
                    c = l * CHUNKS + C_DOWN[f] + 2 * n
                    next_w = W11 if n < KD - 1 else (W8 if f == 0 else 0)
                    if next_w:
                        lower(c + 2, 0, next_w)
                    out_tile(l, 2 * f, n, c + 1, n % 2)
                    if next_w:
                        lower(c + 3, 1, next_w)
                norm_scale(l * N_NORMS + 4 * f + 1)

            def accurate_exp(dst, src, t0, t1, t2):
                V = dve
                V.tensor_scalar(t0, src, -87.3, 88.0, ALU.max, ALU.min)
                V.drain()
                V.tensor_scalar(t1, t0, float(np.log2(np.e)), MAGIC, ALU.mult, ALU.add)
                V.drain()
                V.tensor_scalar(t1, t1, MAGIC, None, ALU.subtract)
                V.drain()
                V.scalar_tensor_tensor(t0, t1, -LN2_HI, t0, ALU.mult, ALU.add)
                V.drain()
                V.scalar_tensor_tensor(t0, t1, -LN2_LO, t0, ALU.mult, ALU.add)
                V.tensor_scalar(smi[:], t1, 127.0, None, ALU.add)
                V.drain()
                V.tensor_scalar(smi[:], smi[:], 23, None, ALU.logical_shift_left)
                V.memset(t2, 1.0 / 40320)
                fact = [5040.0, 720.0, 120.0, 24.0, 6.0, 2.0, 1.0, 1.0]
                for q_ in fact:
                    V.drain()
                    V.tensor_tensor(t2, t2, t0, ALU.mult)
                    V.drain()
                    V.tensor_scalar(t2, t2, 1.0 / q_, None, ALU.add)
                V.tensor_scalar(t1, src, -87.3, None, ALU.is_ge)
                V.drain()
                V.tensor_tensor(t2, t2, smi[:].bitcast(F32), ALU.mult)
                V.drain()
                V.tensor_tensor(dst, t2, t1, ALU.mult)
                V.drain()

            def turns_off(w, k, parts):
                dve.tensor_scalar(k, w, float(1 / TWO_PI), MAGIC, ALU.mult, ALU.add)
                dve.drain()
                dve.tensor_scalar(k, k, MAGIC, None, ALU.subtract)
                for part in parts:
                    dve.drain()
                    dve.scalar_tensor_tensor(w, k, -part, w, ALU.mult, ALU.add)
                dve.drain()

            with dve.Fori(0, DEPTH) as l:
                dve.tensor_copy(prm[:], params_all[:, bass.ds(l, 1), :].rearrange("p a b -> p (a b)"))
                dve.drain()
                for nrm in (1, 5):
                    a = PC_GAIN + KD * nrm
                    ins = dve.tensor_scalar(prm[:, a:a + KD], prm[:, a:a + KD], 0.5, None, ALU.mult)
                ins.then_inc(prm_ready, 1)
                dve.drain()
                for u in range(2):
                    lower(l * CHUNKS + u, u, W8)
                for k in range(KD):
                    x_lower(l, 0, k)
                ffn(l, 0)
                residual(l, 0, True)

                def S(i):
                    return sm[:, i, :]

                def state_steps():
                    accurate_exp(S(SM_DT), prm[:, PC_LDT:PC_LDT + 8], S(SM_T0), S(SM_T1), S(SM_T2))
                    dve.tensor_tensor(S(SM_T3), prm[:, PC_ARE:PC_ARE + 8], S(SM_DT), ALU.mult)
                    dve.drain()
                    accurate_exp(S(SM_ER), S(SM_T3), S(SM_T0), S(SM_T1), S(SM_T2))
                    dve.tensor_tensor(S(SM_Y), prm[:, PC_AIM:PC_AIM + 8], S(SM_DT), ALU.mult)
                    dve.drain()
                    turns_off(S(SM_Y), S(SM_T1), (C1, C2, C3))
                    dve.tensor_scalar(S(SM_Y), S(SM_Y), -PI_F, PI_F, ALU.max, ALU.min).then_inc(dt_arg, 1)
                    dve.drain()

                def state_weights():
                    are, aim = prm[:, PC_ARE:PC_ARE + 8], prm[:, PC_AIM:PC_AIM + 8]
                    dve.wait_ge(small_landed, 128 * l + 128)
                    dve.wait_ge(dt_sin, l + 1)
                    V = dve
                    V.tensor_copy(y_hi[:], S(SM_Y))
                    V.tensor_tensor(S(SM_T2), S(SM_T1), S(SM_T1), ALU.mult)
                    V.drain()
                    V.tensor_tensor(S(SM_YLO), S(SM_Y), y_hi[:].bitcast(F32), ALU.subtract)
                    V.tensor_scalar(S(SM_T2), S(SM_T2), -2.0, 1.0, ALU.mult, ALU.add)
                    V.drain()
                    V.tensor_tensor(S(SM_T2), S(SM_T2), S(SM_ER), ALU.mult)
                    V.tensor_tensor(S(SM_T0), S(SM_T0), S(SM_ER), ALU.mult)
                    V.drain()
                    V.tensor_scalar(S(SM_T2), S(SM_T2), -1.0, None, ALU.add)
                    V.tensor_tensor(S(SM_T3), are, are, ALU.mult)
                    V.tensor_tensor(S(SM_T4), aim, aim, ALU.mult)
                    V.drain()
                    V.tensor_tensor(S(SM_T3), S(SM_T3), S(SM_T4), ALU.add)
                    V.drain()
                    V.reciprocal(S(SM_T3), S(SM_T3))
                    V.tensor_tensor(S(SM_T1), S(SM_T2), are, ALU.mult)
                    V.tensor_tensor(S(SM_T4), S(SM_T0), aim, ALU.mult)
                    V.tensor_tensor(S(SM_T5), S(SM_T0), are, ALU.mult)
                    V.drain()
                    V.tensor_tensor(S(SM_T1), S(SM_T1), S(SM_T4), ALU.add)
                    V.tensor_tensor(S(SM_T2), S(SM_T2), aim, ALU.mult)
                    V.drain()
                    V.tensor_tensor(S(SM_T5), S(SM_T5), S(SM_T2), ALU.subtract)
                    V.tensor_tensor(S(SM_KR), S(SM_T1), S(SM_T3), ALU.mult)
                    V.drain()
                    V.tensor_tensor(S(SM_KI), S(SM_T5), S(SM_T3), ALU.mult)
                    V.drain()
                    kr = S(SM_KR).unsqueeze(2).to_broadcast([P, N_STATE_TILES, 32])
                    ki = S(SM_KI).unsqueeze(2).to_broadcast([P, N_STATE_TILES, 32])
                    scratch = prod_scratch
                    V.tensor_tensor(wc2[:, 0], wc[:, 0], kr, ALU.mult)
                    V.tensor_tensor(scratch, wc[:, 1], ki, ALU.mult)
                    V.tensor_tensor(wc2[:, 1], wc[:, 0], ki, ALU.mult)
                    V.drain()
                    V.tensor_tensor(wc2[:, 0], wc2[:, 0], scratch, ALU.subtract)
                    V.drain()
                    V.tensor_tensor(scratch, wc[:, 1], kr, ALU.mult)
                    V.drain()
                    V.scalar_tensor_tensor(wc2[:, 1], wc2[:, 1], -1.0, scratch, ALU.mult, ALU.subtract)
                    V.drain()

                prod_scratch = tab_k[:, 0:256].rearrange("p (a b) -> p a b", a=N_STATE_TILES)

                def tables(j):
                    g = N_STATE_TILES * l + j
                    if j == 0:
                        dve.wait_ge(time_landed, 16 * l + 16)
                    dve.tensor_scalar(tab_w[:], time_f[:], y_hi[:, j:j + 1].bitcast(F32), None, ALU.mult)
                    dve.drain()
                    turns_off(tab_w[:], tab_k[:], (C1, C23))
                    dve.scalar_tensor_tensor(tab_w[:], time_f[:], sm[:, SM_YLO, j:j + 1], tab_w[:], ALU.mult, ALU.add)
                    dve.drain()
                    dve.tensor_scalar(tab_w[:], tab_w[:], -PI_F, PI_F, ALU.max, ALU.min)
                    dve.drain()
                    if j:
                        dve.wait_ge(st_made, g)
                    dve.sem_inc(tab_arg, 1)

                def tables_end(j):
                    g = N_STATE_TILES * l + j
                    dve.wait_ge(tab_sin, g + 1)
                    dve.tensor_scalar(tab_c[:], tab_c[:], -2.0, 1.0, ALU.mult, ALU.add).then_inc(tab_made, 1)

                def scans(j):
                    g = N_STATE_TILES * l + j
                    dve.wait_ge(rt_made, g + 1)
                    decay = sm[:, SM_ER, j:j + 1].to_broadcast([P, SEQ])
                    dve.tensor_tensor_scan(st_re[:], decay, rt_re[:], 0.0, ALU.mult, ALU.add)
                    dve.tensor_tensor_scan(st_im[:], decay, rt_im[:], 0.0, ALU.mult, ALU.add).then_inc(scanned, 1)

                def sgu_norm():
                    dve.wait_ge(sgu_turned, l + 1)
                    for b in range(TB):
                        dve.tensor_copy(v_tok[:, b, :], (ps6, ps7)[b // 2][:, b % 2 * 2 * P:(b % 2 + 1) * 2 * P])
                    dve.drain()
                    for b in range(TB):
                        dve.bn_stats(lnst[:, b, :], v_tok[:, b, :])
                    dve.drain()
                    for b in range(TB):
                        dve.bn_aggr(lnmv[:, b, :], lnst[:, b, :])
                    dve.drain()
                    dve.tensor_scalar(lnrs[:], lnmv[:, :, 1], LN_EPS, None, ALU.add).then_inc(sgu_var, 1)

                def sgu_norm_end():
                    dve.wait_ge(sgu_rs, l + 1)
                    for b in range(TB):
                        dve.tensor_scalar(v_tok[:, b, :], v_tok[:, b, :], lnmv[:, b, 0:1], lnrs[:, b:b + 1],
                                          ALU.subtract, ALU.mult)
                    dve.memset(wsgu[CHUNK:P, :, 0:CHUNK], 0.0)
                    for r, op in ((0, ALU.mult), (1, ALU.add)):
                        dve.drain()
                        ins = dve.tensor_tensor(v_tok[:], v_tok[:], lnr[:, r:r + 1, :].to_broadcast([P, TB, 2 * P]), op)
                    ins.then_inc(sgu_normed, 1)

                def sgu_gate():
                    dve.wait_ge(sgu_mixed, l + 1)
                    dve.wait_ge(sgu_g, 4 * l + 4)
                    for i in range(2):
                        mixed = (ps6, ps7)[i][:].rearrange("p (b n) -> p b n", b=TB)
                        dve.tensor_tensor(sgu_v[:, i, :].rearrange("p (b n) -> p b n", b=TB), mixed,
                                          bsgu[:, i:i + 1, :].to_broadcast([P, TB, P]), ALU.add)
                        dve.drain()
                        dve.tensor_tensor(sgu_u[:, i, :], sgu_u[:, i, :], sgu_v[:, i, :], ALU.mult).then_inc(sgu_done, 1)

                def lower_of(lo, hi, full, made, value, inc):
                    dve.wait_ge(made, value)
                    dve.tensor_tensor(lo, full, hi.bitcast(F32), ALU.subtract).then_inc(inc, 1)

                def rope_angles():
                    dve.wait_ge(small_landed, 128 * l + 128)
                    dve.tensor_copy(rope_c[:], rope_pos[:])
                    dve.drain()
                    dve.tensor_scalar(rope_c[:], rope_c[:], invf[:, 0:1], None, ALU.mult)
                    dve.drain()
                    turns_off(rope_c[:], att_e[:].rearrange("p a b -> p (a b)"), (C1, C2, C3))
                    dve.tensor_scalar(rope_c[:], rope_c[:], -PI_F, PI_F, ALU.max, ALU.min).then_inc(rope_ang, 1)

                def rope(i):
                    if i == 0:
                        dve.wait_ge(rope_sin, l + 1)
                        dve.tensor_scalar(rope_c[:], rope_c[:], -2.0, 1.0, ALU.mult, ALU.add)
                        dve.drain()
                    def by_chunk(a):
                        return a.rearrange("p (c q) -> p c q", c=N_WIN)
                    z = by_chunk(k_pad[:, CHUNK:]) if i == 0 else q[:, :, i - 1, :]
                    t_ = by_chunk(att_e[:].rearrange("p a b -> p (a b)"))
                    dve.wait_ge(rotated, 5 * l + i + 1)
                    dve.tensor_tensor(t_, by_chunk((ps6, ps7)[i % 2][:]), by_chunk(rope_s[:]), ALU.mult)
                    dve.tensor_tensor(z, z, by_chunk(rope_c[:]), ALU.mult)
                    dve.drain()
                    dve.tensor_tensor(z, z, t_, ALU.add).then_inc(roped, 1)
                    dve.drain()

                def conv(i):
                    w = PC_CONV + i
                    y = conv3[:, 0, :]
                    dve.tensor_tensor(conv_pad[:, 2:2 + SEQ], conv3[:, 1, :], conv3[:, 0, :], ALU.mult)
                    dve.drain()
                    dve.tensor_scalar(y, conv_pad[:, 0:SEQ], prm[:, w:w + 1], None, ALU.mult)
                    for tap in (1, 2):
                        dve.drain()
                        dve.scalar_tensor_tensor(y, conv_pad[:, tap:tap + SEQ], prm[:, w + 2 * tap:w + 2 * tap + 1], y,
                                                 ALU.mult, ALU.add)
                    dve.drain()
                    dve.tensor_tensor(y, y, conv3[:, 2, :], ALU.mult).then_inc(conv_done, 1)

                def shift_scores(c):
                    g = N_WIN * l + c
                    k0 = CHUNK if c == 0 else 0
                    s4 = ps6[:].rearrange("p (j k) -> p j k", j=4)[:, :, k0:]
                    sink = prm[:, PC_SINK:PC_SINK + 4]
                    dve.wait_ge(scored, g + 1)
                    if c:
                        dve.wait_ge(turned, g)
                    else:
                        dve.memset(att_e[:, :, 0:CHUNK], 0.0)
                    dve.tensor_reduce(asm[:, 0, :], s4, AX.X, ALU.max)
                    dve.drain()
                    dve.scalar_tensor_tensor(asm[:, 1, :], asm[:, 0, :], HEAD_DIM ** -0.5, sink, ALU.mult, ALU.max)
                    dve.drain()
                    dve.tensor_tensor(asm[:, 2, :], sink, asm[:, 1, :], ALU.subtract)
                    dve.scalar_tensor_tensor(att_e[:, :, k0:], s4, HEAD_DIM ** -0.5,
                                             asm[:, 1, :].unsqueeze(2).to_broadcast([P, 4, P - k0]),
                                             ALU.mult, ALU.subtract).then_inc(shifted, 1)

                def make_probs(c):
                    g = N_WIN * l + c
                    dve.wait_ge(exped, g + 1)
                    dve.tensor_reduce(asm[:, 4, :], att_e[:], AX.X, ALU.add)
                    dve.drain()
                    dve.tensor_tensor(asm[:, 4, :], asm[:, 4, :], asm[:, 3, :], ALU.add)
                    dve.drain()
                    dve.reciprocal(asm[:, 5, :], asm[:, 4, :])
                    dve.drain()
                    dve.tensor_tensor(att_e[:], att_e[:], asm[:, 5, :].unsqueeze(2).to_broadcast([P, 4, P]), ALU.mult)\
                       .then_inc(probs_made, 1)

                def attention_out(c):
                    lower_of(att_lo[:, c], att_hi[:, c],
                             ps7[:, 0:2 * P].rearrange("p (t q) -> p t q", t=4), att_hi_made, N_WIN * l + c + 1,
                             att_lo_made)

                def ssm_result(i):
                    dve.wait_ge(y_mul, N_STATE_TILES * l + 4 * i + 4)
                    dve.scalar_tensor_tensor(u_ssm[:, i, :], u_ssm[:, i, :], prm[:, PC_D + i:PC_D + i + 1], ps_y[:],
                                             ALU.mult, ALU.add).then_inc(y_out, 1)

                def side_work(t):
                    if t == 0:
                        state_steps()
                    if t == 2:
                        state_weights()
                    for j in range(N_STATE_TILES):
                        t0 = ssm_start(j)
                        if t == t0 + 2:
                            scans(j)
                        if t == t0:
                            tables(j)
                            tables_end(j)
                    if t == T_SGU_TURN:
                        sgu_norm()
                        sgu_norm_end()
                    if t == T_SGU_MIX:
                        sgu_gate()
                    if t == T_SGU_MIX + 1:
                        for i in range(2):
                            lower_of(sgu_lo[:, i, :], sgu_hi[:, i, :], sgu_u[:, i, :], sgu_hi_made, 2 * l + i + 1,
                                     sgu_lo_made)
                    if t == 8:
                        rope_angles()
                    if T_ROPE <= t < T_ROPE + 3:
                        for i in range(2 * (t - T_ROPE), min(2 * (t - T_ROPE) + 2, 5)):
                            rope(i)
                    if t in (14, 17):
                        i = (t - 14) // 3
                        conv(i)
                        lower_of(conv_lo[:, i, :], conv_hi[:, i, :], conv3[:, 0, :], conv_hi_made, 2 * l + i + 1,
                                 conv_lo_made)
                    if att_group(t) is not None:
                        shift_scores(att_group(t))
                        make_probs(att_group(t))
                    if att_group(t - 2) is not None:
                        attention_out(att_group(t - 2))
                    for i in range(2):
                        if t == ssm_start(4 * i + 3) + 4:
                            ssm_result(i)
                    if t == T_GLU:
                        for i in range(2):
                            lower_of(ssm_lo[:, i, :], ssm_hi[:, i, :], u_ssm[:, i, :], ssm_hi_made, 2 * l + i + 1,
                                     ssm_lo_made)

                for pad in (k_pad, v_pad):
                    dve.memset(pad[:, 0:CHUNK], 0.0)
                dve.memset(conv_pad[:, 0:2], 0.0)
                in_place = {"ssm": (u_ssm, u_ready), "sgu_v": (sgu_v, sgu_z), "sgu_u": (sgu_u, sgu_z),
                            "k": (k_pad, qk_ready), "v": (v_pad, qk_ready), "q": (q, qk_ready)}
                for s, (name, tile) in enumerate(W_IN_TILES):
                    if name in ("k", "v"):
                        dst = in_place[name][0][:, CHUNK:]
                    elif name in in_place and name != "q":
                        dst = in_place[name][0][:, tile, :]
                    elif name != "q":
                        dst = conv3[:, ("cx", "cc", "cb").index(name), :]
                    if s == 0:
                        lower(l * CHUNKS + C_IN + 2, 0, W8)
                        norm_scale(l * N_NORMS + 2)
                    dve.drain()
                    dve.wait_ge(chunk_done, l * CHUNKS + C_IN + s + 3)
                    src, r_ = acc[s % 2][0][:], rstd[:]
                    if name == "q":
                        dst = q[:, :, tile, :]
                        src, r_ = (a.rearrange("p (c q) -> p c q", c=N_WIN) for a in (src, r_))
                    dve.tensor_tensor(dst, src, r_, ALU.mult).then_inc(acc_free, 1)
                    dve.drain()
                    if name in in_place:
                        dve.sem_inc(in_place[name][1], 1)
                    if s:
                        lower(l * CHUNKS + C_IN + s + 2, s % 2, W8 if s < N_IN - 2 else MIX_W[0])
                    side_work(s)

                for s in range(4 * KD):
                    b, n, u = s // KD, s % KD, s % 2
                    nb = (s + 2) // KD
                    g = 4 * KD * l + s
                    dve.wait_ge(chunk_done, l * CHUNKS + C_MIX + s + 3)
                    dve.tensor_tensor(gate_in[:, u, :], acc[u][0][:], rstd[:], ALU.mult).then_inc(gate_scaled, 1)
                    lower(l * CHUNKS + C_MIX + s + 2, u, MIX_W[nb] if nb < 4 else W8)
                    dve.drain()
                    dve.wait_ge(gate_made, g + 1)
                    dst = merged[:, n, :] if b == CONV else gate[:, u, :]
                    dve.tensor_tensor(dst, gate[:, u, :], acc[u][1][:], ALU.mult).then_inc(gated, 1)
                    dve.wait_ge(gated, g + 1)
                    dve.sem_inc(acc_free, 1)
                    if b == SSM:
                        lower_of(mrg_lo[:, n, :], mrg_hi[:, n, :], merged[:, n, :], mrg_hi_made, KD * l + n + 1,
                                 mrg_lo_made)
                    side_work(N_IN + s)
                for n in range(KD):
                    out_tile(l, 1, n, l * CHUNKS + C_OUT + n, n % 2)
                    lower(l * CHUNKS + C_OUT + n + 2, n % 2, W8)
                norm_scale(l * N_NORMS + 3)
                residual(l, 1, True)
                ffn(l, 1)
                residual(l, 2, False)


def _tiles(w, k):
    lead = w.shape[:-2]
    n = w.shape[-1] // P
    w = w.reshape(*lead, k, P, n, P)
    m = len(lead)
    w = w.transpose(*range(m), m + 2, m + 1, m, m + 3)
    return np.ascontiguousarray(w).reshape(*lead, n, P, k * P)


def _columns(v):
    v = v.reshape(*v.shape[:-1], v.shape[-1] // P, P)
    return np.moveaxis(v, -1, 0)


def _layout(x, positions, norm_gains, ffn_w1, ffn_w3, ffn_w2, w_in, attn_sinks, ssm_a_re, ssm_a_im, ssm_log_dt,
            ssm_b_re, ssm_b_im, ssm_c_re, ssm_c_im, ssm_d, ssm_glu_w, sgu_ln_g, sgu_ln_b, sgu_w, sgu_b, conv_w,
            w_branch, w_gate, b_gate, w_out):
    L = DEPTH
    head_order = np.array([64 * (4 * kv + t) + d for t in range(4) for kv in range(2) for d in range(64)])
    cols = []
    for name, tile in W_IN_TILES:
        base = W_IN_COLS[name]
        own = head_order if name == "q" else np.arange(2 * P)
        cols.append(base + own[tile * P:(tile + 1) * P])
    win = _tiles(w_in[:, :, np.concatenate(cols)], KD).reshape(L * N_IN, P, W8)
    up = np.stack([_tiles(ffn_w1, KD), _tiles(ffn_w3, KD)], axis=3).reshape(L * 2 * UP_CH, P, W8)
    down = _tiles(ffn_w2, KF).reshape(L, 2, KD, P, 2, W11).transpose(0, 1, 2, 4, 3, 5)
    down = np.ascontiguousarray(down).reshape(L * 2 * DOWN_CH, P, W11)
    mix = []
    for b in range(4):
        rows = BRANCH_ROW0[b] + (head_order if b == ATT else np.arange(BRANCH_K[b] * P))
        g = _tiles(w_gate[:, :, REF_BRANCH[b], :], KD)
        w = _tiles(w_branch[:, rows, :], BRANCH_K[b])
        mix.append(np.concatenate([g, w], axis=-1).reshape(L * KD, P, MIX_W[b]))
    prm = np.zeros((P, L, PC_N), np.float32)
    prm[:, :, PC_GAIN:PC_GAIN + 48] = _columns(norm_gains).reshape(P, L, 48)
    prm[:, :, PC_BGATE:PC_BGATE + 32] = _columns(b_gate[:, list(REF_BRANCH), :]).reshape(P, L, 32)
    for col, a in ((PC_ARE, ssm_a_re), (PC_AIM, ssm_a_im), (PC_LDT, np.repeat(ssm_log_dt[:, :, None], 64, axis=2))):
        prm[:, :, col:col + 8] = _columns(a.reshape(L, 1024))
    prm[:, :, PC_D:PC_D + 2] = _columns(ssm_d)
    prm[:, :, PC_CONV:PC_CONV + 6] = _columns(conv_w).reshape(P, L, 6)
    sink = attn_sinks.reshape(L, 2, 2, 2).transpose(3, 0, 1, 2).reshape(2, L, 4)
    prm[:, :, PC_SINK:PC_SINK + 4] = np.repeat(sink, 64, axis=0)
    sb = np.zeros((L, P, 2, 2, P), np.float32)
    sc = np.zeros((L, P, 2, N_STATE_TILES, 32), np.float32)
    for g in range(16):
        j, h = g // 2, g % 2
        r = 32 * (j % 4) + 16 * h
        for part, (b, c) in enumerate(((ssm_b_re, ssm_c_re), (ssm_b_im, ssm_c_im))):
            sb[:, r:r + 16, j // 4, part, 64 * h:64 * h + 64] = b[:, g].transpose(0, 2, 1)
            sc[:, 64 * h:64 * h + 64, part, j, 16 * h:16 * h + 16] = c[:, g].transpose(0, 2, 1)
    glu = np.ascontiguousarray(ssm_glu_w.reshape(L, 2, P, 2 * P).transpose(0, 2, 1, 3))
    sgw = np.ascontiguousarray(sgu_w.transpose(0, 3, 1, 2))
    sgb = np.repeat(sgu_b.reshape(L, 2, 2, P).transpose(0, 2, 1, 3), 64, axis=1)
    rot = np.zeros((P, P), np.float32)
    invf = np.zeros((P, 1), np.float32)
    freq = np.float32(ROPE_THETA) ** (-np.arange(0, ROT_DIM, 2, dtype=np.float32) / ROT_DIM)
    half = ROT_DIM // 2
    for h0 in (0, HEAD_DIM):
        for i in range(half):
            rot[h0 + half + i, h0 + i] = -1.0
            rot[h0 + i, h0 + half + i] = 1.0
            invf[h0 + i] = invf[h0 + half + i] = freq[i]
    return {
        "x_in": np.ascontiguousarray(x[0].T.reshape(KD, P, SEQ).transpose(1, 0, 2)),
        "pos_in": positions,
        "params_in": prm, "w_up": up, "w_down": down, "w_in": win,
        "w_conv": mix[0], "w_sgu": mix[1], "w_att": mix[2], "w_ssm": mix[3],
        "w_out": _tiles(w_out, KD).reshape(L * OUT_CH, P, W8),
        "ssm_b": sb, "ssm_c": sc, "glu_w": glu, "sgu_w": sgw, "sgu_bias": np.ascontiguousarray(sgb),
        "ln_rows": np.stack([sgu_ln_g, sgu_ln_b], axis=1),
        "ident_in": np.eye(P, dtype=np.float32), "rot_in": rot, "invf_in": invf,
        "time_in": np.tile(np.arange(SEQ, dtype=np.float32), (P, 1)),
    }


def kernel(**inputs):
    import concourse.bacc as _bacc
    from concourse.bass_utils import run_bass_kernel_spmd as _run

    arrays = _layout(**{n: np.asarray(a) for n, a in inputs.items()})
    nc = _bacc.Bacc("TRN2", target_bir_lowering=False, num_devices=1)
    aps = {n: nc.dram_tensor(n, a.shape, mybir.dt.from_np(a.dtype), kind="ExternalInput").ap()
           for n, a in arrays.items()}
    out = nc.dram_tensor("out", (P, KD, SEQ), F32, kind="ExternalOutput").ap()
    build_encoder(nc, **aps, out=out)
    got = _run(nc, [arrays], core_ids=[0]).results[0]["out"]
    return np.ascontiguousarray(got.transpose(1, 0, 2).reshape(D_MODEL, SEQ).T)[None]
```

```python
from contextlib import ExitStack

import numpy as np

import concourse.bass as bass
from concourse import mybir

F32 = mybir.dt.float32
F32R = mybir.dt.float32r
I32 = mybir.dt.int32
ALU = mybir.AluOpType
ACT = mybir.ActivationFunctionType
AX = mybir.AxisListType

P = 128
DEPTH, SEQ, D_MODEL, D_FF = 2, 512, 1024, 2816
KD = D_MODEL // P
KF = D_FF // P
KF2 = KF // 2
TB = SEQ // P
CHUNK, HEAD_DIM, N_WIN = 64, 64, SEQ // 64
ROT_DIM, ROPE_THETA = 16, 500000.0
RMS_EPS, LN_EPS = 1e-6, 1e-5
N_STATE_TILES = 8

CONV, SGU, ATT, SSM = range(4)
REF_BRANCH = (3, 2, 0, 1)
BRANCH_K = (2, 2, 4, 2)
BRANCH_ROW0 = (1024, 768, 0, 512)

W_IN_COLS = {"ssm": 768, "sgu_v": 1280, "sgu_u": 1024, "k": 512, "v": 640, "q": 0,
             "cx": 1536, "cb": 1792, "cc": 2048}
W_IN_TILES = [("ssm", 0), ("ssm", 1), ("sgu_v", 0), ("sgu_v", 1), ("k", 0), ("q", 0), ("q", 1), ("q", 2), ("q", 3),
              ("cx", 0), ("cc", 0), ("cb", 0), ("v", 0), ("cx", 1), ("cc", 1), ("cb", 1), ("sgu_u", 0), ("sgu_u", 1)]
N_IN = len(W_IN_TILES)

SLOT = 12 * P
UP_CH, DOWN_CH, IN_CH, MIX_CH, OUT_CH = 2 * KF, 2 * KD, N_IN, 4 * KD, KD
C_UP = (0, UP_CH + DOWN_CH + IN_CH + MIX_CH + OUT_CH)
C_DOWN = (UP_CH, C_UP[1] + UP_CH)
C_IN = UP_CH + DOWN_CH
C_MIX = C_IN + IN_CH
C_OUT = C_MIX + MIX_CH
CHUNKS = C_DOWN[1] + DOWN_CH
A_UP = (0, KF + KD + N_IN + 4 * KD + KD)
A_DOWN = (KF, A_UP[1] + KF)
A_IN = KF + KD
A_MIX = A_IN + N_IN
A_OUT = A_MIX + 4 * KD
STEPS = A_DOWN[1] + KD
N_NORMS = 6
W8, W11 = KD * P, KF2 * P
MIX_W = [(KD + k) * P for k in BRANCH_K]

T_SGU_TURN, T_SGU_MIX, T_SGU_GATE, T_WINDOWS, T_ATT, T_GLU = 5, 14, 18, 15, 16, 39
T_ROPE = {8: (0, 1), 10: (2, 3), 13: (4,)}
T_SSM = {5 + 4 * j: j for j in range(N_STATE_TILES)}
T_ANGLES = {max(t - 5, 2): j for t, j in T_SSM.items()}
POOL_TURNS_FROM = 3
T_SSM_OUT = {5 + 4 * (4 * i + 3) + 3: i for i in range(2)}
T_CONV = {11: 0, 15: 1}


def att_group(t):
    return (t - T_ATT) // 2 if t >= T_ATT and (t - T_ATT) % 2 == 0 and (t - T_ATT) // 2 < N_WIN else None


PC_GAIN, PC_BGATE, PC_ARE, PC_AIM, PC_LDT, PC_D, PC_CONV, PC_SINK, PC_N = 0, 48, 80, 88, 96, 104, 106, 112, 116

TWO_PI = 2 * np.pi
C1 = 6.28125
C2 = float(np.float32(np.round((TWO_PI - C1) * 2**20) / 2**20))
C3 = float(np.float32(TWO_PI - C1 - C2))
C23 = float(np.float32(TWO_PI - C1))
PI_F = 3.1415925
MAGIC = 1.5 * 2**23
LN2_HI = 0.693359375
LN2_LO = float(np.float32(np.log(2.0) - LN2_HI))


def build_encoder(nc, x_in, pos_in, params_in, w_up, w_down, w_in, w_conv, w_sgu, w_att, w_ssm, w_out,
                  ssm_b, ssm_c, glu_w, sgu_w, sgu_bias, ln_rows, ident_in, rot_in, invf_in, time_in, out):
    mix_dram = (w_conv, w_sgu, w_att, w_ssm)
    base = (nc.sbuf_base + 63) // 64 * 64

    with ExitStack() as ctx:
        def sem(name):
            return ctx.enter_context(nc.semaphore(name))

        def bank(name):
            return ctx.enter_context(nc.psum_tensor(name, [P, SEQ], F32))

        top = [base]

        def place(name, shape, dt=F32, at=None):
            size = 4 * int(np.prod(shape[1:]))
            off = at
            if at is None:
                off = top[0]
                top[0] += (size + 31) // 32 * 32
            return nc.alloc_sbuf_tensor_at(name, shape, dt, offset=off)

        x = place("x", [P, KD, SEQ])
        w_raw = place("w_raw", [P, 2, SLOT])
        w_hi = place("w_hi", [P, 2, SLOT], F32R)
        w_lo = place("w_lo", [P, 2, SLOT], F32R)
        at_xhi = top[0]
        x_hi = place("x_hi", [P, KD, SEQ], F32R)
        x_lo = place("x_lo", [P, KD, SEQ], F32R)
        h_out = place("h_out", [P, KD, SEQ], at=at_xhi)
        rstd = place("rstd", [P, SEQ])
        sq_sum = place("sq_sum", [P, SEQ])
        at_sq = top[0]
        sq = place("sq", [P, 2, SEQ])
        gate_in = place("gate_in", [P, 2, SEQ], at=at_sq)
        ident = place("ident", [P, P])
        rot = place("rot", [P, P])
        ones = place("ones", [P, P])
        at_diag = top[0]
        diag = place("diag", [P, TB, P])
        time_f = place("time_f", [P, SEQ], at=at_diag)
        params_all = place("params_all", [P, DEPTH, PC_N])
        prm = place("prm", [P, PC_N])
        invf = place("invf", [P, 1])
        mean_sq = place("mean_sq", [P, TB])
        rs = place("rs", [P, TB])
        minus_half = place("minus_half", [P, TB])
        region = top[0]

        hid_hi = place("hid_hi", [P, KF, SEQ], F32R)
        hid_lo = place("hid_lo", [P, KF, SEQ], F32R)
        up_a = place("up_a", [P, 2, SEQ])
        up_b = place("up_b", [P, 2, SEQ])
        up_s = place("up_s", [P, 2, SEQ])
        up_h = place("up_h", [P, 2, SEQ])
        ffn_end = top[0]
        assert ffn_end <= nc.sbuf_usable_end
        top[0] = region
        at_merged = top[0]
        conv3 = place("conv3", [P, 3, SEQ])
        conv_pad = place("conv_pad", [P, SEQ + 8])
        rope_c = place("rope_c", [P, SEQ])
        rope_s = place("rope_s", [P, SEQ])
        rope_pos = nc.alloc_sbuf_tensor_at("rope_pos", [P, SEQ], I32, offset=top[0] - 4 * SEQ)
        sgu_v = place("sgu_v", [P, 2, SEQ])
        merged = place("merged", [P, KD, SEQ], at=at_merged)
        at_z = top[0]
        q = place("q", [P, N_WIN, 4, CHUNK])
        att_hi = place("att_hi", [P, N_WIN, 4, CHUNK], F32R, at=at_z)
        k_pad = place("k_pad", [P, CHUNK + SEQ])
        v_pad = place("v_pad", [P, CHUNK + SEQ])
        u_ssm = place("u_ssm", [P, 2, SEQ])
        sgu_u = place("sgu_u", [P, 2, SEQ])
        sgu_hi = place("sgu_hi", [P, 2, SEQ], F32R)
        sgu_lo = place("sgu_lo", [P, 2, SEQ], F32R)
        v_win = place("v_win", [P, N_WIN, P])
        assert top[0] - at_z >= 2 * 4 * KD * SEQ
        mrg_hi = place("mrg_hi", [P, KD, SEQ], F32R, at=at_z)
        mrg_lo = place("mrg_lo", [P, KD, SEQ], F32R, at=at_z + 4 * KD * SEQ)
        at_conv = top[0]
        conv_hi = place("conv_hi", [P, 2, SEQ], F32R)
        conv_lo = place("conv_lo", [P, 2, SEQ], F32R)
        ssm_hi = place("ssm_hi", [P, 2, SEQ], F32R, at=at_conv)
        ssm_lo = place("ssm_lo", [P, 2, SEQ], F32R, at=at_conv + 8 * SEQ)
        att_lo = place("att_lo", [P, N_WIN, 4, CHUNK], F32R)
        v_tok = place("v_tok", [P, TB, 2 * P])
        att_e = place("att_e", [P, 4, P])
        att_pt = place("att_pt", [P, 4, P])
        tab_c = place("tab_c", [P, 2, SEQ])
        tab_s = place("tab_s", [P, 2, SEQ])
        tab_k = place("tab_k", [P, SEQ])
        st_re = place("st_re", [P, SEQ])
        st_im = place("st_im", [P, SEQ])
        rt_re = place("rt_re", [P, SEQ])
        rt_im = place("rt_im", [P, SEQ])
        prod = place("prod", [P, SEQ])
        gate = place("gate", [P, 2, SEQ])
        wglu = place("wglu", [P, 2, 2 * P])
        wsgu = place("wsgu", [P, 4, P])
        bsgu = place("bsgu", [P, 2, P])
        lnr = place("lnr", [P, 2, 2 * P])
        top[0] = max(top[0], ffn_end)
        wb = place("wb", [P, 2, 2, P])
        wc = place("wc", [P, 2, N_STATE_TILES, 32])
        wc2 = place("wc2", [P, 2, N_STATE_TILES, 32])
        sm = place("sm", [P, 13, N_STATE_TILES])
        y_hi = place("y_hi", [P, N_STATE_TILES], F32R)
        smi = nc.alloc_sbuf_tensor_at("smi", [P, N_STATE_TILES], I32, offset=top[0])
        top[0] += 32
        lnst = place("lnst", [P, TB, 6])
        lnmv = place("lnmv", [P, TB, 2])
        lnrs = place("lnrs", [P, TB])
        asm = place("asm", [P, 6, 4])
        assert top[0] <= nc.sbuf_usable_end, (top[0], nc.sbuf_usable_end)
        SM_DT, SM_ER, SM_Y, SM_YLO, SM_KR, SM_KI, SM_T0, SM_T1, SM_T2, SM_T3, SM_T4, SM_T5, SM_YT = range(13)

        acc = [[bank("acc00"), bank("acc01")], [bank("acc10"), bank("acc11")]]
        ps_y, ps_v, ps6, ps7 = bank("ps_y"), bank("ps_v"), bank("ps6"), bank("ps7")

        raw_landed = [sem("raw_landed0"), sem("raw_landed1")]
        hi_made = sem("hi_made")
        lo_made = sem("lo_made")
        chunk_done = sem("chunk_done")
        acc_free = sem("acc_free")
        params_landed = sem("params_landed")
        consts_landed = sem("consts_landed")
        state_landed = sem("state_landed")
        small_landed = sem("small_landed")
        time_landed = sem("time_landed")
        x_landed = [sem(f"x_landed{k}") for k in range(KD)]
        set_up = sem("set_up")
        x_new = sem("x_new")
        xhi_made = sem("xhi_made")
        xlo_made = sem("xlo_made")
        tmp_made = sem("tmp_made")
        sq_made = sem("sq_made")
        sq_added = sem("sq_added")
        sums_made = sem("sums_made")
        mean_made = sem("mean_made")
        rs_made = sem("rs_made")
        diag_made = sem("diag_made")
        rstd_spread = sem("rstd_spread")
        rstd_made = sem("rstd_made")
        prm_ready = sem("prm_ready")
        a_made = sem("a_made")
        b_made = acc_free
        silu_made = sem("silu_made")
        hid_made = sem("hid_made")
        hid_hi_made = sem("hid_hi_made")
        hid_lo_made = sem("hid_lo_made")
        h_made = sem("h_made")
        gate_scaled = sem("gate_scaled")
        gate_made = sem("gate_made")
        gated = sem("gated")
        merged_added = sem("merged_added")
        mrg_hi_made = sem("mrg_hi_made")
        mrg_lo_made = sem("mrg_lo_made")
        u_ready = sem("u_ready")
        sgu_z = sem("sgu_z")
        sgu_g = sem("sgu_g")
        sgu_turned = sem("sgu_turned")
        sgu_var = sem("sgu_var")
        sgu_rs = sem("sgu_rs")
        sgu_scaled = sem("sgu_scaled")
        sgu_normed = sem("sgu_normed")
        sgu_biased = sem("sgu_biased")
        sgu_mixed = sem("sgu_mixed")
        sgu_done = sem("sgu_done")
        sgu_hi_made = sem("sgu_hi_made")
        sgu_lo_made = sem("sgu_lo_made")
        rope_ang = sem("rope_ang")
        rope_sin = sem("rope_sin")
        qk_ready = sem("qk_ready")
        rotated = sem("rotated")
        roped = sem("roped")
        win_turned = sem("win_turned")
        win_ready = sem("win_ready")
        conv_lo_made = sem("conv_lo_made")
        scored = sem("scored")
        shifted = sem("shifted")
        exped = sem("exped")
        probs_made = sem("probs_made")
        turned = sem("turned")
        pt_made = sem("pt_made")
        att_out = sem("att_out")
        att_lo_made = sem("att_lo_made")
        dt_arg = sem("dt_arg")
        dt_sin = sem("dt_sin")
        ssm_prep = sem("ssm_prep")
        tab_arg = sem("tab_arg")
        tab_made = sem("tab_made")
        v_mul = sem("v_mul")
        v_out = sem("v_out")
        rt_made = sem("rt_made")
        scanned = sem("scanned")
        st_re_made = sem("st_re_made")
        st_im_made = sem("st_im_made")
        y_mul = sem("y_mul")
        y_out = sem("y_out")
        y_gelu = sem("y_gelu")
        glu_mul = sem("glu_mul")
        glu_sig = sem("glu_sig")
        ssm_out = sem("ssm_out")
        ssm_hi_made = sem("ssm_hi_made")
        ssm_lo_made = sem("ssm_lo_made")
        stored = sem("stored")

        block = ctx.enter_context(nc.Block())

        @block.sync
        def _(sp):
            def load(c, u, width, src):
                sp.wait_ge(lo_made, c + 1)
                sp.dma_start(w_raw[:, u, 0:width], src).then_inc(raw_landed[u], 16)

            def load_phase(c0, n, width, dram, row0):
                with sp.Fori(0, n // 2) as i:
                    for u in range(2):
                        load(c0 + 2 * i + u, u, width, dram[row0 + 2 * i + u])

            with sp.Fori(0, DEPTH) as l:
                c = l * CHUNKS
                load_phase(c + C_UP[0], UP_CH, W8, w_up, l * 2 * UP_CH)
                for dst, dram in ((wb, ssm_b), (wc, ssm_c)):
                    sp.dma_start(dst[:], dram[l]).then_inc(state_landed, 16)
                load_phase(c + C_DOWN[0], DOWN_CH, W11, w_down, l * 2 * DOWN_CH)
                load_phase(c + C_IN, 4, W8, w_in, l * IN_CH)
                sp.wait_ge(chunk_done, c + C_IN + 2)
                for dst, dram in ((wglu, glu_w), (wsgu, sgu_w), (bsgu, sgu_bias)):
                    sp.dma_start(dst[:], dram[l]).then_inc(small_landed, 16)
                for r in range(2):
                    sp.dma_start(lnr[:, r, :], ln_rows[l, r:r + 1, :].partition_broadcast(P)).then_inc(small_landed, 16)
                sp.dma_start(rope_pos[:], pos_in.partition_broadcast(P)).then_inc(small_landed, 16)
                load_phase(c + C_IN + 4, IN_CH - 4, W8, w_in, l * IN_CH + 4)
                for b in range(4):
                    load_phase(c + C_MIX + KD * b, KD, MIX_W[b], mix_dram[b], l * KD)
                load_phase(c + C_OUT, OUT_CH, W8, w_out, l * OUT_CH)
                load_phase(c + C_UP[1], UP_CH, W8, w_up, l * 2 * UP_CH + UP_CH)
                load_phase(c + C_DOWN[1], DOWN_CH, W11, w_down, l * 2 * DOWN_CH + DOWN_CH)
            for k in range(KD):
                sp.wait_ge(x_new, 3 * KD * DEPTH + k + 1)
                sp.dma_start(out[:, k, :], x[:, k, :]).then_inc(stored, 16)
            sp.wait_ge(stored, 16 * KD)

        @block.tensor
        def _(pe):
            def product(ps, slot, blk, hi, lo, start, stop):
                wh = w_hi[:, slot, blk * P:(blk + 1) * P]
                pe.matmul(ps[:], wh, hi, start=start, stop=False)
                pe.matmul(ps[:], wh, lo, start=False, stop=False)
                return pe.matmul(ps[:], w_lo[:, slot, blk * P:(blk + 1) * P], hi, start=False, stop=stop)

            def chunk_ready(c):
                pe.wait_ge(lo_made, c + 3)

            def norm_sums(n):
                pe.wait_ge(sq_added, 6 * (n + 1))
                pe.wait_ge(sq_made, 8 * (n + 1))
                for b in range(TB):
                    pe.matmul(ps6[:, b:b + 1], sq_sum[:, b * P:(b + 1) * P], ones[:, 0:1], start=True, stop=False)
                    mm = pe.matmul(ps6[:, b:b + 1], sq[:, 1, b * P:(b + 1) * P], ones[:, 0:1], start=False, stop=True)
                mm.then_inc(sums_made, 1)

            def norm_spread(n):
                pe.wait_ge(diag_made, n + 1)
                pe.matmul(ps7[:], ones[:], diag[:].rearrange("p b n -> p (b n)"), start=True, stop=True)\
                  .then_inc(rstd_spread, 1)

            def first_chunks(c, a, banks, xr):
                for u in range(2):
                    pe.wait_ge(acc_free, a + u + 1)
                    chunk_ready(c + u)
                for k in range(KD):
                    pe.wait_ge(xlo_made, xr + k + 1)
                    for u in range(2):
                        mm = product(banks[u], u, k, x_hi[:, k, :], x_lo[:, k, :], k == 0, k == KD - 1)
                        if k == KD - 1:
                            mm.then_inc(chunk_done, 1)

            def up_step(c, a, u, extra=None):
                pe.wait_ge(acc_free, a + 1)
                for part in range(2):
                    chunk_ready(c + part)
                    for k in range(KD):
                        mm = product(acc[u][part], part, k, x_hi[:, k, :], x_lo[:, k, :], k == 0, k == KD - 1)
                    mm.then_inc(chunk_done, 1)
                    if extra is not None and part == 0:
                        extra()

            def ffn(l, f):
                c, a = l * CHUNKS + C_UP[f], l * STEPS + A_UP[f]
                n = l * N_NORMS + 4 * f
                first_chunks(c, a, acc[0], l * 3 * KD + 2 * KD * f)
                norm_sums(n)
                up_step(c + 2, a + 1, 1, lambda: norm_spread(n))
                with pe.Fori(1, KF // 2) as i:
                    for u in range(2):
                        up_step(c + 4 * i + 2 * u, a + 2 * i + u, u)
                c, a = l * CHUNKS + C_DOWN[f], l * STEPS + A_DOWN[f]
                hid = (2 * l + f) * KF
                with pe.Fori(0, KD // 2) as i:
                    for u in range(2):
                        pe.wait_ge(acc_free, a + 2 * i + u + 1)
                        for part in range(2):
                            chunk_ready(c + 4 * i + 2 * u + part)
                            pe.wait_ge(hid_lo_made, hid + KF2 * (part + 1))
                            for b in range(KF2):
                                k = KF2 * part + b
                                mm = product(acc[u][0], part, b, hid_hi[:, k, :], hid_lo[:, k, :], k == 0, k == KF - 1)
                            mm.then_inc(chunk_done, 1)
                norm_sums(n + 1)
                norm_spread(n + 1)

            with pe.Fori(0, DEPTH) as l:
                ffn(l, 0)

                def sgu_turn():
                    pe.wait_ge(sgu_g, 4 * l + 2)
                    for b in range(TB):
                        for t in range(2):
                            mm = pe.transpose((ps6, ps7)[b // 2][:, (b % 2 * 2 + t) * P:(b % 2 * 2 + t + 1) * P],
                                              sgu_v[:, t, b * P:(b + 1) * P], ident[:])
                    mm.then_inc(sgu_turned, 1)

                def sgu_mix():
                    pe.wait_ge(roped, 5 * l + 5)
                    pe.wait_ge(sgu_normed, l + 1)
                    for t in range(2):
                        for b in range(TB):
                            for g in range(2):
                                h = 2 * t + g
                                mm = pe.matmul((ps6, ps7)[t][64 * g:64 * g + 64, b * P:(b + 1) * P],
                                               v_tok[:, b, 64 * h:64 * h + 64], wsgu[:, h, :], start=True, stop=True)
                    mm.then_inc(sgu_mixed, 1)

                def rotate(i):
                    pe.wait_ge(qk_ready, 6 * l + (1 if i == 0 else 2 + i))
                    pe.wait_ge(sgu_var, l + 1)
                    if i >= 2:
                        pe.wait_ge(roped, 5 * l + i - 1)
                    src = k_pad[:, CHUNK:] if i == 0 else q[:, :, i - 1, :]
                    pe.matmul((ps6, ps7)[i % 2][:], rot[:], src, start=True, stop=True).then_inc(rotated, 1)

                def windows():
                    pe.wait_ge(sgu_biased, 2 * l + 2)
                    pe.wait_ge(qk_ready, 6 * l + 6)
                    for half in range(2):
                        for w in range(4):
                            c = 4 * half + w
                            mm = pe.transpose((ps6, ps7)[half][:, w * P:(w + 1) * P],
                                              v_pad[:, CHUNK * c:CHUNK * c + P], ident[:])
                        mm.then_inc(win_turned, 1)

                def scores(c):
                    if c == 0:
                        pe.wait_ge(win_ready, 2 * l + 2)
                    else:
                        pe.wait_ge(shifted, N_WIN * l + c)
                    for kv in range(2):
                        if kv:
                            pe.drain()
                        for pair in range(2):
                            j = 2 * kv + pair
                            mm = pe.matmul(ps6[:, j * P:(j + 1) * P],
                                           q[64 * kv:64 * kv + 64, c, 2 * pair:2 * pair + 2, :].rearrange("p a b -> p (a b)"),
                                           k_pad[64 * kv:64 * kv + 64, CHUNK * c:CHUNK * c + P], start=True, stop=True)
                    mm.then_inc(scored, 1)

                def turn_probs(c):
                    pe.wait_ge(probs_made, N_WIN * l + c + 1)
                    if c:
                        pe.wait_ge(att_lo_made, N_WIN * l + c)
                    for j in range(4):
                        mm = pe.transpose(ps7[:, j * P:(j + 1) * P], att_e[:, j, :], ident[:])
                    mm.then_inc(turned, 1)

                def attend(c):
                    pe.wait_ge(pt_made, N_WIN * l + c + 1)
                    for kv in range(2):
                        mm = pe.matmul(ps7[64 * kv:64 * kv + 64, 0:2 * P], v_win[:, c, 64 * kv:64 * kv + 64],
                                       att_pt[:, 2 * kv:2 * kv + 2, :].rearrange("p a b -> p (a b)"),
                                       start=True, stop=True)
                    mm.then_inc(att_out, 1)

                def ssm_in(j, bank_im):
                    if j == 0:
                        pe.wait_ge(state_landed, 32 * l + 32)
                        pe.wait_ge(u_ready, 2 * l + 2)
                    else:
                        pe.wait_ge(v_out, N_STATE_TILES * l + j)
                    r = 32 * (j % 4)
                    u = u_ssm[r:r + 32, j // 4, :]
                    pe.matmul(ps_v[:], wb[r:r + 32, j // 4, 0, :], u, start=True, stop=True)
                    pe.matmul(bank_im[:], wb[r:r + 32, j // 4, 1, :], u, start=True, stop=True).then_inc(v_mul, 1)

                def ssm_y(j):
                    pe.wait_ge(st_re_made, N_STATE_TILES * l + j + 1)
                    pe.wait_ge(st_im_made, N_STATE_TILES * l + j + 1)
                    if j == 4:
                        pe.wait_ge(y_out, 2 * l + 1)
                    r = 32 * (j % 4)
                    pe.matmul(ps_y[r:r + 32, :], wc2[:, 0, j, :], rt_re[:], start=True, stop=False)
                    pe.matmul(ps_y[r:r + 32, :], wc2[:, 1, j, :], rt_im[:], start=False, stop=True).then_inc(y_mul, 1)

                def glu():
                    pe.wait_ge(y_gelu, 2 * l + 2)
                    pe.wait_ge(att_lo_made, N_WIN * (l + 1))
                    for m in range(2):
                        for k in range(2):
                            mm = pe.matmul((ps6, ps7)[m][:], wglu[:, k, m * P:(m + 1) * P], u_ssm[:, k, :],
                                           start=(k == 0), stop=(k == 1))
                        mm.then_inc(glu_mul, 1)

                def side_work(t):
                    if t - 4 in T_SSM:
                        ssm_y(T_SSM[t - 4])
                    if t == T_SGU_TURN:
                        sgu_turn()
                    if t == T_SGU_MIX:
                        sgu_mix()
                    for i in T_ROPE.get(t, ()):
                        rotate(i)
                    if t == T_WINDOWS:
                        windows()
                    if att_group(t - 4) is not None:
                        attend(att_group(t - 4))
                    if att_group(t - 3) is not None:
                        turn_probs(att_group(t - 3))
                    if att_group(t) is not None:
                        scores(att_group(t))
                    if t == T_GLU:
                        glu()

                n = l * N_NORMS + 2
                c, a = l * CHUNKS + C_IN, l * STEPS + A_IN
                first_chunks(c, a, (acc[0][0], acc[1][0]), l * 3 * KD + KD)
                norm_sums(n)
                for s in range(2, N_IN):
                    if s >= 4:
                        pe.wait_ge(acc_free, a + s + 1)
                    side_work(s)
                    if s in T_SSM:
                        ssm_in(T_SSM[s], acc[s % 2][1])
                    chunk_ready(c + s)
                    for k in range(KD):
                        mm = product(acc[s % 2][s in (2, 3)], s % 2, k, x_hi[:, k, :], x_lo[:, k, :],
                                     k == 0, k == KD - 1)
                    mm.then_inc(chunk_done, 1)
                    if s == 2:
                        norm_spread(n)

                parts = ((conv_hi, conv_lo), (sgu_hi, sgu_lo), (att_hi, att_lo), (ssm_hi, ssm_lo))

                def mix_step(b, c, a, u, t):
                    pe.wait_ge(acc_free, a + 1)
                    if t is not None:
                        side_work(t)
                        if t in T_SSM:
                            ssm_in(T_SSM[t], acc[u][1])
                    chunk_ready(c)
                    for k in range(KD):
                        product(acc[u][0], u, k, x_hi[:, k, :], x_lo[:, k, :], k == 0, k == KD - 1)
                    for s, count in ((conv_lo_made, 2), (sgu_lo_made, 2), (att_lo_made, N_WIN), (ssm_lo_made, 2))[b:b + 1]:
                        pe.wait_ge(s, count * l + count)
                    if t in T_SSM:
                        pe.wait_ge(v_out, N_STATE_TILES * l + T_SSM[t] + 1)
                    hi, lo = parts[b]
                    for k in range(BRANCH_K[b]):
                        at = (slice(None), slice(None), k) if b == ATT else (slice(None), k)
                        mm = product(acc[u][1], u, KD + k, hi[at], lo[at], k == 0, k == BRANCH_K[b] - 1)
                    mm.then_inc(chunk_done, 1)

                for b in range(3):
                    for s in range(KD):
                        t = N_IN + KD * b + s
                        mix_step(b, l * CHUNKS + C_MIX + KD * b + s, l * STEPS + A_MIX + KD * b + s, s % 2, t)
                with pe.Fori(0, KD // 2) as i:
                    for u in range(2):
                        s = 3 * KD + 2 * i + u
                        mix_step(SSM, l * CHUNKS + C_MIX + s, l * STEPS + A_MIX + s, u, None)

                with pe.Fori(0, KD // 2) as i:
                    for u in range(2):
                        pe.wait_ge(mrg_lo_made, KD * l + KD)
                        pe.wait_ge(acc_free, l * STEPS + A_OUT + 2 * i + u + 1)
                        chunk_ready(l * CHUNKS + C_OUT + 2 * i + u)
                        for k in range(KD):
                            mm = product(acc[u][0], u, k, mrg_hi[:, k, :], mrg_lo[:, k, :], k == 0, k == KD - 1)
                        mm.then_inc(chunk_done, 1)
                norm_sums(l * N_NORMS + 3)
                norm_spread(l * N_NORMS + 3)
                ffn(l, 1)

        @block.scalar
        def _(act):
            def upper(c, c0, u, width):
                act.wait_ge(raw_landed[u], 8 * (c - u) + 16)
                act.wait_ge(chunk_done, c + 1)
                act.activation(w_hi[:, u, 0:width], w_raw[:, u, 0:width], ACT.Copy).then_inc(hi_made, 1)

            def square(n, k, src):
                if k == 0:
                    act.activation(sq_sum[:], src, ACT.Square).then_inc(sq_made, 1)
                    return
                if k >= 3:
                    act.wait_ge(sq_added, 6 * n + k - 2)
                act.activation(sq[:, k % 2, :], src, ACT.Square).then_inc(sq_made, 1)

            def x_upper(l, r):
                for k in range(KD):
                    g = PC_GAIN + 2 * KD * r + k
                    act.wait_ge(x_new, 3 * KD * l + KD * r + k + 1)
                    act.activation(x_hi[:, k, :], x[:, k, :], ACT.Copy, scale=prm[:, g:g + 1]).then_inc(xhi_made, 1)
                    square(l * N_NORMS + 2 * r, k, x[:, k, :])

            def up_step(l, f, m, u, next_w, first=False):
                c, h = l * CHUNKS + C_UP[f] + 2 * m, (2 * l + f) * KF + m
                upper(c + 2, 0, 0, next_w)
                if first:
                    upper(c + 3, 0, 1, next_w)
                act.wait_ge(a_made, h + 1)
                act.activation(up_s[:, u, :], up_a[:, u, :], ACT.Silu).then_inc(silu_made, 1)
                if not first:
                    upper(c + 3, 0, 1, next_w)
                act.wait_ge(hid_made, h + 1)
                act.activation(hid_hi[:, bass.ds(m, 1), :], up_h[:, u:u + 1, :], ACT.Copy).then_inc(hid_hi_made, 1)

            def ffn(l, f):
                up_step(l, f, 0, 0, W8, True)
                up_step(l, f, 1, 1, W8)
                with act.Fori(1, KF // 2 - 1) as i:
                    for u in range(2):
                        up_step(l, f, 2 * i + u, u, W8)
                up_step(l, f, KF - 2, 0, W8)
                up_step(l, f, KF - 1, 1, W11)
                for n in range(KD):
                    c = l * CHUNKS + C_DOWN[f] + 2 * n
                    next_w = W11 if n < KD - 1 else (W8 if f == 0 else 0)
                    if next_w:
                        upper(c + 2, 0, 0, next_w)
                    act.wait_ge(h_made, 3 * KD * l + 2 * KD * f + n + 1)
                    square(l * N_NORMS + 4 * f + 1, n, h_out[:, n, :])
                    if next_w:
                        upper(c + 3, 0, 1, next_w)
                    if f == 0 and n == 4:
                        act.wait_ge(dt_arg, l + 1)
                        act.activation(sm[:, SM_T0, :], sm[:, SM_Y, :], ACT.Sin)
                        act.activation(sm[:, SM_T1, :], sm[:, SM_Y, :], ACT.Sin, scale=0.5).then_inc(dt_sin, 1)

            act.dma_start(params_all[:], params_in).then_inc(params_landed, 16)
            for k in range(KD):
                act.dma_start(x[:, k, :], x_in[:, k, :]).then_inc(x_landed[k], 16)
            for dst, src in ((ident, ident_in), (rot, rot_in), (invf, invf_in)):
                act.dma_start(dst[:], src).then_inc(consts_landed, 16)
            with act.Fori(0, DEPTH) as l:
                act.wait_ge(prm_ready, l + 1)
                for u in range(2):
                    upper(l * CHUNKS + u, 0, u, W8)
                x_upper(l, 0)
                ffn(l, 0)
                x_upper(l, 1)

                def state_inputs(j, bank_im):
                    g = N_STATE_TILES * l + j
                    if j:
                        act.wait_ge(y_mul, g)
                    act.wait_ge(v_mul, g + 1)
                    act.activation(st_im[:], bank_im[:], ACT.Copy)
                    act.activation(st_re[:], ps_v[:], ACT.Copy).then_inc(v_out, 1)

                def tables(j):
                    g = N_STATE_TILES * l + j
                    act.wait_ge(tab_arg, g + 1)
                    if j > 1:
                        act.wait_ge(st_re_made, g - 1)
                        act.wait_ge(st_im_made, g - 1)
                    c, s = tab_c[:, j % 2, :], tab_s[:, j % 2, :]
                    act.activation(s, c, ACT.Sin, scale=2 * PI_F)
                    act.drain()
                    act.activation(c, c, ACT.Sin, scale=PI_F)
                    act.drain()
                    act.activation(c, c, ACT.Square)
                    act.drain()
                    act.activation(c, c, ACT.Copy, scale=-2.0, bias=1.0).then_inc(tab_made, 1)

                def side_work(t):
                    if t == 2:
                        act.wait_ge(rstd_made, 3 * l + 2)
                        act.dma_start(time_f[:], time_in).then_inc(time_landed, 16)
                    for i, at in enumerate((2, 3, 16, 17)):
                        if t == at:
                            z = (sgu_v if i < 2 else sgu_u)[:, i % 2, :]
                            act.wait_ge(sgu_z, 4 * l + i + 1)
                            act.activation(z, z, ACT.Gelu_apprx_tanh).then_inc(sgu_g, 1)
                    if t + 2 in T_SSM:
                        tables(T_SSM[t + 2])
                    if t == T_SGU_GATE + 1:
                        for i in range(2):
                            act.wait_ge(sgu_done, 2 * l + i + 1)
                            act.activation(sgu_hi[:, i, :], sgu_u[:, i, :], ACT.Copy).then_inc(sgu_hi_made, 1)
                    if t == 5:
                        act.wait_ge(rope_ang, l + 1)
                        act.activation(rope_s[:], rope_c[:], ACT.Sin)
                        act.drain()
                        act.activation(rope_c[:], rope_c[:], ACT.Sin, scale=0.5)
                        act.drain()
                        act.activation(rope_c[:], rope_c[:], ACT.Square).then_inc(rope_sin, 1)
                    if t == T_WINDOWS - 1:
                        for half in range(2):
                            act.wait_ge(win_turned, 2 * l + half + 1)
                            act.activation(v_win[:, 4 * half:4 * half + 4, :].rearrange("p a b -> p (a b)"),
                                           (ps6, ps7)[half][:], ACT.Copy).then_inc(win_ready, 1)
                    c = att_group(t - 2)
                    if c is not None:
                        act.wait_ge(turned, N_WIN * l + c + 1)
                        act.activation(att_pt[:].rearrange("p a b -> p (a b)"), ps7[:], ACT.Copy).then_inc(pt_made, 1)
                    c = att_group(t)
                    if c is not None:
                        act.wait_ge(shifted, N_WIN * l + c + 1)
                        keys = att_e[:, :, CHUNK:] if c == 0 else att_e[:]
                        act.activation(keys, keys, ACT.Exp)
                        act.activation(asm[:, 3, :], asm[:, 2, :], ACT.Exp).then_inc(exped, 1)
                    if t in T_SSM_OUT:
                        i = T_SSM_OUT[t]
                        act.wait_ge(y_out, 2 * l + i + 1)
                        act.activation(u_ssm[:, i, :], u_ssm[:, i, :], ACT.Gelu_apprx_tanh).then_inc(y_gelu, 1)
                    if t == T_GLU - 1:
                        for i in range(2):
                            act.wait_ge(glu_mul, 2 * l + i + 1)
                            act.activation((st_re, st_im)[i][:], (ps6, ps7)[i][:], ACT.Sigmoid).then_inc(glu_sig, 1)
                    if t == T_GLU:
                        for i in range(2):
                            act.wait_ge(ssm_out, 2 * l + i + 1)
                            act.activation(ssm_hi[:, i, :], u_ssm[:, i, :], ACT.Copy).then_inc(ssm_hi_made, 1)

                for s in range(N_IN):
                    if s in T_SSM:
                        state_inputs(T_SSM[s], acc[s % 2][1])
                    upper(l * CHUNKS + C_IN + s + 2, 0, s % 2, W8 if s < N_IN - 2 else MIX_W[0])
                    side_work(s)

                for s in range(4 * KD):
                    b, n, u = s // KD, s % KD, s % 2
                    nb = (s + 2) // KD
                    if N_IN + s in T_SSM:
                        state_inputs(T_SSM[N_IN + s], acc[u][1])
                    upper(l * CHUNKS + C_MIX + s + 2, 0, u, MIX_W[nb] if nb < 4 else W8)
                    if s > KD + 1:
                        act.wait_ge(merged_added, 3 * KD * l + s - KD - 1)
                    bg = PC_BGATE + s
                    act.wait_ge(gate_scaled, 4 * KD * l + s + 1)
                    act.activation(gate[:, u, :], gate_in[:, u, :], ACT.Sigmoid, bias=prm[:, bg:bg + 1])\
                       .then_inc(gate_made, 1)
                    if b == SSM:
                        act.wait_ge(merged_added, 3 * KD * l + s - KD + 1)
                        act.activation(mrg_hi[:, n, :], merged[:, n, :], ACT.Copy).then_inc(mrg_hi_made, 1)
                    side_work(N_IN + s)
                for n in range(KD):
                    upper(l * CHUNKS + C_OUT + n + 2, 0, n % 2, W8)
                    act.wait_ge(h_made, 3 * KD * l + KD + n + 1)
                    square(l * N_NORMS + 3, n, h_out[:, n, :])
                x_upper(l, 2)
                ffn(l, 1)

        @block.gpsimd
        def _(pool):
            pool.wait_ge(set_up, 1)
            for k in range(KD):
                pool.wait_ge(x_landed[k], 16)
                pool.sem_inc(x_new, 1)

            def add_squares(n, k):
                pool.wait_ge(sq_made, 8 * n + k + 1)
                pool.tensor_tensor(sq_sum[:], sq_sum[:], sq[:, k % 2, :], ALU.add).then_inc(sq_added, 1)
                pool.drain()

            def inverse_root(n):
                pool.wait_ge(mean_made, n + 1)
                pool.tensor_tensor(rs[:], mean_sq[:], minus_half[:], ALU.pow).then_inc(rs_made, 1)

            def norm(n):
                for k in range(1, KD - 1):
                    add_squares(n, k)
                inverse_root(n)

            def ffn(l, f):
                norm(l * N_NORMS + 4 * f)
                with pool.Fori(0, KF // 2) as i:
                    for u in range(2):
                        h = (2 * l + f) * KF + 2 * i + u
                        pool.wait_ge(silu_made, h + 1)
                        pool.wait_ge(b_made, l * STEPS + A_UP[f] + 2 * i + u + 3)
                        pool.tensor_tensor(up_h[:, u, :], up_s[:, u, :], up_b[:, u, :], ALU.mult).then_inc(hid_made, 1)
                norm(l * N_NORMS + 4 * f + 1)

            with pool.Fori(0, DEPTH) as l:
                ffn(l, 0)
                norm(l * N_NORMS + 2)

                def turn(j, out, a, b, op):
                    pool.tensor_tensor(out[:], tab_c[:, j % 2, :], a[:], ALU.mult)
                    pool.tensor_tensor(prod[:], tab_s[:, j % 2, :], b[:], ALU.mult)
                    pool.drain()
                    ins = pool.tensor_tensor(out[:], out[:], prod[:], op)
                    return ins

                for t in range(N_IN + 4 * KD):
                    if t in T_SSM:
                        j = T_SSM[t]
                        g = N_STATE_TILES * l + j
                        pool.wait_ge(tab_made, g + 1)
                        pool.wait_ge(v_out, g + 1)
                        turn(j, rt_re, st_re, st_im, ALU.add)
                        pool.drain()
                        turn(j, rt_im, st_im, st_re, ALU.subtract).then_inc(rt_made, 1)
                        pool.drain()
                    if t == T_SGU_TURN - 1:
                        pool.wait_ge(sgu_var, l + 1)
                        pool.tensor_tensor(lnrs[:], lnrs[:], minus_half[:], ALU.pow).then_inc(sgu_rs, 1)
                    if t == T_GLU - 1:
                        for i in range(2):
                            pool.wait_ge(glu_sig, 2 * l + 2)
                            pool.tensor_tensor(u_ssm[:, i, :], u_ssm[:, i, :], (st_re, st_im)[i][:], ALU.mult)\
                                .then_inc(ssm_out, 1)
                    if t >= N_IN + KD:
                        s = t - N_IN
                        pool.wait_ge(gated, 4 * KD * l + s + 1)
                        pool.tensor_tensor(merged[:, s % KD, :], merged[:, s % KD, :], gate[:, s % 2, :], ALU.add)\
                            .then_inc(merged_added, 1)
                    if t - 1 in T_SSM:
                        j = T_SSM[t - 1]
                        pool.wait_ge(scanned, N_STATE_TILES * l + j + 1)
                        turn(j, rt_re, st_re, st_im, ALU.subtract).then_inc(st_re_made, 1)
                        pool.drain()
                        if j >= POOL_TURNS_FROM:
                            turn(j, rt_im, st_im, st_re, ALU.add).then_inc(st_im_made, 1)
                            pool.drain()
                    if t == T_SGU_TURN + 2:
                        pool.wait_ge(sgu_scaled, l + 1)
                        for r, op in ((0, ALU.mult), (1, ALU.add)):
                            ins = pool.tensor_tensor(v_tok[:], v_tok[:],
                                                     lnr[:, r:r + 1, :].to_broadcast([P, TB, 2 * P]), op)
                            if r == 0:
                                pool.drain()
                        ins.then_inc(sgu_normed, 1)
                    if t == T_SGU_GATE:
                        for i in range(2):
                            pool.wait_ge(sgu_g, 4 * l + i + 3)
                            pool.tensor_tensor(sgu_u[:, i, :], sgu_u[:, i, :], sgu_v[:, i, :], ALU.mult)\
                                .then_inc(sgu_done, 1)
                norm(l * N_NORMS + 3)
                ffn(l, 1)

        @block.vector
        def _(dve):
            dve.memset(ones[:], 1.0)
            dve.memset(minus_half[:], -0.5).then_inc(set_up, 1)
            dve.memset(mean_sq[:], 0.0).then_inc(lo_made, 2)
            dve.memset(rs[:], 0.0).then_inc(chunk_done, 2)
            dve.memset(diag[:, 0, 0:8], 0.0).then_inc(acc_free, 2)
            dve.wait_ge(params_landed, 16)

            def lower(c, u, width):
                dve.wait_ge(hi_made, c + 1)
                dve.tensor_tensor(w_lo[:, u, 0:width], w_raw[:, u, 0:width], w_hi[:, u, 0:width].bitcast(F32),
                                  ALU.subtract).then_inc(lo_made, 1)

            def norm_scale(n, between=None):
                dve.wait_ge(consts_landed, 48)
                dve.wait_ge(sums_made, n + 1)
                dve.tensor_scalar(mean_sq[:], ps6[:, 0:TB], 1.0 / D_MODEL, RMS_EPS, ALU.mult, ALU.add)\
                   .then_inc(mean_made, 1)
                dve.wait_ge(rs_made, n + 1)
                dve.tensor_tensor(diag[:], ident[:].unsqueeze(1).to_broadcast([P, TB, P]),
                                  rs[:].unsqueeze(2).to_broadcast([P, TB, P]), ALU.mult).then_inc(diag_made, 1)
                if between is not None:
                    between()
                dve.wait_ge(rstd_spread, n + 1)

            def keep_rstd():
                dve.tensor_copy(rstd[:], ps7[:]).then_inc(rstd_made, 1)
                dve.drain()

            def x_lower(l, r, k):
                g = PC_GAIN + 2 * KD * r + k
                dve.wait_ge(xhi_made, 3 * KD * l + KD * r + k + 1)
                dve.scalar_tensor_tensor(x_lo[:, k, :], x[:, k, :], prm[:, g:g + 1], x_hi[:, k, :].bitcast(F32),
                                         ALU.mult, ALU.subtract).then_inc(xlo_made, 1)

            def residual(l, p, split):
                def scale(k):
                    g = PC_GAIN + KD * (2 * p + 1) + k
                    dve.scalar_tensor_tensor(h_out[:, k, :], h_out[:, k, :], prm[:, g:g + 1], ps7[:],
                                             ALU.mult, ALU.mult).then_inc(tmp_made, 1)
                scale(0)
                for k in range(KD):
                    if k + 1 < KD:
                        scale(k + 1)
                    dve.wait_ge(tmp_made, 3 * KD * l + KD * p + k + 1)
                    dve.tensor_tensor(x[:, k, :], x[:, k, :], h_out[:, k, :], ALU.add).then_inc(x_new, 1)
                    if split and k:
                        x_lower(l, p + 1, k - 1)
                if split:
                    x_lower(l, p + 1, KD - 1)

            def up_out(l, f, m, u, part):
                src = acc[u][part]
                dve.wait_ge(chunk_done, l * CHUNKS + C_UP[f] + 2 * m + part + 3)
                ins = dve.tensor_tensor((up_a, up_b)[part][:, u, :], src[:], rstd[:], ALU.mult)
                ins.then_inc((a_made, acc_free)[part], 1)

            def up_step(l, f, m, u, next_w, norm=None):
                c, h = l * CHUNKS + C_UP[f] + 2 * m, (2 * l + f) * KF + m
                if norm is not None:
                    lower(c + 2, 0, next_w)
                    norm_scale(norm, lambda: lower(c + 3, 1, next_w))
                    keep_rstd()
                up_out(l, f, m, u, 0)
                if norm is None:
                    lower(c + 2, 0, next_w)
                up_out(l, f, m, u, 1)
                if norm is None:
                    lower(c + 3, 1, next_w)
                dve.wait_ge(hid_hi_made, h + 1)
                dve.tensor_tensor(hid_lo[:, bass.ds(m, 1), :], up_h[:, u:u + 1, :],
                                  hid_hi[:, bass.ds(m, 1), :].bitcast(F32), ALU.subtract).then_inc(hid_lo_made, 1)

            def out_tile(l, p, n, c_last, u):
                dve.wait_ge(chunk_done, c_last + 3)
                dve.tensor_copy(h_out[:, n, :], acc[u][0][:]).then_inc(h_made, 1)
                dve.wait_ge(h_made, 3 * KD * l + KD * p + n + 1)
                dve.sem_inc(acc_free, 1)

            def ffn(l, f):
                up_step(l, f, 0, 0, W8, l * N_NORMS + 4 * f)
                up_step(l, f, 1, 1, W8)
                with dve.Fori(1, KF // 2 - 1) as i:
                    for u in range(2):
                        up_step(l, f, 2 * i + u, u, W8)
                up_step(l, f, KF - 2, 0, W8)
                up_step(l, f, KF - 1, 1, W11)
                for n in range(KD):
                    c = l * CHUNKS + C_DOWN[f] + 2 * n
                    next_w = W11 if n < KD - 1 else (W8 if f == 0 else 0)
                    if next_w:
                        lower(c + 2, 0, next_w)
                    out_tile(l, 2 * f, n, c + 1, n % 2)
                    if next_w:
                        lower(c + 3, 1, next_w)
                    if f == 0 and n in state_work:
                        state_work[n](l)
                norm_scale(l * N_NORMS + 4 * f + 1)

            def accurate_exp(dst, src, t0, t1, t2):
                V = dve
                V.tensor_scalar(t0, src, -87.3, 88.0, ALU.max, ALU.min)
                V.drain()
                V.tensor_scalar(t1, t0, float(np.log2(np.e)), MAGIC, ALU.mult, ALU.add)
                V.drain()
                V.tensor_scalar(t1, t1, MAGIC, None, ALU.subtract)
                V.drain()
                V.scalar_tensor_tensor(t0, t1, -LN2_HI, t0, ALU.mult, ALU.add)
                V.drain()
                V.scalar_tensor_tensor(t0, t1, -LN2_LO, t0, ALU.mult, ALU.add)
                V.tensor_scalar(smi[:], t1, 127.0, None, ALU.add)
                V.drain()
                V.tensor_scalar(smi[:], smi[:], 23, None, ALU.logical_shift_left)
                V.memset(t2, 1.0 / 40320)
                fact = [5040.0, 720.0, 120.0, 24.0, 6.0, 2.0, 1.0, 1.0]
                for q_ in fact:
                    V.drain()
                    V.tensor_tensor(t2, t2, t0, ALU.mult)
                    V.drain()
                    V.tensor_scalar(t2, t2, 1.0 / q_, None, ALU.add)
                V.tensor_scalar(t1, src, -87.3, None, ALU.is_ge)
                V.drain()
                V.tensor_tensor(t2, t2, smi[:].bitcast(F32), ALU.mult)
                V.drain()
                V.tensor_tensor(dst, t2, t1, ALU.mult)
                V.drain()

            def turns_off(w, k, parts):
                dve.tensor_scalar(k, w, float(1 / TWO_PI), MAGIC, ALU.mult, ALU.add)
                dve.drain()
                dve.tensor_scalar(k, k, MAGIC, None, ALU.subtract)
                for part in parts:
                    dve.drain()
                    dve.scalar_tensor_tensor(w, k, -part, w, ALU.mult, ALU.add)
                dve.drain()

            def S(i):
                return sm[:, i, :]

            def state_dt(l):
                accurate_exp(S(SM_DT), prm[:, PC_LDT:PC_LDT + 8], S(SM_T0), S(SM_T1), S(SM_T2))
                dve.tensor_tensor(S(SM_T3), prm[:, PC_ARE:PC_ARE + 8], S(SM_DT), ALU.mult)
                dve.drain()

            def state_decay(l):
                accurate_exp(S(SM_ER), S(SM_T3), S(SM_T0), S(SM_T1), S(SM_T2))

            def state_angle(l):
                dve.tensor_tensor(S(SM_Y), prm[:, PC_AIM:PC_AIM + 8], S(SM_DT), ALU.mult)
                dve.drain()
                turns_off(S(SM_Y), S(SM_T1), (C1, C2, C3))
                dve.tensor_scalar(S(SM_Y), S(SM_Y), -PI_F, PI_F, ALU.max, ALU.min).then_inc(dt_arg, 1)
                dve.drain()

            def state_weights(l):
                are, aim = prm[:, PC_ARE:PC_ARE + 8], prm[:, PC_AIM:PC_AIM + 8]
                dve.wait_ge(state_landed, 32 * l + 32)
                dve.wait_ge(dt_sin, l + 1)
                V = dve
                V.tensor_scalar(y_hi[:], S(SM_Y), float(1 / TWO_PI), None, ALU.mult)
                V.tensor_tensor(S(SM_T2), S(SM_T1), S(SM_T1), ALU.mult)
                for part, of in ((C1, SM_Y), (C2, SM_YLO), (C3, SM_YLO)):
                    V.drain()
                    V.scalar_tensor_tensor(S(SM_YLO), y_hi[:].bitcast(F32), -part, S(of), ALU.mult, ALU.add)
                V.drain()
                V.tensor_scalar(S(SM_YLO), S(SM_YLO), float(1 / TWO_PI), None, ALU.mult)
                V.drain()
                V.tensor_tensor(S(SM_YT), S(SM_YLO), y_hi[:].bitcast(F32), ALU.add)
                V.tensor_scalar(S(SM_T2), S(SM_T2), -2.0, 1.0, ALU.mult, ALU.add)
                V.drain()
                V.tensor_tensor(S(SM_T2), S(SM_T2), S(SM_ER), ALU.mult)
                V.tensor_tensor(S(SM_T0), S(SM_T0), S(SM_ER), ALU.mult)
                V.drain()
                V.tensor_scalar(S(SM_T2), S(SM_T2), -1.0, None, ALU.add)
                V.tensor_tensor(S(SM_T3), are, are, ALU.mult)
                V.tensor_tensor(S(SM_T4), aim, aim, ALU.mult)
                V.drain()
                V.tensor_tensor(S(SM_T3), S(SM_T3), S(SM_T4), ALU.add)
                V.drain()
                V.reciprocal(S(SM_T3), S(SM_T3))
                V.tensor_tensor(S(SM_T1), S(SM_T2), are, ALU.mult)
                V.tensor_tensor(S(SM_T4), S(SM_T0), aim, ALU.mult)
                V.tensor_tensor(S(SM_T5), S(SM_T0), are, ALU.mult)
                V.drain()
                V.tensor_tensor(S(SM_T1), S(SM_T1), S(SM_T4), ALU.add)
                V.tensor_tensor(S(SM_T2), S(SM_T2), aim, ALU.mult)
                V.drain()
                V.tensor_tensor(S(SM_T5), S(SM_T5), S(SM_T2), ALU.subtract)
                V.tensor_tensor(S(SM_KR), S(SM_T1), S(SM_T3), ALU.mult)
                V.drain()
                V.tensor_tensor(S(SM_KI), S(SM_T5), S(SM_T3), ALU.mult)
                V.drain()
                kr = S(SM_KR).unsqueeze(2).to_broadcast([P, N_STATE_TILES, 32])
                ki = S(SM_KI).unsqueeze(2).to_broadcast([P, N_STATE_TILES, 32])
                scratch = up_a[:, 0, 0:256].rearrange("p (a b) -> p a b", a=N_STATE_TILES)
                V.tensor_tensor(wc2[:, 0], wc[:, 0], kr, ALU.mult)
                V.tensor_tensor(scratch, wc[:, 1], ki, ALU.mult)
                V.tensor_tensor(wc2[:, 1], wc[:, 0], ki, ALU.mult)
                V.drain()
                V.tensor_tensor(wc2[:, 0], wc2[:, 0], scratch, ALU.subtract)
                V.drain()
                V.tensor_tensor(scratch, wc[:, 1], kr, ALU.mult)
                V.drain()
                V.scalar_tensor_tensor(wc2[:, 1], wc2[:, 1], -1.0, scratch, ALU.mult, ALU.subtract)
                V.drain()

            state_work = {1: state_dt, 2: state_decay, 3: state_angle, 5: state_weights}

            with dve.Fori(0, DEPTH) as l:
                dve.tensor_copy(prm[:], params_all[:, bass.ds(l, 1), :].rearrange("p a b -> p (a b)"))
                dve.drain()
                for nrm in (1, 5):
                    a = PC_GAIN + KD * nrm
                    ins = dve.tensor_scalar(prm[:, a:a + KD], prm[:, a:a + KD], 0.5, None, ALU.mult)
                ins.then_inc(prm_ready, 1)
                dve.drain()
                for u in range(2):
                    lower(l * CHUNKS + u, u, W8)
                for k in range(KD):
                    x_lower(l, 0, k)
                ffn(l, 0)
                residual(l, 0, True)

                def angles(j):
                    if j == 0:
                        dve.wait_ge(time_landed, 16 * l + 16)
                    if j > 1:
                        dve.wait_ge(st_re_made, N_STATE_TILES * l + j - 1)
                        dve.wait_ge(st_im_made, N_STATE_TILES * l + j - 1)
                    w = tab_c[:, j % 2, :]
                    dve.tensor_scalar(tab_k[:], time_f[:], sm[:, SM_YT, j:j + 1], MAGIC, ALU.mult, ALU.add)
                    dve.drain()
                    dve.tensor_scalar(tab_k[:], tab_k[:], MAGIC, None, ALU.subtract)
                    dve.drain()
                    dve.scalar_tensor_tensor(w, time_f[:], y_hi[:, j:j + 1].bitcast(F32), tab_k[:],
                                             ALU.mult, ALU.subtract)
                    dve.drain()
                    dve.scalar_tensor_tensor(w, time_f[:], sm[:, SM_YLO, j:j + 1], w, ALU.mult, ALU.add)
                    dve.drain()
                    dve.tensor_scalar(w, w, -0.5, 0.5, ALU.max, ALU.min).then_inc(tab_arg, 1)

                def scans(j):
                    g = N_STATE_TILES * l + j
                    dve.wait_ge(rt_made, g + 1)
                    decay = sm[:, SM_ER, j:j + 1].to_broadcast([P, SEQ])
                    dve.tensor_tensor_scan(st_re[:], decay, rt_re[:], 0.0, ALU.mult, ALU.add)
                    dve.tensor_tensor_scan(st_im[:], decay, rt_im[:], 0.0, ALU.mult, ALU.add).then_inc(scanned, 1)
                    dve.drain()
                    if j >= POOL_TURNS_FROM:
                        return
                    dve.tensor_tensor(rt_im[:], tab_c[:, j % 2, :], st_im[:], ALU.mult)
                    dve.tensor_tensor(tab_k[:], tab_s[:, j % 2, :], st_re[:], ALU.mult)
                    dve.drain()
                    dve.tensor_tensor(rt_im[:], rt_im[:], tab_k[:], ALU.add).then_inc(st_im_made, 1)

                def sgu_norm():
                    dve.wait_ge(sgu_turned, l + 1)
                    for b in range(TB):
                        dve.tensor_copy(v_tok[:, b, :], (ps6, ps7)[b // 2][:, b % 2 * 2 * P:(b % 2 + 1) * 2 * P])
                    dve.drain()
                    for b in range(TB):
                        dve.bn_stats(lnst[:, b, :], v_tok[:, b, :])
                    dve.drain()
                    for b in range(TB):
                        dve.bn_aggr(lnmv[:, b, :], lnst[:, b, :])
                    dve.drain()
                    dve.tensor_scalar(lnrs[:], lnmv[:, :, 1], LN_EPS, None, ALU.add).then_inc(sgu_var, 1)

                def sgu_norm_end():
                    dve.wait_ge(sgu_rs, l + 1)
                    for b in range(TB):
                        dve.tensor_scalar(v_tok[:, b, :], v_tok[:, b, :], lnmv[:, b, 0:1], lnrs[:, b:b + 1],
                                          ALU.subtract, ALU.mult)
                    dve.memset(wsgu[CHUNK:P, :, 0:CHUNK], 0.0)
                    dve.drain()
                    dve.sem_inc(sgu_scaled, 1)

                def sgu_bias_add():
                    dve.wait_ge(sgu_mixed, l + 1)
                    for i in range(2):
                        mixed = (ps6, ps7)[i][:].rearrange("p (b n) -> p b n", b=TB)
                        dve.tensor_tensor(sgu_v[:, i, :].rearrange("p (b n) -> p b n", b=TB), mixed,
                                          bsgu[:, i:i + 1, :].to_broadcast([P, TB, P]), ALU.add).then_inc(sgu_biased, 1)

                def lower_of(lo, hi, full, made, value, inc):
                    dve.wait_ge(made, value)
                    dve.tensor_tensor(lo, full, hi.bitcast(F32), ALU.subtract).then_inc(inc, 1)

                def halves(hi, lo, full):
                    dve.tensor_copy(hi, full)
                    dve.drain()
                    return dve.tensor_tensor(lo, full, hi.bitcast(F32), ALU.subtract)

                def rope_angles():
                    dve.wait_ge(small_landed, 96 * l + 96)
                    dve.tensor_copy(rope_c[:], rope_pos[:])
                    dve.drain()
                    dve.tensor_scalar(rope_c[:], rope_c[:], invf[:, 0:1], None, ALU.mult)
                    dve.drain()
                    turns_off(rope_c[:], att_e[:].rearrange("p a b -> p (a b)"), (C1, C2, C3))
                    dve.tensor_scalar(rope_c[:], rope_c[:], -PI_F, PI_F, ALU.max, ALU.min).then_inc(rope_ang, 1)

                def rope(i):
                    if i == 0:
                        dve.wait_ge(rope_sin, l + 1)
                        dve.tensor_scalar(rope_c[:], rope_c[:], -2.0, 1.0, ALU.mult, ALU.add)
                        dve.drain()
                    def by_chunk(a):
                        return a.rearrange("p (c q) -> p c q", c=N_WIN)
                    z = by_chunk(k_pad[:, CHUNK:]) if i == 0 else q[:, :, i - 1, :]
                    t_ = by_chunk(att_e[:].rearrange("p a b -> p (a b)"))
                    dve.wait_ge(rotated, 5 * l + i + 1)
                    dve.tensor_tensor(t_, by_chunk((ps6, ps7)[i % 2][:]), by_chunk(rope_s[:]), ALU.mult)
                    dve.tensor_tensor(z, z, by_chunk(rope_c[:]), ALU.mult)
                    dve.drain()
                    dve.tensor_tensor(z, z, t_, ALU.add).then_inc(roped, 1)
                    dve.drain()

                def conv(i):
                    w = PC_CONV + i
                    y = conv3[:, 0, :]
                    dve.tensor_tensor(conv_pad[:, 2:2 + SEQ], conv3[:, 1, :], conv3[:, 0, :], ALU.mult)
                    dve.drain()
                    dve.tensor_scalar(y, conv_pad[:, 0:SEQ], prm[:, w:w + 1], None, ALU.mult)
                    for tap in (1, 2):
                        dve.drain()
                        dve.scalar_tensor_tensor(y, conv_pad[:, tap:tap + SEQ], prm[:, w + 2 * tap:w + 2 * tap + 1], y,
                                                 ALU.mult, ALU.add)
                    dve.drain()
                    dve.tensor_tensor(y, y, conv3[:, 2, :], ALU.mult)
                    dve.drain()
                    halves(conv_hi[:, i, :], conv_lo[:, i, :], y).then_inc(conv_lo_made, 1)

                def shift_scores(c):
                    g = N_WIN * l + c
                    k0 = CHUNK if c == 0 else 0
                    s4 = ps6[:].rearrange("p (j k) -> p j k", j=4)[:, :, k0:]
                    sink = prm[:, PC_SINK:PC_SINK + 4]
                    dve.wait_ge(scored, g + 1)
                    if c:
                        dve.wait_ge(turned, g)
                    else:
                        dve.memset(att_e[:, :, 0:CHUNK], 0.0)
                    dve.tensor_reduce(asm[:, 0, :], s4, AX.X, ALU.max)
                    dve.drain()
                    dve.scalar_tensor_tensor(asm[:, 1, :], asm[:, 0, :], HEAD_DIM ** -0.5, sink, ALU.mult, ALU.max)
                    dve.drain()
                    dve.tensor_tensor(asm[:, 2, :], sink, asm[:, 1, :], ALU.subtract)
                    dve.scalar_tensor_tensor(att_e[:, :, k0:], s4, HEAD_DIM ** -0.5,
                                             asm[:, 1, :].unsqueeze(2).to_broadcast([P, 4, P - k0]),
                                             ALU.mult, ALU.subtract).then_inc(shifted, 1)

                def make_probs(c):
                    g = N_WIN * l + c
                    dve.wait_ge(exped, g + 1)
                    dve.tensor_reduce(asm[:, 4, :], att_e[:], AX.X, ALU.add)
                    dve.drain()
                    dve.tensor_tensor(asm[:, 4, :], asm[:, 4, :], asm[:, 3, :], ALU.add)
                    dve.drain()
                    dve.reciprocal(asm[:, 5, :], asm[:, 4, :])
                    dve.drain()
                    dve.tensor_tensor(att_e[:], att_e[:], asm[:, 5, :].unsqueeze(2).to_broadcast([P, 4, P]), ALU.mult)\
                       .then_inc(probs_made, 1)

                def attention_out(c):
                    dve.wait_ge(att_out, N_WIN * l + c + 1)
                    halves(att_hi[:, c], att_lo[:, c], ps7[:, 0:2 * P].rearrange("p (t q) -> p t q", t=4))\
                        .then_inc(att_lo_made, 1)

                def ssm_result(i):
                    dve.wait_ge(y_mul, N_STATE_TILES * l + 4 * i + 4)
                    dve.scalar_tensor_tensor(u_ssm[:, i, :], u_ssm[:, i, :], prm[:, PC_D + i:PC_D + i + 1], ps_y[:],
                                             ALU.mult, ALU.add).then_inc(y_out, 1)

                def side_work(t):
                    if t - 1 in T_SSM:
                        scans(T_SSM[t - 1])
                    if att_group(t - 3) is not None:
                        attention_out(att_group(t - 3))
                    if att_group(t - 1) is not None:
                        make_probs(att_group(t - 1))
                    if att_group(t) is not None:
                        shift_scores(att_group(t))
                    if t in T_ANGLES:
                        angles(T_ANGLES[t])
                    if t == T_SGU_TURN - 1:
                        sgu_norm()
                    if t == T_SGU_TURN:
                        sgu_norm_end()
                    if t == T_SGU_MIX - 1:
                        sgu_bias_add()
                    if t == T_SGU_GATE + 5:
                        for i in range(2):
                            lower_of(sgu_lo[:, i, :], sgu_hi[:, i, :], sgu_u[:, i, :], sgu_hi_made, 2 * l + i + 1,
                                     sgu_lo_made)
                    if t == 3:
                        rope_angles()
                    for i in T_ROPE.get(t + 1, ()):
                        rope(i)
                    if t in T_CONV:
                        conv(T_CONV[t])
                    if t in T_SSM_OUT:
                        ssm_result(T_SSM_OUT[t])
                    if t == T_GLU + 1:
                        for i in range(2):
                            lower_of(ssm_lo[:, i, :], ssm_hi[:, i, :], u_ssm[:, i, :], ssm_hi_made, 2 * l + i + 1,
                                     ssm_lo_made)

                for pad in (k_pad, v_pad):
                    dve.memset(pad[:, 0:CHUNK], 0.0)
                dve.memset(conv_pad[:, 0:2], 0.0)
                in_place = {"ssm": (u_ssm, u_ready), "sgu_v": (sgu_v, sgu_z), "sgu_u": (sgu_u, sgu_z),
                            "k": (k_pad, qk_ready), "v": (v_pad, qk_ready), "q": (q, qk_ready)}
                for s, (name, tile) in enumerate(W_IN_TILES):
                    if name in ("k", "v"):
                        dst = in_place[name][0][:, CHUNK:]
                    elif name in in_place and name != "q":
                        dst = in_place[name][0][:, tile, :]
                    elif name != "q":
                        dst = conv3[:, ("cx", "cc", "cb").index(name), :]
                    if s == 0:
                        lower(l * CHUNKS + C_IN + 2, 0, W8)
                        norm_scale(l * N_NORMS + 2, lambda: lower(l * CHUNKS + C_IN + 3, 1, W8))
                        keep_rstd()
                    dve.drain()
                    dve.wait_ge(chunk_done, l * CHUNKS + C_IN + s + 3)
                    src, r_ = acc[s % 2][s in (2, 3)][:], rstd[:]
                    if name == "q":
                        dst = q[:, :, tile, :]
                        src, r_ = (a.rearrange("p (c q) -> p c q", c=N_WIN) for a in (src, r_))
                    dve.tensor_tensor(dst, src, r_, ALU.mult).then_inc(acc_free, 1)
                    dve.drain()
                    if name in in_place:
                        dve.sem_inc(in_place[name][1], 1)
                    if s >= 2:
                        lower(l * CHUNKS + C_IN + s + 2, s % 2, W8 if s < N_IN - 2 else MIX_W[0])
                    side_work(s)

                def merged_lower(n):
                    lower_of(mrg_lo[:, n, :], mrg_hi[:, n, :], merged[:, n, :], mrg_hi_made, KD * l + n + 1, mrg_lo_made)

                for s in range(4 * KD):
                    b, n, u = s // KD, s % KD, s % 2
                    nb = (s + 2) // KD
                    g = 4 * KD * l + s
                    dve.wait_ge(chunk_done, l * CHUNKS + C_MIX + s + 3)
                    dve.tensor_tensor(gate_in[:, u, :], acc[u][0][:], rstd[:], ALU.mult).then_inc(gate_scaled, 1)
                    lower(l * CHUNKS + C_MIX + s + 2, u, MIX_W[nb] if nb < 4 else W8)
                    dve.drain()
                    dve.wait_ge(gate_made, g + 1)
                    dst = merged[:, n, :] if b == CONV else gate[:, u, :]
                    dve.tensor_tensor(dst, gate[:, u, :], acc[u][1][:], ALU.mult).then_inc(gated, 1)
                    dve.wait_ge(gated, g + 1)
                    dve.sem_inc(acc_free, 1)
                    side_work(N_IN + s)
                    if b == SSM and n:
                        merged_lower(n - 1)
                merged_lower(KD - 1)
                for n in range(KD):
                    out_tile(l, 1, n, l * CHUNKS + C_OUT + n, n % 2)
                    lower(l * CHUNKS + C_OUT + n + 2, n % 2, W8)
                norm_scale(l * N_NORMS + 3)
                residual(l, 1, True)
                ffn(l, 1)
                residual(l, 2, False)


def _tiles(w, k):
    lead = w.shape[:-2]
    n = w.shape[-1] // P
    w = w.reshape(*lead, k, P, n, P)
    m = len(lead)
    w = w.transpose(*range(m), m + 2, m + 1, m, m + 3)
    return np.ascontiguousarray(w).reshape(*lead, n, P, k * P)


def _columns(v):
    v = v.reshape(*v.shape[:-1], v.shape[-1] // P, P)
    return np.moveaxis(v, -1, 0)


def _layout(x, positions, norm_gains, ffn_w1, ffn_w3, ffn_w2, w_in, attn_sinks, ssm_a_re, ssm_a_im, ssm_log_dt,
            ssm_b_re, ssm_b_im, ssm_c_re, ssm_c_im, ssm_d, ssm_glu_w, sgu_ln_g, sgu_ln_b, sgu_w, sgu_b, conv_w,
            w_branch, w_gate, b_gate, w_out):
    L = DEPTH
    head_order = np.array([64 * (4 * kv + t) + d for t in range(4) for kv in range(2) for d in range(64)])
    cols = []
    for name, tile in W_IN_TILES:
        base = W_IN_COLS[name]
        own = head_order if name == "q" else np.arange(2 * P)
        cols.append(base + own[tile * P:(tile + 1) * P])
    win = _tiles(w_in[:, :, np.concatenate(cols)], KD).reshape(L * N_IN, P, W8)
    up = np.stack([_tiles(ffn_w1, KD), _tiles(ffn_w3, KD)], axis=3).reshape(L * 2 * UP_CH, P, W8)
    down = _tiles(ffn_w2, KF).reshape(L, 2, KD, P, 2, W11).transpose(0, 1, 2, 4, 3, 5)
    down = np.ascontiguousarray(down).reshape(L * 2 * DOWN_CH, P, W11)
    mix = []
    for b in range(4):
        rows = BRANCH_ROW0[b] + (head_order if b == ATT else np.arange(BRANCH_K[b] * P))
        g = _tiles(w_gate[:, :, REF_BRANCH[b], :], KD)
        w = _tiles(w_branch[:, rows, :], BRANCH_K[b])
        mix.append(np.concatenate([g, w], axis=-1).reshape(L * KD, P, MIX_W[b]))
    prm = np.zeros((P, L, PC_N), np.float32)
    prm[:, :, PC_GAIN:PC_GAIN + 48] = _columns(norm_gains).reshape(P, L, 48)
    prm[:, :, PC_BGATE:PC_BGATE + 32] = _columns(b_gate[:, list(REF_BRANCH), :]).reshape(P, L, 32)
    for col, a in ((PC_ARE, ssm_a_re), (PC_AIM, ssm_a_im), (PC_LDT, np.repeat(ssm_log_dt[:, :, None], 64, axis=2))):
        prm[:, :, col:col + 8] = _columns(a.reshape(L, 1024))
    prm[:, :, PC_D:PC_D + 2] = _columns(ssm_d)
    prm[:, :, PC_CONV:PC_CONV + 6] = _columns(conv_w).reshape(P, L, 6)
    sink = attn_sinks.reshape(L, 2, 2, 2).transpose(3, 0, 1, 2).reshape(2, L, 4)
    prm[:, :, PC_SINK:PC_SINK + 4] = np.repeat(sink, 64, axis=0)
    sb = np.zeros((L, P, 2, 2, P), np.float32)
    sc = np.zeros((L, P, 2, N_STATE_TILES, 32), np.float32)
    for g in range(16):
        j, h = g // 2, g % 2
        r = 32 * (j % 4) + 16 * h
        for part, (b, c) in enumerate(((ssm_b_re, ssm_c_re), (ssm_b_im, ssm_c_im))):
            sb[:, r:r + 16, j // 4, part, 64 * h:64 * h + 64] = b[:, g].transpose(0, 2, 1)
            sc[:, 64 * h:64 * h + 64, part, j, 16 * h:16 * h + 16] = c[:, g].transpose(0, 2, 1)
    glu = np.ascontiguousarray(ssm_glu_w.reshape(L, 2, P, 2 * P).transpose(0, 2, 1, 3))
    sgw = np.ascontiguousarray(sgu_w.transpose(0, 3, 1, 2))
    sgb = np.repeat(sgu_b.reshape(L, 2, 2, P).transpose(0, 2, 1, 3), 64, axis=1)
    rot = np.zeros((P, P), np.float32)
    invf = np.zeros((P, 1), np.float32)
    freq = np.float32(ROPE_THETA) ** (-np.arange(0, ROT_DIM, 2, dtype=np.float32) / ROT_DIM)
    half = ROT_DIM // 2
    for h0 in (0, HEAD_DIM):
        for i in range(half):
            rot[h0 + half + i, h0 + i] = -1.0
            rot[h0 + i, h0 + half + i] = 1.0
            invf[h0 + i] = invf[h0 + half + i] = freq[i]
    return {
        "x_in": np.ascontiguousarray(x[0].T.reshape(KD, P, SEQ).transpose(1, 0, 2)),
        "pos_in": positions,
        "params_in": prm, "w_up": up, "w_down": down, "w_in": win,
        "w_conv": mix[0], "w_sgu": mix[1], "w_att": mix[2], "w_ssm": mix[3],
        "w_out": _tiles(w_out, KD).reshape(L * OUT_CH, P, W8),
        "ssm_b": sb, "ssm_c": sc, "glu_w": glu, "sgu_w": sgw, "sgu_bias": np.ascontiguousarray(sgb),
        "ln_rows": np.stack([sgu_ln_g, sgu_ln_b], axis=1),
        "ident_in": np.eye(P, dtype=np.float32), "rot_in": rot, "invf_in": invf,
        "time_in": np.tile(np.arange(SEQ, dtype=np.float32), (P, 1)),
    }


def kernel(**inputs):
    import concourse.bacc as _bacc
    from concourse.bass_utils import run_bass_kernel_spmd as _run

    arrays = _layout(**{n: np.asarray(a) for n, a in inputs.items()})
    nc = _bacc.Bacc("TRN2", target_bir_lowering=False, num_devices=1)
    aps = {n: nc.dram_tensor(n, a.shape, mybir.dt.from_np(a.dtype), kind="ExternalInput").ap()
           for n, a in arrays.items()}
    out = nc.dram_tensor("out", (P, KD, SEQ), F32, kind="ExternalOutput").ap()
    build_encoder(nc, **aps, out=out)
    got = _run(nc, [arrays], core_ids=[0]).results[0]["out"]
    return np.ascontiguousarray(got.transpose(1, 0, 2).reshape(D_MODEL, SEQ).T)[None]
```

```python
from contextlib import ExitStack

import numpy as np

import concourse.bass as bass
from concourse import mybir

F32 = mybir.dt.float32
F32R = mybir.dt.float32r
I32 = mybir.dt.int32
ALU = mybir.AluOpType
ACT = mybir.ActivationFunctionType
AX = mybir.AxisListType

P = 128
DEPTH, SEQ, D_MODEL, D_FF = 2, 512, 1024, 2816
KD = D_MODEL // P
KF = D_FF // P
KF2 = KF // 2
TB = SEQ // P
CHUNK, HEAD_DIM, N_WIN = 64, 64, SEQ // 64
ROT_DIM, ROPE_THETA = 16, 500000.0
RMS_EPS, LN_EPS = 1e-6, 1e-5
N_STATE_TILES = 8

CONV, SGU, ATT, SSM = range(4)
REF_BRANCH = (3, 2, 0, 1)
BRANCH_K = (2, 2, 4, 2)
BRANCH_ROW0 = (1024, 768, 0, 512)

W_IN_COLS = {"ssm": 768, "sgu_v": 1280, "sgu_u": 1024, "k": 512, "v": 640, "q": 0,
             "cx": 1536, "cb": 1792, "cc": 2048}
W_IN_TILES = [("ssm", 0), ("ssm", 1), ("sgu_v", 0), ("sgu_v", 1), ("k", 0), ("q", 0), ("q", 1), ("q", 2), ("q", 3),
              ("cx", 0), ("cc", 0), ("cb", 0), ("v", 0), ("cx", 1), ("cc", 1), ("cb", 1), ("sgu_u", 0), ("sgu_u", 1)]
N_IN = len(W_IN_TILES)

SLOT = 12 * P
UP_CH, DOWN_CH, IN_CH, MIX_CH, OUT_CH = 2 * KF, 2 * KD, N_IN, 4 * KD, KD
C_UP = (0, UP_CH + DOWN_CH + IN_CH + MIX_CH + OUT_CH)
C_DOWN = (UP_CH, C_UP[1] + UP_CH)
C_IN = UP_CH + DOWN_CH
C_MIX = C_IN + IN_CH
C_OUT = C_MIX + MIX_CH
CHUNKS = C_DOWN[1] + DOWN_CH
A_UP = (0, KF + KD + N_IN + 4 * KD + KD)
A_DOWN = (KF, A_UP[1] + KF)
A_IN = KF + KD
A_MIX = A_IN + N_IN
A_OUT = A_MIX + 4 * KD
STEPS = A_DOWN[1] + KD
N_NORMS = 6
H = SEQ // 2
X_UNITS = 2 * KD


def squares_before(l, r):
    return (2 * KD + 1) * (l * (N_NORMS // 2) + r // 2) + KD * (r % 2)
W8, W11 = KD * P, KF2 * P
MIX_W = [(KD + k) * P for k in BRANCH_K]

T_SGU_TURN, T_SGU_MIX, T_SGU_GATE, T_WINDOWS, T_ATT, T_GLU = 5, 14, 18, 15, 16, 39
T_ROPE = {8: (0, 1), 10: (2, 3), 13: (4,)}
T_SSM = {5 + 4 * j: j for j in range(N_STATE_TILES)}
T_ANGLES = {2: 0, 5: 1, **{t - 5: j for t, j in T_SSM.items() if j > 1}}
POOL_TURNS_FROM = 1
T_SSM_OUT = {5 + 4 * (4 * i + 3) + 3: i for i in range(2)}
T_CONV = {11: 0, 15: 1}


def att_group(t):
    return (t - T_ATT) // 2 if t >= T_ATT and (t - T_ATT) % 2 == 0 and (t - T_ATT) // 2 < N_WIN else None


PC_GAIN, PC_BGATE, PC_ARE, PC_AIM, PC_LDT, PC_D, PC_CONV, PC_SINK, PC_N = 0, 48, 80, 88, 96, 104, 106, 112, 116

TWO_PI = 2 * np.pi
C1 = 6.28125
C2 = float(np.float32(np.round((TWO_PI - C1) * 2**20) / 2**20))
C3 = float(np.float32(TWO_PI - C1 - C2))
PI_F = 3.1415925
MAGIC = 1.5 * 2**23
LN2_HI = 0.693359375
LN2_LO = float(np.float32(np.log(2.0) - LN2_HI))


def build_encoder(nc, x_in, pos_in, params_in, w_up, w_down, w_in, w_conv, w_sgu, w_att, w_ssm, w_out,
                  ssm_b, ssm_c, glu_w, sgu_w, sgu_bias, ln_rows, consts_in, time_in, out):
    mix_dram = (w_conv, w_sgu, w_att, w_ssm)
    base = (nc.sbuf_base + 63) // 64 * 64

    with ExitStack() as ctx:
        def sem(name):
            return ctx.enter_context(nc.semaphore(name))

        def bank(name):
            return ctx.enter_context(nc.psum_tensor(name, [P, SEQ], F32))

        top = [base]

        def place(name, shape, dt=F32, at=None):
            size = 4 * int(np.prod(shape[1:]))
            off = at
            if at is None:
                off = top[0]
                top[0] += (size + 31) // 32 * 32
            return nc.alloc_sbuf_tensor_at(name, shape, dt, offset=off)

        x = place("x", [P, KD, SEQ])
        w_raw = place("w_raw", [P, 2, SLOT])
        w_hi = place("w_hi", [P, 2, SLOT], F32R)
        w_lo = place("w_lo", [P, 2, SLOT], F32R)
        at_xhi = top[0]
        x_hi = place("x_hi", [P, KD, SEQ], F32R)
        x_lo = place("x_lo", [P, KD, SEQ], F32R)
        h_out = place("h_out", [P, KD, SEQ], at=at_xhi)
        rstd = place("rstd", [P, SEQ])
        sq_sum = place("sq_sum", [P, SEQ])
        at_sq = top[0]
        sq = place("sq", [P, 2, SEQ])
        gate_in = place("gate_in", [P, 2, SEQ], at=at_sq)
        consts = place("consts", [P, 2 * P + 1])
        ident, rot, invf = consts[:, 0:P], consts[:, P:2 * P], consts[:, 2 * P:]
        ones = place("ones", [P, P])
        at_diag = top[0]
        diag = place("diag", [P, TB, P])
        time_f = place("time_f", [P, SEQ], at=at_diag)
        params_all = place("params_all", [P, DEPTH, PC_N])
        prm = place("prm", [P, PC_N])
        mean_sq = place("mean_sq", [P, TB])
        rs = place("rs", [P, TB])
        minus_half = place("minus_half", [P, TB])
        region = top[0]

        hid_hi = place("hid_hi", [P, KF, SEQ], F32R)
        hid_lo = place("hid_lo", [P, KF, SEQ], F32R)
        up_a = place("up_a", [P, 2, SEQ])
        up_b = place("up_b", [P, 2, SEQ])
        up_s = place("up_s", [P, 2, SEQ])
        up_h = place("up_h", [P, 2, SEQ])
        ffn_end = top[0]
        assert ffn_end <= nc.sbuf_usable_end
        top[0] = region
        at_merged = top[0]
        conv3 = place("conv3", [P, 3, SEQ])
        conv_pad = place("conv_pad", [P, SEQ + 8])
        rope_c = place("rope_c", [P, SEQ])
        rope_s = place("rope_s", [P, SEQ])
        rope_pos = nc.alloc_sbuf_tensor_at("rope_pos", [P, SEQ], I32, offset=top[0] - 4 * SEQ)
        sgu_v = place("sgu_v", [P, 2, SEQ])
        merged = place("merged", [P, KD, SEQ], at=at_merged)
        at_z = top[0]
        q = place("q", [P, N_WIN, 4, CHUNK])
        att_hi = place("att_hi", [P, N_WIN, 4, CHUNK], F32R, at=at_z)
        k_pad = place("k_pad", [P, CHUNK + SEQ])
        v_pad = place("v_pad", [P, CHUNK + SEQ])
        u_ssm = place("u_ssm", [P, 2, SEQ])
        sgu_u = place("sgu_u", [P, 2, SEQ])
        sgu_hi = place("sgu_hi", [P, 2, SEQ], F32R)
        sgu_lo = place("sgu_lo", [P, 2, SEQ], F32R)
        v_win = place("v_win", [P, N_WIN, P])
        assert top[0] - at_z >= 2 * 4 * KD * SEQ
        mrg_hi = place("mrg_hi", [P, KD, SEQ], F32R, at=at_z)
        mrg_lo = place("mrg_lo", [P, KD, SEQ], F32R, at=at_z + 4 * KD * SEQ)
        at_conv = top[0]
        conv_hi = place("conv_hi", [P, 2, SEQ], F32R)
        conv_lo = place("conv_lo", [P, 2, SEQ], F32R)
        ssm_hi = place("ssm_hi", [P, 2, SEQ], F32R, at=at_conv)
        ssm_lo = place("ssm_lo", [P, 2, SEQ], F32R, at=at_conv + 8 * SEQ)
        att_lo = place("att_lo", [P, N_WIN, 4, CHUNK], F32R)
        v_tok = place("v_tok", [P, TB, 2 * P])
        att_e = place("att_e", [P, 4, P])
        att_pt = place("att_pt", [P, 4, P])
        tab_c = place("tab_c", [P, 2, SEQ])
        tab_s = place("tab_s", [P, 2, SEQ])
        tab_k = place("tab_k", [P, SEQ])
        st_re = place("st_re", [P, SEQ])
        st_im = place("st_im", [P, SEQ])
        rt_re = place("rt_re", [P, SEQ])
        rt_im = place("rt_im", [P, SEQ])
        prod = place("prod", [P, SEQ])
        gate = place("gate", [P, 2, SEQ])
        wglu = place("wglu", [P, 2, 2 * P])
        wsgu = place("wsgu", [P, 4, P])
        bsgu = place("bsgu", [P, 2, P])
        lnr = place("lnr", [P, 2, 2 * P])
        top[0] = max(top[0], ffn_end)
        wb = place("wb", [P, 2, 2, P])
        wc = place("wc", [P, 2, N_STATE_TILES, 32])
        wc2 = place("wc2", [P, 2, N_STATE_TILES, 32])
        sm = place("sm", [P, 13, N_STATE_TILES])
        y_hi = place("y_hi", [P, N_STATE_TILES], F32R)
        smi = nc.alloc_sbuf_tensor_at("smi", [P, N_STATE_TILES], I32, offset=top[0])
        top[0] += 32
        lnst = place("lnst", [P, TB, 6])
        lnmv = place("lnmv", [P, TB, 2])
        lnrs = place("lnrs", [P, TB])
        asm = place("asm", [P, 6, 4])
        assert top[0] <= nc.sbuf_usable_end, (top[0], nc.sbuf_usable_end)
        SM_DT, SM_ER, SM_Y, SM_YLO, SM_KR, SM_KI, SM_T0, SM_T1, SM_T2, SM_T3, SM_T4, SM_T5, SM_YT = range(13)

        acc = [[bank("acc00"), bank("acc01")], [bank("acc10"), bank("acc11")]]
        ps_y, ps_v, ps6, ps7 = bank("ps_y"), bank("ps_v"), bank("ps6"), bank("ps7")
        spare = [ps_y, ps_v]
        in_bank = [acc[0][0], acc[1][0], acc[0][1], acc[1][1], ps_y] + [acc[s % 2][0] for s in range(5, N_IN)]

        raw_landed = [sem("raw_landed0"), sem("raw_landed1")]
        hi_made = sem("hi_made")
        lo_made = sem("lo_made")
        chunk_done = sem("chunk_done")
        acc_free = sem("acc_free")
        params_landed = sem("params_landed")
        consts_landed = sem("consts_landed")
        state_landed = sem("state_landed")
        small_landed = sem("small_landed")
        time_landed = sem("time_landed")
        x_landed = [sem(f"x_landed{k}") for k in range(KD // 2)]
        set_up = sem("set_up")
        x_new = sem("x_new")
        xhi_made = sem("xhi_made")
        xlo_made = sem("xlo_made")
        tmp_made = sem("tmp_made")
        sq_made = sem("sq_made")
        sq_added = sem("sq_added")
        sums_made = sem("sums_made")
        mean_made = sem("mean_made")
        rs_made = sem("rs_made")
        diag_made = sem("diag_made")
        rstd_spread = sem("rstd_spread")
        rstd_made = sem("rstd_made")
        prm_ready = sem("prm_ready")
        a_made = sem("a_made")
        silu_made = sem("silu_made")
        hid_made = sem("hid_made")
        hid_hi_made = sem("hid_hi_made")
        hid_lo_made = sem("hid_lo_made")
        half_done = sem("half_done")
        h_made = sem("h_made")
        gate_scaled = sem("gate_scaled")
        gate_made = sem("gate_made")
        gated = sem("gated")
        merged_added = sem("merged_added")
        mrg_hi_made = sem("mrg_hi_made")
        mrg_lo_made = sem("mrg_lo_made")
        u_ready = sem("u_ready")
        sgu_z = sem("sgu_z")
        sgu_g = sem("sgu_g")
        sgu_turned = sem("sgu_turned")
        sgu_var = sem("sgu_var")
        sgu_normed = sem("sgu_normed")
        sgu_biased = sem("sgu_biased")
        sgu_mixed = sem("sgu_mixed")
        sgu_done = sem("sgu_done")
        sgu_hi_made = sem("sgu_hi_made")
        sgu_lo_made = sem("sgu_lo_made")
        rope_ang = sem("rope_ang")
        rope_sin = sem("rope_sin")
        qk_ready = sem("qk_ready")
        rotated = sem("rotated")
        roped = sem("roped")
        win_turned = sem("win_turned")
        win_ready = sem("win_ready")
        conv_lo_made = sem("conv_lo_made")
        scored = sem("scored")
        shifted = sem("shifted")
        exped = sem("exped")
        probs_made = sem("probs_made")
        turned = sem("turned")
        pt_made = sem("pt_made")
        att_out = sem("att_out")
        att_lo_made = sem("att_lo_made")
        dt_arg = sem("dt_arg")
        dt_sin = sem("dt_sin")
        tab_arg = sem("tab_arg")
        tab_made = sem("tab_made")
        v_mul = sem("v_mul")
        v_out = sem("v_out")
        rt_made = sem("rt_made")
        scanned = sem("scanned")
        st_re_made = sem("st_re_made")
        st_im_made = sem("st_im_made")
        y_mul = sem("y_mul")
        y_out = sem("y_out")
        y_gelu = sem("y_gelu")
        glu_mul = sem("glu_mul")
        glu_sig = sem("glu_sig")
        ssm_out = sem("ssm_out")
        ssm_hi_made = sem("ssm_hi_made")
        ssm_lo_made = sem("ssm_lo_made")
        stored = sem("stored")

        block = ctx.enter_context(nc.Block())

        @block.sync
        def _(sp):
            def load(c, u, width, src):
                sp.wait_ge(lo_made, c + 1)
                sp.dma_start(w_raw[:, u, 0:width], src).then_inc(raw_landed[u], 16)

            def load_phase(c0, n, width, dram, row0):
                with sp.Fori(0, n // 2) as i:
                    for u in range(2):
                        load(c0 + 2 * i + u, u, width, dram[row0 + 2 * i + u])

            with sp.Fori(0, DEPTH) as l:
                c = l * CHUNKS
                load_phase(c + C_UP[0], UP_CH, W8, w_up, l * 2 * UP_CH)
                for dst, dram in ((wb, ssm_b), (wc, ssm_c)):
                    sp.dma_start(dst[:], dram[l]).then_inc(state_landed, 16)
                load_phase(c + C_DOWN[0], DOWN_CH, W11, w_down, l * 2 * DOWN_CH)
                load_phase(c + C_IN, 4, W8, w_in, l * IN_CH)
                sp.wait_ge(chunk_done, c + C_IN + 2)
                for dst, dram in ((wglu, glu_w), (wsgu, sgu_w), (bsgu, sgu_bias)):
                    sp.dma_start(dst[:], dram[l]).then_inc(small_landed, 16)
                for r in range(2):
                    sp.dma_start(lnr[:, r, :], ln_rows[l, r:r + 1, :].partition_broadcast(P)).then_inc(small_landed, 16)
                sp.dma_start(rope_pos[:], pos_in.partition_broadcast(P)).then_inc(small_landed, 16)
                load_phase(c + C_IN + 4, IN_CH - 4, W8, w_in, l * IN_CH + 4)
                for b in range(4):
                    load_phase(c + C_MIX + KD * b, KD, MIX_W[b], mix_dram[b], l * KD)
                load_phase(c + C_OUT, OUT_CH, W8, w_out, l * OUT_CH)
                load_phase(c + C_UP[1], UP_CH, W8, w_up, l * 2 * UP_CH + UP_CH)
                load_phase(c + C_DOWN[1], DOWN_CH, W11, w_down, l * 2 * DOWN_CH + DOWN_CH)
            for i in range(1, X_UNITS, 2):
                h, k = i // KD, i % KD - 1
                sp.wait_ge(x_new, 3 * X_UNITS * DEPTH + i + 1)
                sp.dma_start(out[:, k:k + 2, h * H:(h + 1) * H], x[:, k:k + 2, h * H:(h + 1) * H]).then_inc(stored, 16)
            sp.wait_ge(stored, 16 * KD)

        @block.tensor
        def _(pe):
            def product(ps, slot, blk, hi, lo, start, stop):
                wh = w_hi[:, slot, blk * P:(blk + 1) * P]
                pe.matmul(ps, wh, hi, start=start, stop=False)
                pe.matmul(ps, wh, lo, start=False, stop=False)
                return pe.matmul(ps, w_lo[:, slot, blk * P:(blk + 1) * P], hi, start=False, stop=stop)

            def chunk_ready(c):
                pe.wait_ge(lo_made, c + 3)

            def norm_sums(l, r, h=None):
                pe.wait_ge(sq_added, 6 * (l * N_NORMS + r + 1))
                pe.wait_ge(sq_made, squares_before(l, r) + KD + (h or 0))
                for b in range(TB) if h is None else range(2 * h, 2 * h + 2):
                    pe.matmul(ps6[:, b:b + 1], sq_sum[:, b * P:(b + 1) * P], ones[:, 0:1], start=True, stop=False)
                    mm = pe.matmul(ps6[:, b:b + 1], sq[:, 1, b * P:(b + 1) * P], ones[:, 0:1], start=False, stop=True)
                mm.then_inc(sums_made, 2 if h is None else 1)

            def norm_spread(l, r, h=None):
                pe.wait_ge(diag_made, 2 * (l * N_NORMS + r) + (2 if h is None else h + 1))
                if h is None:
                    mm = pe.matmul(ps7[:], ones[:], diag[:].rearrange("p b n -> p (b n)"), start=True, stop=True)
                else:
                    mm = pe.matmul((ps7, ps_v)[h][:, 0:H], ones[:],
                                   diag[:, 2 * h:2 * h + 2, :].rearrange("p b n -> p (b n)"), start=True, stop=True)
                mm.then_inc(rstd_spread, 2 if h is None else 1)

            def first_chunks(l, r, c, a, banks):
                xr = (3 * l + r // 2) * X_UNITS
                for u in range(2):
                    pe.wait_ge(acc_free, a + u + 1)
                if r == 0:
                    for u in range(2):
                        chunk_ready(c + u)
                        for k in range(KD):
                            if u == 0:
                                pe.wait_ge(xlo_made, xr + 2 * k + 2)
                            mm = product(banks[u][:], u, k, x_hi[:, k, :], x_lo[:, k, :], k == 0, k == KD - 1)
                        mm.then_inc(chunk_done, 1)
                    return

                def half_tile(h, u, k):
                    hs = slice(h * H, (h + 1) * H)
                    mm = product(banks[u][:, hs], u, k, x_hi[:, k, hs], x_lo[:, k, hs], k == 0, k == KD - 1)
                    if h == 1 and k == KD - 1:
                        mm.then_inc(chunk_done, 1)

                sums_at, spread_at = (None, 2) if r == 4 else (0, 3)
                if sums_at is None:
                    norm_sums(l, r - 1, 1)
                chunk_ready(c)
                for h in range(2):
                    for k in range(KD):
                        pe.wait_ge(xlo_made, xr + KD * h + k + 1)
                        half_tile(h, 0, k)
                        if h == 0 and k == sums_at:
                            norm_sums(l, r - 1, 1)
                        if h == 0 and k == spread_at:
                            norm_spread(l, r - 1, 1)
                    if h == 0:
                        chunk_ready(c + 1)
                    for k in range(KD):
                        half_tile(h, 1, k)

            def last_tile(l, r, c, blocks, hi, lo):
                total = sum(blocks)
                for h in range(2):
                    hs = slice(h * H, (h + 1) * H)
                    k = 0
                    for part, n in enumerate(blocks):
                        if h == 0:
                            chunk_ready(c + part)
                        for b in range(n):
                            slot = (len(blocks) + part) % 2
                            mm = product(acc[1][h][:, 0:H], slot, b, hi[:, k, hs], lo[:, k, hs], k == 0, k == total - 1)
                            if h == 1 and k == total // 4:
                                norm_sums(l, r, 0)
                            if h == 1 and k == max(total // 2, KD - 1):
                                norm_spread(l, r, 0)
                            k += 1
                        if h == 1:
                            mm.then_inc(chunk_done, 1)
                    if h == 0:
                        mm.then_inc(half_done, 1)

            def up_step(c, a, banks, norm=None):
                if banks != spare:
                    pe.wait_ge(acc_free, a + 1)
                for part in range(2):
                    chunk_ready(c + part)
                    for k in range(KD):
                        mm = product(banks[part][:], part, k, x_hi[:, k, :], x_lo[:, k, :], k == 0, k == KD - 1)
                        if k == KD - 1:
                            mm.then_inc(chunk_done, 1)
                        if norm is not None and (part, k) == (0, 4):
                            norm_sums(*norm)
                        if norm is not None and (part, k) == (1, 1):
                            norm_spread(*norm)

            def ffn(l, f):
                c, a = l * CHUNKS + C_UP[f], l * STEPS + A_UP[f]
                first_chunks(l, 4 * f, c, a, acc[0])
                up_step(c + 2, a + 1, acc[1], (l, 4 * f))
                up_step(c + 4, a + 2, spare)
                up_step(c + 6, a + 3, acc[1])
                with pe.Fori(2, KF // 2) as i:
                    for u in range(2):
                        up_step(c + 4 * i + 2 * u, a + 2 * i + u, acc[u])
                c, a = l * CHUNKS + C_DOWN[f], l * STEPS + A_DOWN[f]
                hid = (2 * l + f) * KF

                def down_step(c, a, u):
                    pe.wait_ge(acc_free, a + 1)
                    for part in range(2):
                        chunk_ready(c + part)
                        pe.wait_ge(hid_lo_made, hid + KF2 * (part + 1))
                        for b in range(KF2):
                            k = KF2 * part + b
                            mm = product(acc[u][0][:], part, b, hid_hi[:, k, :], hid_lo[:, k, :], k == 0, k == KF - 1)
                        mm.then_inc(chunk_done, 1)

                with pe.Fori(0, KD // 2 - 1) as i:
                    for u in range(2):
                        down_step(c + 4 * i + 2 * u, a + 2 * i + u, u)
                down_step(c + 2 * KD - 4, a + KD - 2, 0)
                pe.wait_ge(acc_free, a + KD)
                c = c + 2 * KD - 2
                last_tile(l, 4 * f + 1, c, (KF2, KF2), hid_hi, hid_lo)

            with pe.Fori(0, DEPTH) as l:
                ffn(l, 0)

                def sgu_turn():
                    pe.wait_ge(sgu_g, 4 * l + 2)
                    for b in range(TB):
                        for t in range(2):
                            mm = pe.transpose((ps6, ps7)[b // 2][:, (b % 2 * 2 + t) * P:(b % 2 * 2 + t + 1) * P],
                                              sgu_v[:, t, b * P:(b + 1) * P], ident[:])
                    mm.then_inc(sgu_turned, 1)

                def sgu_mix():
                    pe.wait_ge(roped, 5 * l + 5)
                    pe.wait_ge(sgu_normed, l + 1)
                    for t in range(2):
                        for b in range(TB):
                            for g in range(2):
                                h = 2 * t + g
                                mm = pe.matmul((ps6, ps7)[t][64 * g:64 * g + 64, b * P:(b + 1) * P],
                                               v_tok[:, b, 64 * h:64 * h + 64], wsgu[:, h, :], start=True, stop=True)
                    mm.then_inc(sgu_mixed, 1)

                def rotate(i):
                    pe.wait_ge(qk_ready, 6 * l + (1 if i == 0 else 2 + i))
                    pe.wait_ge(sgu_var, l + 1)
                    if i >= 2:
                        pe.wait_ge(roped, 5 * l + i - 1)
                    src = k_pad[:, CHUNK:] if i == 0 else q[:, :, i - 1, :]
                    pe.matmul((ps6, ps7)[i % 2][:], rot[:], src, start=True, stop=True).then_inc(rotated, 1)

                def windows():
                    pe.wait_ge(sgu_biased, 2 * l + 2)
                    pe.wait_ge(qk_ready, 6 * l + 6)
                    for half in range(2):
                        for w in range(4):
                            c = 4 * half + w
                            mm = pe.transpose((ps6, ps7)[half][:, w * P:(w + 1) * P],
                                              v_pad[:, CHUNK * c:CHUNK * c + P], ident[:])
                        mm.then_inc(win_turned, 1)

                def scores(c):
                    if c == 0:
                        pe.wait_ge(win_ready, 2 * l + 2)
                    else:
                        pe.wait_ge(shifted, N_WIN * l + c)
                    for kv in range(2):
                        if kv:
                            pe.drain()
                        for pair in range(2):
                            j = 2 * kv + pair
                            mm = pe.matmul(ps6[:, j * P:(j + 1) * P],
                                           q[64 * kv:64 * kv + 64, c, 2 * pair:2 * pair + 2, :].rearrange("p a b -> p (a b)"),
                                           k_pad[64 * kv:64 * kv + 64, CHUNK * c:CHUNK * c + P], start=True, stop=True)
                    mm.then_inc(scored, 1)

                def turn_probs(c):
                    pe.wait_ge(probs_made, N_WIN * l + c + 1)
                    if c:
                        pe.wait_ge(att_lo_made, N_WIN * l + c)
                    for j in range(4):
                        mm = pe.transpose(ps7[:, j * P:(j + 1) * P], att_e[:, j, :], ident[:])
                    mm.then_inc(turned, 1)

                def attend(c):
                    pe.wait_ge(pt_made, N_WIN * l + c + 1)
                    for kv in range(2):
                        mm = pe.matmul(ps7[64 * kv:64 * kv + 64, 0:2 * P], v_win[:, c, 64 * kv:64 * kv + 64],
                                       att_pt[:, 2 * kv:2 * kv + 2, :].rearrange("p a b -> p (a b)"),
                                       start=True, stop=True)
                    mm.then_inc(att_out, 1)

                def ssm_in(j, bank_im):
                    if j == 0:
                        pe.wait_ge(state_landed, 32 * l + 32)
                        pe.wait_ge(u_ready, 2 * l + 2)
                    else:
                        pe.wait_ge(v_out, N_STATE_TILES * l + j)
                    r = 32 * (j % 4)
                    u = u_ssm[r:r + 32, j // 4, :]
                    pe.matmul(ps_v[:], wb[r:r + 32, j // 4, 0, :], u, start=True, stop=True)
                    pe.matmul(bank_im[:], wb[r:r + 32, j // 4, 1, :], u, start=True, stop=True).then_inc(v_mul, 1)

                def ssm_y(j):
                    pe.wait_ge(st_re_made, N_STATE_TILES * l + j + 1)
                    pe.wait_ge(st_im_made, N_STATE_TILES * l + j + 1)
                    if j == 4:
                        pe.wait_ge(y_out, 2 * l + 1)
                    r = 32 * (j % 4)
                    pe.matmul(ps_y[r:r + 32, :], wc2[:, 0, j, :], rt_re[:], start=True, stop=False)
                    pe.matmul(ps_y[r:r + 32, :], wc2[:, 1, j, :], rt_im[:], start=False, stop=True).then_inc(y_mul, 1)

                def glu():
                    pe.wait_ge(y_gelu, 2 * l + 2)
                    pe.wait_ge(att_lo_made, N_WIN * (l + 1))
                    for m in range(2):
                        for k in range(2):
                            mm = pe.matmul((ps6, ps7)[m][:], wglu[:, k, m * P:(m + 1) * P], u_ssm[:, k, :],
                                           start=(k == 0), stop=(k == 1))
                        mm.then_inc(glu_mul, 1)

                def side_work(t):
                    if t - 4 in T_SSM:
                        ssm_y(T_SSM[t - 4])
                    if t == T_SGU_TURN:
                        sgu_turn()
                    if t == T_SGU_MIX:
                        sgu_mix()
                    for i in T_ROPE.get(t, ()):
                        rotate(i)
                    if t == T_WINDOWS:
                        windows()
                    if att_group(t - 4) is not None:
                        attend(att_group(t - 4))
                    if att_group(t - 3) is not None:
                        turn_probs(att_group(t - 3))
                    if att_group(t) is not None:
                        scores(att_group(t))
                    if t == T_GLU:
                        glu()

                c, a = l * CHUNKS + C_IN, l * STEPS + A_IN
                first_chunks(l, 2, c, a, in_bank[:2])
                for s in range(2, N_IN):
                    if s >= 5:
                        pe.wait_ge(acc_free, a + s + 1)
                    side_work(s)
                    if s in T_SSM:
                        ssm_in(T_SSM[s], acc[s % 2][1])
                    chunk_ready(c + s)
                    for k in range(KD):
                        mm = product(in_bank[s][:], s % 2, k, x_hi[:, k, :], x_lo[:, k, :], k == 0, k == KD - 1)
                        if k == KD - 1:
                            mm.then_inc(chunk_done, 1)
                        if (s, k) == (2, 4):
                            norm_sums(l, 2)
                        if (s, k) == (3, 1):
                            norm_spread(l, 2)

                parts = ((conv_hi, conv_lo), (sgu_hi, sgu_lo), (att_hi, att_lo), (ssm_hi, ssm_lo))

                def mix_step(b, c, a, u, t):
                    pe.wait_ge(acc_free, a + 1)
                    if t is not None:
                        side_work(t)
                        if t in T_SSM:
                            ssm_in(T_SSM[t], acc[u][1])
                    chunk_ready(c)
                    for k in range(KD):
                        product(acc[u][0][:], u, k, x_hi[:, k, :], x_lo[:, k, :], k == 0, k == KD - 1)
                    for s, count in ((conv_lo_made, 2), (sgu_lo_made, 2), (att_lo_made, N_WIN), (ssm_lo_made, 2))[b:b + 1]:
                        pe.wait_ge(s, count * l + count)
                    if t in T_SSM:
                        pe.wait_ge(v_out, N_STATE_TILES * l + T_SSM[t] + 1)
                    hi, lo = parts[b]
                    for k in range(BRANCH_K[b]):
                        at = (slice(None), slice(None), k) if b == ATT else (slice(None), k)
                        mm = product(acc[u][1][:], u, KD + k, hi[at], lo[at], k == 0, k == BRANCH_K[b] - 1)
                    mm.then_inc(chunk_done, 1)

                for b in range(3):
                    for s in range(KD):
                        t = N_IN + KD * b + s
                        mix_step(b, l * CHUNKS + C_MIX + KD * b + s, l * STEPS + A_MIX + KD * b + s, s % 2, t)
                with pe.Fori(0, KD // 2) as i:
                    for u in range(2):
                        s = 3 * KD + 2 * i + u
                        mix_step(SSM, l * CHUNKS + C_MIX + s, l * STEPS + A_MIX + s, u, None)

                def out_step(n, u, first=False):
                    pe.wait_ge(acc_free, l * STEPS + A_OUT + n + 1)
                    chunk_ready(l * CHUNKS + C_OUT + n)
                    for k in range(KD):
                        if first:
                            pe.wait_ge(mrg_lo_made, KD * l + k + 1)
                        mm = product(acc[u][0][:], u, k, mrg_hi[:, k, :], mrg_lo[:, k, :], k == 0, k == KD - 1)
                    mm.then_inc(chunk_done, 1)

                out_step(0, 0, True)
                out_step(1, 1)
                with pe.Fori(1, KD // 2 - 1) as i:
                    for u in range(2):
                        out_step(2 * i + u, u)
                out_step(KD - 2, 0)
                pe.wait_ge(acc_free, l * STEPS + A_OUT + KD)
                last_tile(l, 3, l * CHUNKS + C_OUT + KD - 1, (KD,), mrg_hi, mrg_lo)
                ffn(l, 1)
                norm_sums(l, 5, 1)
                norm_spread(l, 5, 1)

        @block.scalar
        def _(act):
            def upper(c, u, width):
                act.wait_ge(raw_landed[u], 8 * (c - u) + 16)
                act.wait_ge(chunk_done, c + 1)
                act.activation(w_hi[:, u, 0:width], w_raw[:, u, 0:width], ACT.Copy).then_inc(hi_made, 1)

            def square(l, r, k, src, h=None):
                hs = slice(None) if h is None else slice(h * H, (h + 1) * H)
                if k == 0:
                    act.activation(sq_sum[:], src, ACT.Square).then_inc(sq_made, 1)
                    return
                if k >= 3:
                    act.wait_ge(sq_added, 6 * (l * N_NORMS + r) + k - 2)
                act.activation(sq[:, k % 2, hs], src, ACT.Square).then_inc(sq_made, 1)

            def x_half_upper(l, p, i):
                h, k = i // KD, i % KD
                g = PC_GAIN + 2 * KD * p + k
                act.wait_ge(x_new, X_UNITS * (3 * l + p) + i + 1)
                act.activation(x_hi[:, k, h * H:(h + 1) * H], x[:, k, h * H:(h + 1) * H], ACT.Copy,
                               scale=prm[:, g:g + 1]).then_inc(xhi_made, 1)

            def x_squares(l, p, c):
                for k in range(KD):
                    square(l, 2 * p, k, x[:, k, :])
                    if k == 3:
                        upper(c, 0, W8)

            def x_upper(l):
                for k in range(KD):
                    g = PC_GAIN + k
                    act.wait_ge(x_new, X_UNITS * 3 * l + KD + k + 1)
                    act.activation(x_hi[:, k, :], x[:, k, :], ACT.Copy, scale=prm[:, g:g + 1]).then_inc(xhi_made, 2)
                    if k == 3:
                        upper(l * CHUNKS + 1, 1, W8)

            def last_tile(l, p, c=None):
                def last_square(h):
                    act.wait_ge(h_made, (KD + 1) * (3 * l + p) + KD + h)
                    square(l, 2 * p + 1, KD - 1, h_out[:, KD - 1, h * H:(h + 1) * H], h)
                last_square(0)
                if p == 0:
                    upper(c, 0, W8)
                if p == 2:
                    last_square(1)
                    return
                square_at, upper_at = (0, 1) if p == 1 else (2, 3)
                for i in range(X_UNITS):
                    if i == square_at:
                        last_square(1)
                    x_half_upper(l, p + 1, i)
                    if i == upper_at:
                        upper(c + 1, 1, W8)
                x_squares(l, p + 1, c + 2)

            def up_step(l, f, m, u, next_w):
                c, h = l * CHUNKS + C_UP[f] + 2 * m, (2 * l + f) * KF + m
                first, second = (isinstance(m, int) and m == i for i in range(2))
                if first:
                    upper(c + 3, 1, next_w)
                    upper(c + 4, 0, next_w)
                elif not second:
                    upper(c + 2, 0, next_w)
                act.wait_ge(a_made, h + 1)
                act.activation(up_s[:, u, :], up_a[:, u, :], ACT.Silu).then_inc(silu_made, 1)
                if not first:
                    upper(c + 3, 1, next_w)
                act.wait_ge(hid_made, h + 1)
                act.activation(hid_hi[:, bass.ds(m, 1), :], up_h[:, u:u + 1, :], ACT.Copy).then_inc(hid_hi_made, 1)

            def ffn(l, f):
                up_step(l, f, 0, 0, W8)
                up_step(l, f, 1, 1, W8)
                with act.Fori(1, KF // 2 - 1) as i:
                    for u in range(2):
                        up_step(l, f, 2 * i + u, u, W8)
                up_step(l, f, KF - 2, 0, W8)
                up_step(l, f, KF - 1, 1, W11)
                for n in range(KD - 1):
                    c = l * CHUNKS + C_DOWN[f] + 2 * n
                    upper(c + 2, 0, W11)
                    act.wait_ge(h_made, (KD + 1) * (3 * l + 2 * f) + n + 1)
                    square(l, 4 * f + 1, n, h_out[:, n, :])
                    upper(c + 3, 1, W11)
                    if f == 0 and n == 4:
                        act.wait_ge(dt_arg, l + 1)
                        act.activation(sm[:, SM_T0, :], sm[:, SM_Y, :], ACT.Sin)
                        act.activation(sm[:, SM_T1, :], sm[:, SM_Y, :], ACT.Sin, scale=0.5).then_inc(dt_sin, 1)
                last_tile(l, 2 * f, l * CHUNKS + C_IN)

            act.dma_start(params_all[:], params_in).then_inc(params_landed, 16)
            act.wait_ge(acc_free, 2)
            act.activation(rs[:], rs[:], ACT.Copy)
            for k in range(0, KD, 2):
                act.dma_start(x[:, k:k + 2, :], x_in[:, k:k + 2, :]).then_inc(x_landed[k // 2], 16)
            act.dma_start(consts[:], consts_in).then_inc(consts_landed, 16)
            with act.Fori(0, DEPTH) as l:
                upper(l * CHUNKS, 0, W8)
                act.wait_ge(prm_ready, l + 1)
                x_upper(l)
                x_squares(l, 0, l * CHUNKS + 2)
                ffn(l, 0)

                def state_inputs(j, bank_im):
                    g = N_STATE_TILES * l + j
                    if j:
                        act.wait_ge(y_mul, g)
                    act.wait_ge(v_mul, g + 1)
                    act.activation(st_im[:], bank_im[:], ACT.Copy)
                    act.activation(st_re[:], ps_v[:], ACT.Copy).then_inc(v_out, 1)

                def tables(j):
                    g = N_STATE_TILES * l + j
                    act.wait_ge(tab_arg, g + 1)
                    if j > 1:
                        act.wait_ge(st_re_made, g - 1)
                        act.wait_ge(st_im_made, g - 1)
                    c, s = tab_c[:, j % 2, :], tab_s[:, j % 2, :]
                    act.activation(s, c, ACT.Sin, scale=2 * PI_F)
                    act.drain()
                    act.activation(c, c, ACT.Sin, scale=PI_F)
                    act.drain()
                    act.activation(c, c, ACT.Square)
                    act.drain()
                    act.activation(c, c, ACT.Copy, scale=-2.0, bias=1.0).then_inc(tab_made, 1)

                def side_work(t):
                    if t == 2:
                        act.wait_ge(rstd_made, 3 * l + 2)
                        act.dma_start(time_f[:], time_in).then_inc(time_landed, 16)
                    for i, at in enumerate((2, 3, 16, 17)):
                        if t == at:
                            z = (sgu_v if i < 2 else sgu_u)[:, i % 2, :]
                            act.wait_ge(sgu_z, 4 * l + i + 1)
                            act.activation(z, z, ACT.Gelu_apprx_tanh).then_inc(sgu_g, 1)
                    if t + 2 in T_SSM:
                        tables(T_SSM[t + 2])
                    if t == T_SGU_GATE + 1:
                        for i in range(2):
                            act.wait_ge(sgu_done, 2 * l + i + 1)
                            act.activation(sgu_hi[:, i, :], sgu_u[:, i, :], ACT.Copy).then_inc(sgu_hi_made, 1)
                    if t == 5:
                        act.wait_ge(rope_ang, l + 1)
                        act.activation(rope_s[:], rope_c[:], ACT.Sin)
                        act.drain()
                        act.activation(rope_c[:], rope_c[:], ACT.Sin, scale=0.5)
                        act.drain()
                        act.activation(rope_c[:], rope_c[:], ACT.Square).then_inc(rope_sin, 1)
                    if t == T_WINDOWS - 1:
                        for half in range(2):
                            act.wait_ge(win_turned, 2 * l + half + 1)
                            act.activation(v_win[:, 4 * half:4 * half + 4, :].rearrange("p a b -> p (a b)"),
                                           (ps6, ps7)[half][:], ACT.Copy).then_inc(win_ready, 1)
                    c = att_group(t - 2)
                    if c is not None:
                        act.wait_ge(turned, N_WIN * l + c + 1)
                        act.activation(att_pt[:].rearrange("p a b -> p (a b)"), ps7[:], ACT.Copy).then_inc(pt_made, 1)
                    c = att_group(t)
                    if c is not None:
                        act.wait_ge(shifted, N_WIN * l + c + 1)
                        keys = att_e[:, :, CHUNK:] if c == 0 else att_e[:]
                        act.activation(keys, keys, ACT.Exp)
                        act.activation(asm[:, 3, :], asm[:, 2, :], ACT.Exp).then_inc(exped, 1)
                    if T_SSM_OUT.get(t) == 1:
                        for i in range(2):
                            act.wait_ge(y_out, 2 * l + i + 1)
                            act.activation(u_ssm[:, i, :], u_ssm[:, i, :], ACT.Gelu_apprx_tanh).then_inc(y_gelu, 1)
                    if t == T_GLU - 1:
                        for i in range(2):
                            act.wait_ge(glu_mul, 2 * l + i + 1)
                            act.activation((st_re, st_im)[i][:], (ps6, ps7)[i][:], ACT.Sigmoid).then_inc(glu_sig, 1)
                    if t == T_GLU:
                        for i in range(2):
                            act.wait_ge(ssm_out, 2 * l + i + 1)
                            act.activation(ssm_hi[:, i, :], u_ssm[:, i, :], ACT.Copy).then_inc(ssm_hi_made, 1)

                for s in range(N_IN):
                    if s in T_SSM:
                        state_inputs(T_SSM[s], acc[s % 2][1])
                    if s:
                        upper(l * CHUNKS + C_IN + s + 2, s % 2, W8 if s < N_IN - 2 else MIX_W[0])
                    side_work(s)

                for s in range(4 * KD):
                    b, n, u = s // KD, s % KD, s % 2
                    nb = (s + 2) // KD
                    if N_IN + s in T_SSM:
                        state_inputs(T_SSM[N_IN + s], acc[u][1])
                    upper(l * CHUNKS + C_MIX + s + 2, u, MIX_W[nb] if nb < 4 else W8)
                    if s > KD + 1:
                        act.wait_ge(merged_added, 3 * KD * l + s - KD - 1)
                    bg = PC_BGATE + s
                    act.wait_ge(gate_scaled, 4 * KD * l + s + 1)
                    act.activation(gate[:, u, :], gate_in[:, u, :], ACT.Sigmoid, bias=prm[:, bg:bg + 1])\
                       .then_inc(gate_made, 1)
                    if b == SSM:
                        act.wait_ge(merged_added, 3 * KD * l + s - KD + 1)
                        act.activation(mrg_hi[:, n, :], merged[:, n, :], ACT.Copy).then_inc(mrg_hi_made, 1)
                    side_work(N_IN + s)
                for n in range(KD - 1):
                    upper(l * CHUNKS + C_OUT + n + 2, n % 2, W8)
                    act.wait_ge(h_made, (KD + 1) * (3 * l + 1) + n + 1)
                    square(l, 3, n, h_out[:, n, :])
                last_tile(l, 1, l * CHUNKS + C_UP[1])
                ffn(l, 1)

        @block.gpsimd
        def _(pool):
            pool.wait_ge(set_up, 1)
            for k in range(KD):
                pool.wait_ge(x_landed[k // 2], 16)
                pool.sem_inc(x_new, 1 if k else KD + 1)

            def output_norm(l, p):
                r = 2 * p + 1
                for k in range(1, KD - 1):
                    pool.wait_ge(sq_made, squares_before(l, r) + k + 1)
                    pool.tensor_tensor(sq_sum[:], sq_sum[:], sq[:, k % 2, :], ALU.add).then_inc(sq_added, 1)
                    pool.drain()
                inverse_root(l, r, 0)
                for i in range(1, X_UNITS):
                    h, k = i // KD, i % KD
                    pool.wait_ge(tmp_made, X_UNITS * (3 * l + p) + i + 1)
                    if i == 1:
                        pool.wait_ge(x_new, X_UNITS * (3 * l + p + 1) + 1)
                    xk = x[:, k, h * H:(h + 1) * H]
                    pool.tensor_tensor(xk, xk, h_out[:, k, h * H:(h + 1) * H], ALU.add).then_inc(x_new, 1)
                    if i == (4, 2, 5)[p]:
                        inverse_root(l, r, 1)

            def inverse_root(l, r, h=None):
                b = slice(None) if h is None else slice(2 * h, 2 * h + 2)
                pool.wait_ge(mean_made, 2 * (l * N_NORMS + r) + (2 if h is None else h + 1))
                pool.tensor_tensor(rs[:, b], mean_sq[:, b], minus_half[:, b], ALU.pow).then_inc(rs_made, 2 if h is None else 1)

            def ffn(l, f):
                inverse_root(l, 4 * f)
                with pool.Fori(0, KF // 2) as i:
                    for u in range(2):
                        h = (2 * l + f) * KF + 2 * i + u
                        pool.wait_ge(silu_made, h + 1)
                        pool.wait_ge(acc_free, l * STEPS + A_UP[f] + 2 * i + u + 3)
                        pool.tensor_tensor(up_h[:, u, :], up_s[:, u, :], up_b[:, u, :], ALU.mult).then_inc(hid_made, 1)
                output_norm(l, 2 * f)

            with pool.Fori(0, DEPTH) as l:
                ffn(l, 0)
                inverse_root(l, 2)

                def turn(j, out, a, b, op):
                    pool.tensor_tensor(out[:], tab_c[:, j % 2, :], a[:], ALU.mult)
                    pool.tensor_tensor(prod[:], tab_s[:, j % 2, :], b[:], ALU.mult)
                    pool.drain()
                    ins = pool.tensor_tensor(out[:], out[:], prod[:], op)
                    return ins

                for t in range(N_IN + 4 * KD):
                    if t in T_SSM:
                        j = T_SSM[t]
                        g = N_STATE_TILES * l + j
                        pool.wait_ge(tab_made, g + 1)
                        pool.wait_ge(v_out, g + 1)
                        turn(j, rt_re, st_re, st_im, ALU.add)
                        pool.drain()
                        turn(j, rt_im, st_im, st_re, ALU.subtract).then_inc(rt_made, 1)
                        pool.drain()
                    if t == T_GLU - 1:
                        for i in range(2):
                            pool.wait_ge(glu_sig, 2 * l + 2)
                            pool.tensor_tensor(u_ssm[:, i, :], u_ssm[:, i, :], (st_re, st_im)[i][:], ALU.mult)\
                                .then_inc(ssm_out, 1)
                    if t >= N_IN + KD:
                        s = t - N_IN
                        pool.wait_ge(gated, 4 * KD * l + s + 1)
                        pool.tensor_tensor(merged[:, s % KD, :], merged[:, s % KD, :], gate[:, s % 2, :], ALU.add)\
                            .then_inc(merged_added, 1)
                    if t - 1 in T_SSM:
                        j = T_SSM[t - 1]
                        pool.wait_ge(scanned, N_STATE_TILES * l + j + 1)
                        turn(j, rt_re, st_re, st_im, ALU.subtract).then_inc(st_re_made, 1)
                        pool.drain()
                        if j >= POOL_TURNS_FROM:
                            turn(j, rt_im, st_im, st_re, ALU.add).then_inc(st_im_made, 1)
                            pool.drain()
                    if t == T_SGU_TURN + 2:
                        pool.wait_ge(sgu_var, l + 1)
                        pool.tensor_tensor(lnrs[:], lnrs[:], minus_half[:], ALU.pow)
                        pool.drain()
                        for b in range(TB):
                            pool.tensor_scalar(v_tok[:, b, :], v_tok[:, b, :], lnmv[:, b, 0:1], lnrs[:, b:b + 1],
                                               ALU.subtract, ALU.mult)
                        pool.drain()
                        for r, op in ((0, ALU.mult), (1, ALU.add)):
                            ins = pool.tensor_tensor(v_tok[:], v_tok[:],
                                                     lnr[:, r:r + 1, :].to_broadcast([P, TB, 2 * P]), op)
                            if r == 0:
                                pool.drain()
                        ins.then_inc(sgu_normed, 1)
                    if t == T_SGU_GATE:
                        for i in range(2):
                            pool.wait_ge(sgu_g, 4 * l + i + 3)
                            pool.tensor_tensor(sgu_u[:, i, :], sgu_u[:, i, :], sgu_v[:, i, :], ALU.mult)\
                                .then_inc(sgu_done, 1)
                output_norm(l, 1)
                ffn(l, 1)

        @block.vector
        def _(dve):
            dve.memset(ones[:], 1.0)
            dve.memset(minus_half[:], -0.5).then_inc(set_up, 1)
            dve.memset(mean_sq[:], 0.0).then_inc(lo_made, 2)
            dve.memset(rs[:], 0.0).then_inc(chunk_done, 2)
            dve.memset(diag[:, 0, 0:8], 0.0).then_inc(acc_free, 2)
            dve.wait_ge(params_landed, 16)

            def lower(c, u, width):
                dve.wait_ge(hi_made, c + 1)
                dve.tensor_tensor(w_lo[:, u, 0:width], w_raw[:, u, 0:width], w_hi[:, u, 0:width].bitcast(F32),
                                  ALU.subtract).then_inc(lo_made, 1)

            def mean(l, r, h=None):
                b = slice(0, TB) if h is None else slice(2 * h, 2 * h + 2)
                v = 2 if h is None else 1
                dve.wait_ge(sums_made, 2 * (l * N_NORMS + r) + (h or 0) + v)
                dve.tensor_scalar(mean_sq[:, b], ps6[:, b], 1.0 / D_MODEL, RMS_EPS, ALU.mult, ALU.add)\
                   .then_inc(mean_made, v)

            def make_diag(l, r, h=None):
                b = slice(0, TB) if h is None else slice(2 * h, 2 * h + 2)
                n, v = (TB, 2) if h is None else (2, 1)
                dve.wait_ge(rs_made, 2 * (l * N_NORMS + r) + (h or 0) + v)
                dve.tensor_tensor(diag[:, b], ident[:].unsqueeze(1).to_broadcast([P, n, P]),
                                  rs[:, b].unsqueeze(2).to_broadcast([P, n, P]), ALU.mult).then_inc(diag_made, v)

            def pre_norm(l, r, c, chunks):
                for k in range(1, KD - 1):
                    dve.wait_ge(sq_made, squares_before(l, r) + k + 1)
                    dve.tensor_tensor(sq_sum[:], sq_sum[:], sq[:, k % 2, :], ALU.add).then_inc(sq_added, 1)
                    dve.drain()
                    if k == 2:
                        lower(c, 0, W8)
                lower(c + 1, 1, W8)
                mean(l, r)
                dve.wait_ge(consts_landed, 16)
                make_diag(l, r)
                if chunks == 3:
                    lower(c + 2, 0, W8)
                dve.wait_ge(rstd_spread, 2 * (l * N_NORMS + r) + 2)
                dve.tensor_copy(rstd[:], ps7[:]).then_inc(rstd_made, 1)
                dve.drain()

            def x_lower(l, r, k, h=None):
                g = PC_GAIN + 2 * KD * r + k
                hs = slice(None) if h is None else slice(h * H, (h + 1) * H)
                done = 2 * k + 2 if h is None else KD * h + k + 1
                dve.wait_ge(xhi_made, X_UNITS * (3 * l + r) + done)
                dve.scalar_tensor_tensor(x_lo[:, k, hs], x[:, k, hs], prm[:, g:g + 1], x_hi[:, k, hs].bitcast(F32),
                                         ALU.mult, ALU.subtract).then_inc(xlo_made, 2 if h is None else 1)

            def last_tile(l, p, last, c=None):
                r = 2 * p + 1

                def out_half(h):
                    dve.tensor_copy(h_out[:, KD - 1, h * H:(h + 1) * H], acc[1][h][:, 0:H]).then_inc(h_made, 1)

                def scale(i):
                    h, k = i // KD, i % KD
                    g = PC_GAIN + KD * r + k
                    hk = h_out[:, k, h * H:(h + 1) * H]
                    if k == 0:
                        dve.wait_ge(rstd_spread, 2 * (l * N_NORMS + r) + h + 1)
                    dve.scalar_tensor_tensor(hk, hk, prm[:, g:g + 1], (ps7, ps_v)[h][:, 0:H], ALU.mult, ALU.mult)\
                       .then_inc(tmp_made, 1)

                def second_half():
                    dve.wait_ge(chunk_done, last + 3)
                    out_half(1)
                    dve.wait_ge(h_made, (KD + 1) * (3 * l + p + 1))
                    dve.sem_inc(acc_free, 1)

                dve.wait_ge(half_done, 3 * l + p + 1)
                out_half(0)
                mean(l, r, 0)
                make_diag(l, r, 0)
                if p == 1:
                    second_half()
                scale(0)
                dve.wait_ge(tmp_made, X_UNITS * (3 * l + p) + 1)
                dve.tensor_tensor(x[:, 0, 0:H], x[:, 0, 0:H], h_out[:, 0, 0:H], ALU.add).then_inc(x_new, 1)
                if p == 2:
                    for i in range(1, X_UNITS):
                        scale(i)
                        if i == 5:
                            second_half()
                        if i == 7:
                            mean(l, r, 1)
                            make_diag(l, r, 1)
                    dve.drain()
                    return
                scale(1)
                if p == 0:
                    lower(c, 0, W8)
                if p == 1:
                    mean(l, r, 1)
                x_lower(l, p + 1, 0, 0)
                if p == 0:
                    second_half()
                scale(2)
                x_lower(l, p + 1, 1, 0)
                scale(3)
                scale(4)
                for i in range(2, X_UNITS):
                    x_lower(l, p + 1, i % KD, i // KD)
                    if i + 3 < X_UNITS:
                        scale(i + 3)
                    if p == 0 and i == 2:
                        mean(l, r, 1)
                    if i == (2 if p == 1 else 3):
                        make_diag(l, r, 1)
                    if i == 6:
                        lower(c + 1, 1, W8)

            def up_out(l, f, m, u, part, banks):
                src = banks[part]
                dve.wait_ge(chunk_done, l * CHUNKS + C_UP[f] + 2 * m + part + 3)
                ins = dve.tensor_tensor((up_a, up_b)[part][:, u, :], src[:], rstd[:], ALU.mult)
                ins.then_inc((a_made, acc_free)[part], 1)

            def up_step(l, f, m, u, next_w, banks=None):
                c, h = l * CHUNKS + C_UP[f] + 2 * m, (2 * l + f) * KF + m
                first, second = (isinstance(m, int) and m == i for i in range(2))
                banks = banks or acc[u]
                if first:
                    pre_norm(l, 4 * f, c + 2, 3)
                up_out(l, f, m, u, 0, banks)
                if not first and not second:
                    lower(c + 2, 0, next_w)
                up_out(l, f, m, u, 1, banks)
                if not first:
                    lower(c + 3, 1, next_w)
                dve.wait_ge(hid_hi_made, h + 1)
                dve.tensor_tensor(hid_lo[:, bass.ds(m, 1), :], up_h[:, u:u + 1, :],
                                  hid_hi[:, bass.ds(m, 1), :].bitcast(F32), ALU.subtract).then_inc(hid_lo_made, 1)

            def out_tile(l, p, n, c_last, u):
                dve.wait_ge(chunk_done, c_last + 3)
                dve.tensor_copy(h_out[:, n, :], acc[u][0][:]).then_inc(h_made, 1)
                dve.wait_ge(h_made, (KD + 1) * (3 * l + p) + n + 1)
                dve.sem_inc(acc_free, 1)

            def ffn(l, f):
                up_step(l, f, 0, 0, W8)
                up_step(l, f, 1, 1, W8)
                up_step(l, f, 2, 0, W8, banks=spare)
                up_step(l, f, 3, 1, W8)
                with dve.Fori(2, KF // 2 - 1) as i:
                    for u in range(2):
                        up_step(l, f, 2 * i + u, u, W8)
                up_step(l, f, KF - 2, 0, W8)
                up_step(l, f, KF - 1, 1, W11)
                for n in range(KD - 1):
                    c = l * CHUNKS + C_DOWN[f] + 2 * n
                    lower(c + 2, 0, W11)
                    out_tile(l, 2 * f, n, c + 1, n % 2)
                    lower(c + 3, 1, W11)
                    if f == 0 and n in state_work:
                        state_work[n](l)
                last_tile(l, 2 * f, l * CHUNKS + C_DOWN[f] + 2 * KD - 1, l * CHUNKS + C_IN)

            def accurate_exp(dst, src, t0, t1, t2):
                V = dve
                V.tensor_scalar(t0, src, -87.3, 88.0, ALU.max, ALU.min)
                V.drain()
                V.tensor_scalar(t1, t0, float(np.log2(np.e)), MAGIC, ALU.mult, ALU.add)
                V.drain()
                V.tensor_scalar(t1, t1, MAGIC, None, ALU.subtract)
                V.drain()
                V.scalar_tensor_tensor(t0, t1, -LN2_HI, t0, ALU.mult, ALU.add)
                V.drain()
                V.scalar_tensor_tensor(t0, t1, -LN2_LO, t0, ALU.mult, ALU.add)
                V.tensor_scalar(smi[:], t1, 127.0, None, ALU.add)
                V.drain()
                V.tensor_scalar(smi[:], smi[:], 23, None, ALU.logical_shift_left)
                V.memset(t2, 1.0 / 40320)
                fact = [5040.0, 720.0, 120.0, 24.0, 6.0, 2.0, 1.0, 1.0]
                for q_ in fact:
                    V.drain()
                    V.tensor_tensor(t2, t2, t0, ALU.mult)
                    V.drain()
                    V.tensor_scalar(t2, t2, 1.0 / q_, None, ALU.add)
                V.tensor_scalar(t1, src, -87.3, None, ALU.is_ge)
                V.drain()
                V.tensor_tensor(t2, t2, smi[:].bitcast(F32), ALU.mult)
                V.drain()
                V.tensor_tensor(dst, t2, t1, ALU.mult)
                V.drain()

            def turns_off(w, k, parts):
                dve.tensor_scalar(k, w, float(1 / TWO_PI), MAGIC, ALU.mult, ALU.add)
                dve.drain()
                dve.tensor_scalar(k, k, MAGIC, None, ALU.subtract)
                for part in parts:
                    dve.drain()
                    dve.scalar_tensor_tensor(w, k, -part, w, ALU.mult, ALU.add)
                dve.drain()

            def S(i):
                return sm[:, i, :]

            def state_dt(l):
                accurate_exp(S(SM_DT), prm[:, PC_LDT:PC_LDT + 8], S(SM_T0), S(SM_T1), S(SM_T2))
                dve.tensor_tensor(S(SM_T3), prm[:, PC_ARE:PC_ARE + 8], S(SM_DT), ALU.mult)
                dve.drain()

            def state_decay(l):
                accurate_exp(S(SM_ER), S(SM_T3), S(SM_T0), S(SM_T1), S(SM_T2))

            def state_angle(l):
                dve.tensor_tensor(S(SM_Y), prm[:, PC_AIM:PC_AIM + 8], S(SM_DT), ALU.mult)
                dve.drain()
                turns_off(S(SM_Y), S(SM_T1), (C1, C2, C3))
                dve.tensor_scalar(S(SM_Y), S(SM_Y), -PI_F, PI_F, ALU.max, ALU.min).then_inc(dt_arg, 1)
                dve.drain()

            def state_weights(l):
                are, aim = prm[:, PC_ARE:PC_ARE + 8], prm[:, PC_AIM:PC_AIM + 8]
                dve.wait_ge(state_landed, 32 * l + 32)
                dve.wait_ge(dt_sin, l + 1)
                V = dve
                V.tensor_scalar(y_hi[:], S(SM_Y), float(1 / TWO_PI), None, ALU.mult)
                V.tensor_tensor(S(SM_T2), S(SM_T1), S(SM_T1), ALU.mult)
                for part, of in ((C1, SM_Y), (C2, SM_YLO), (C3, SM_YLO)):
                    V.drain()
                    V.scalar_tensor_tensor(S(SM_YLO), y_hi[:].bitcast(F32), -part, S(of), ALU.mult, ALU.add)
                V.drain()
                V.tensor_scalar(S(SM_YLO), S(SM_YLO), float(1 / TWO_PI), None, ALU.mult)
                V.drain()
                V.tensor_tensor(S(SM_YT), S(SM_YLO), y_hi[:].bitcast(F32), ALU.add)
                V.tensor_scalar(S(SM_T2), S(SM_T2), -2.0, 1.0, ALU.mult, ALU.add)
                V.drain()
                V.tensor_tensor(S(SM_T2), S(SM_T2), S(SM_ER), ALU.mult)
                V.tensor_tensor(S(SM_T0), S(SM_T0), S(SM_ER), ALU.mult)
                V.drain()
                V.tensor_scalar(S(SM_T2), S(SM_T2), -1.0, None, ALU.add)
                V.tensor_tensor(S(SM_T3), are, are, ALU.mult)
                V.tensor_tensor(S(SM_T4), aim, aim, ALU.mult)
                V.drain()
                V.tensor_tensor(S(SM_T3), S(SM_T3), S(SM_T4), ALU.add)
                V.drain()
                V.reciprocal(S(SM_T3), S(SM_T3))
                V.tensor_tensor(S(SM_T1), S(SM_T2), are, ALU.mult)
                V.tensor_tensor(S(SM_T4), S(SM_T0), aim, ALU.mult)
                V.tensor_tensor(S(SM_T5), S(SM_T0), are, ALU.mult)
                V.drain()
                V.tensor_tensor(S(SM_T1), S(SM_T1), S(SM_T4), ALU.add)
                V.tensor_tensor(S(SM_T2), S(SM_T2), aim, ALU.mult)
                V.drain()
                V.tensor_tensor(S(SM_T5), S(SM_T5), S(SM_T2), ALU.subtract)
                V.tensor_tensor(S(SM_KR), S(SM_T1), S(SM_T3), ALU.mult)
                V.drain()
                V.tensor_tensor(S(SM_KI), S(SM_T5), S(SM_T3), ALU.mult)
                V.drain()
                kr = S(SM_KR).unsqueeze(2).to_broadcast([P, N_STATE_TILES, 32])
                ki = S(SM_KI).unsqueeze(2).to_broadcast([P, N_STATE_TILES, 32])
                scratch = up_a[:, 0, 0:256].rearrange("p (a b) -> p a b", a=N_STATE_TILES)
                V.tensor_tensor(wc2[:, 0], wc[:, 0], kr, ALU.mult)
                V.tensor_tensor(scratch, wc[:, 1], ki, ALU.mult)
                V.tensor_tensor(wc2[:, 1], wc[:, 0], ki, ALU.mult)
                V.drain()
                V.tensor_tensor(wc2[:, 0], wc2[:, 0], scratch, ALU.subtract)
                V.drain()
                V.tensor_tensor(scratch, wc[:, 1], kr, ALU.mult)
                V.drain()
                V.scalar_tensor_tensor(wc2[:, 1], wc2[:, 1], -1.0, scratch, ALU.mult, ALU.subtract)
                V.drain()

            state_work = {1: state_dt, 2: state_decay, 3: state_angle, 5: state_weights}

            with dve.Fori(0, DEPTH) as l:
                dve.tensor_copy(prm[:], params_all[:, bass.ds(l, 1), :].rearrange("p a b -> p (a b)"))
                dve.drain()
                for nrm in (1, 5):
                    a = PC_GAIN + KD * nrm
                    ins = dve.tensor_scalar(prm[:, a:a + KD], prm[:, a:a + KD], 0.5, None, ALU.mult)
                ins.then_inc(prm_ready, 1)
                dve.drain()
                lower(l * CHUNKS, 0, W8)
                for k in range(KD):
                    x_lower(l, 0, k)
                    if k == 4:
                        lower(l * CHUNKS + 1, 1, W8)
                ffn(l, 0)

                def angles(j):
                    if j == 0:
                        dve.wait_ge(time_landed, 16 * l + 16)
                    if j > 1:
                        dve.wait_ge(st_re_made, N_STATE_TILES * l + j - 1)
                        dve.wait_ge(st_im_made, N_STATE_TILES * l + j - 1)
                    w = tab_c[:, j % 2, :]
                    dve.tensor_scalar(tab_k[:], time_f[:], sm[:, SM_YT, j:j + 1], MAGIC, ALU.mult, ALU.add)
                    dve.drain()
                    dve.tensor_scalar(tab_k[:], tab_k[:], MAGIC, None, ALU.subtract)
                    dve.drain()
                    dve.scalar_tensor_tensor(w, time_f[:], y_hi[:, j:j + 1].bitcast(F32), tab_k[:],
                                             ALU.mult, ALU.subtract)
                    dve.drain()
                    dve.scalar_tensor_tensor(w, time_f[:], sm[:, SM_YLO, j:j + 1], w, ALU.mult, ALU.add)
                    dve.drain()
                    dve.tensor_scalar(w, w, -0.5, 0.5, ALU.max, ALU.min).then_inc(tab_arg, 1)

                def scans(j):
                    g = N_STATE_TILES * l + j
                    dve.wait_ge(rt_made, g + 1)
                    decay = sm[:, SM_ER, j:j + 1].to_broadcast([P, SEQ])
                    dve.tensor_tensor_scan(st_re[:], decay, rt_re[:], 0.0, ALU.mult, ALU.add)
                    dve.tensor_tensor_scan(st_im[:], decay, rt_im[:], 0.0, ALU.mult, ALU.add).then_inc(scanned, 1)
                    dve.drain()
                    if j >= POOL_TURNS_FROM:
                        return
                    dve.tensor_tensor(rt_im[:], tab_c[:, j % 2, :], st_im[:], ALU.mult)
                    dve.tensor_tensor(tab_k[:], tab_s[:, j % 2, :], st_re[:], ALU.mult)
                    dve.drain()
                    dve.tensor_tensor(rt_im[:], rt_im[:], tab_k[:], ALU.add).then_inc(st_im_made, 1)

                def sgu_norm():
                    dve.wait_ge(sgu_turned, l + 1)
                    for b in range(TB):
                        dve.tensor_copy(v_tok[:, b, :], (ps6, ps7)[b // 2][:, b % 2 * 2 * P:(b % 2 + 1) * 2 * P])
                    dve.drain()
                    for b in range(TB):
                        dve.bn_stats(lnst[:, b, :], v_tok[:, b, :])
                    dve.drain()
                    for b in range(TB):
                        dve.bn_aggr(lnmv[:, b, :], lnst[:, b, :])
                    dve.drain()
                    dve.tensor_scalar(lnrs[:], lnmv[:, :, 1], LN_EPS, None, ALU.add).then_inc(sgu_var, 1)

                def sgu_bias_add():
                    dve.wait_ge(sgu_mixed, l + 1)
                    for i in range(2):
                        mixed = (ps6, ps7)[i][:].rearrange("p (b n) -> p b n", b=TB)
                        dve.tensor_tensor(sgu_v[:, i, :].rearrange("p (b n) -> p b n", b=TB), mixed,
                                          bsgu[:, i:i + 1, :].to_broadcast([P, TB, P]), ALU.add).then_inc(sgu_biased, 1)

                def lower_of(lo, hi, full, made, value, inc):
                    dve.wait_ge(made, value)
                    dve.tensor_tensor(lo, full, hi.bitcast(F32), ALU.subtract).then_inc(inc, 1)

                def halves(hi, lo, full):
                    dve.tensor_copy(hi, full)
                    dve.drain()
                    return dve.tensor_tensor(lo, full, hi.bitcast(F32), ALU.subtract)

                def rope_angles():
                    dve.wait_ge(small_landed, 96 * l + 96)
                    dve.tensor_copy(rope_c[:], rope_pos[:])
                    dve.drain()
                    dve.tensor_scalar(rope_c[:], rope_c[:], invf[:, 0:1], None, ALU.mult)
                    dve.drain()
                    turns_off(rope_c[:], att_e[:].rearrange("p a b -> p (a b)"), (C1, C2, C3))
                    dve.tensor_scalar(rope_c[:], rope_c[:], -PI_F, PI_F, ALU.max, ALU.min).then_inc(rope_ang, 1)

                def rope(i):
                    if i == 0:
                        dve.wait_ge(rope_sin, l + 1)
                        dve.tensor_scalar(rope_c[:], rope_c[:], -2.0, 1.0, ALU.mult, ALU.add)
                        dve.drain()
                    def by_chunk(a):
                        return a.rearrange("p (c q) -> p c q", c=N_WIN)
                    z = by_chunk(k_pad[:, CHUNK:]) if i == 0 else q[:, :, i - 1, :]
                    t_ = by_chunk(att_e[:].rearrange("p a b -> p (a b)"))
                    dve.wait_ge(rotated, 5 * l + i + 1)
                    dve.tensor_tensor(t_, by_chunk((ps6, ps7)[i % 2][:]), by_chunk(rope_s[:]), ALU.mult)
                    dve.tensor_tensor(z, z, by_chunk(rope_c[:]), ALU.mult)
                    dve.drain()
                    dve.tensor_tensor(z, z, t_, ALU.add).then_inc(roped, 1)
                    dve.drain()

                def conv(i):
                    w = PC_CONV + i
                    y = conv3[:, 0, :]
                    dve.tensor_tensor(conv_pad[:, 2:2 + SEQ], conv3[:, 1, :], conv3[:, 0, :], ALU.mult)
                    dve.drain()
                    dve.tensor_scalar(y, conv_pad[:, 0:SEQ], prm[:, w:w + 1], None, ALU.mult)
                    for tap in (1, 2):
                        dve.drain()
                        dve.scalar_tensor_tensor(y, conv_pad[:, tap:tap + SEQ], prm[:, w + 2 * tap:w + 2 * tap + 1], y,
                                                 ALU.mult, ALU.add)
                    dve.drain()
                    dve.tensor_tensor(y, y, conv3[:, 2, :], ALU.mult)
                    dve.drain()
                    halves(conv_hi[:, i, :], conv_lo[:, i, :], y).then_inc(conv_lo_made, 1)

                def shift_scores(c):
                    g = N_WIN * l + c
                    k0 = CHUNK if c == 0 else 0
                    s4 = ps6[:].rearrange("p (j k) -> p j k", j=4)[:, :, k0:]
                    sink = prm[:, PC_SINK:PC_SINK + 4]
                    dve.wait_ge(scored, g + 1)
                    if c:
                        dve.wait_ge(turned, g)
                    else:
                        dve.memset(att_e[:, :, 0:CHUNK], 0.0)
                    dve.tensor_reduce(asm[:, 0, :], s4, AX.X, ALU.max)
                    dve.drain()
                    dve.scalar_tensor_tensor(asm[:, 1, :], asm[:, 0, :], HEAD_DIM ** -0.5, sink, ALU.mult, ALU.max)
                    dve.drain()
                    dve.tensor_tensor(asm[:, 2, :], sink, asm[:, 1, :], ALU.subtract)
                    dve.scalar_tensor_tensor(att_e[:, :, k0:], s4, HEAD_DIM ** -0.5,
                                             asm[:, 1, :].unsqueeze(2).to_broadcast([P, 4, P - k0]),
                                             ALU.mult, ALU.subtract).then_inc(shifted, 1)

                def make_probs(c):
                    g = N_WIN * l + c
                    dve.wait_ge(exped, g + 1)
                    dve.tensor_reduce(asm[:, 4, :], att_e[:], AX.X, ALU.add)
                    dve.drain()
                    dve.tensor_tensor(asm[:, 4, :], asm[:, 4, :], asm[:, 3, :], ALU.add)
                    dve.drain()
                    dve.reciprocal(asm[:, 5, :], asm[:, 4, :])
                    dve.drain()
                    dve.tensor_tensor(att_e[:], att_e[:], asm[:, 5, :].unsqueeze(2).to_broadcast([P, 4, P]), ALU.mult)\
                       .then_inc(probs_made, 1)

                def attention_out(c):
                    dve.wait_ge(att_out, N_WIN * l + c + 1)
                    halves(att_hi[:, c], att_lo[:, c], ps7[:, 0:2 * P].rearrange("p (t q) -> p t q", t=4))\
                        .then_inc(att_lo_made, 1)

                def ssm_result(i):
                    dve.wait_ge(y_mul, N_STATE_TILES * l + 4 * i + 4)
                    dve.scalar_tensor_tensor(u_ssm[:, i, :], u_ssm[:, i, :], prm[:, PC_D + i:PC_D + i + 1], ps_y[:],
                                             ALU.mult, ALU.add).then_inc(y_out, 1)

                def side_work(t):
                    if t - 1 in T_SSM:
                        scans(T_SSM[t - 1])
                    if att_group(t - 3) is not None:
                        attention_out(att_group(t - 3))
                    if att_group(t - 1) is not None:
                        make_probs(att_group(t - 1))
                    if att_group(t) is not None:
                        shift_scores(att_group(t))
                    if t in T_ANGLES:
                        angles(T_ANGLES[t])
                    if t == T_SGU_TURN - 1:
                        sgu_norm()
                    if t == T_SGU_TURN:
                        dve.memset(wsgu[CHUNK:P, :, 0:CHUNK], 0.0)
                    if t == T_SGU_MIX - 1:
                        sgu_bias_add()
                    if t == T_SGU_GATE + 5:
                        for i in range(2):
                            lower_of(sgu_lo[:, i, :], sgu_hi[:, i, :], sgu_u[:, i, :], sgu_hi_made, 2 * l + i + 1,
                                     sgu_lo_made)
                    if t == 3:
                        rope_angles()
                    for i in T_ROPE.get(t + 1, ()):
                        rope(i)
                    if t in T_CONV:
                        conv(T_CONV[t])
                    if t in T_SSM_OUT:
                        ssm_result(T_SSM_OUT[t])
                    if t == T_GLU + 1:
                        for i in range(2):
                            lower_of(ssm_lo[:, i, :], ssm_hi[:, i, :], u_ssm[:, i, :], ssm_hi_made, 2 * l + i + 1,
                                     ssm_lo_made)

                for pad in (k_pad, v_pad):
                    dve.memset(pad[:, 0:CHUNK], 0.0)
                dve.memset(conv_pad[:, 0:2], 0.0)
                in_place = {"ssm": (u_ssm, u_ready), "sgu_v": (sgu_v, sgu_z), "sgu_u": (sgu_u, sgu_z),
                            "k": (k_pad, qk_ready), "v": (v_pad, qk_ready), "q": (q, qk_ready)}
                for s, (name, tile) in enumerate(W_IN_TILES):
                    if name in ("k", "v"):
                        dst = in_place[name][0][:, CHUNK:]
                    elif name in in_place and name != "q":
                        dst = in_place[name][0][:, tile, :]
                    elif name != "q":
                        dst = conv3[:, ("cx", "cc", "cb").index(name), :]
                    if s == 0:
                        pre_norm(l, 2, l * CHUNKS + C_IN + 2, 2)
                    dve.drain()
                    dve.wait_ge(chunk_done, l * CHUNKS + C_IN + s + 3)
                    src, r_ = in_bank[s][:], rstd[:]
                    if name == "q":
                        dst = q[:, :, tile, :]
                        src, r_ = (a.rearrange("p (c q) -> p c q", c=N_WIN) for a in (src, r_))
                    dve.tensor_tensor(dst, src, r_, ALU.mult).then_inc(acc_free, 1)
                    dve.drain()
                    if name in in_place:
                        dve.sem_inc(in_place[name][1], 1)
                    if s >= 2:
                        lower(l * CHUNKS + C_IN + s + 2, s % 2, W8 if s < N_IN - 2 else MIX_W[0])
                    side_work(s)

                def merged_lower(n):
                    lower_of(mrg_lo[:, n, :], mrg_hi[:, n, :], merged[:, n, :], mrg_hi_made, KD * l + n + 1, mrg_lo_made)

                for s in range(4 * KD):
                    b, n, u = s // KD, s % KD, s % 2
                    nb = (s + 2) // KD
                    g = 4 * KD * l + s
                    dve.wait_ge(chunk_done, l * CHUNKS + C_MIX + s + 3)
                    dve.tensor_tensor(gate_in[:, u, :], acc[u][0][:], rstd[:], ALU.mult).then_inc(gate_scaled, 1)
                    lower(l * CHUNKS + C_MIX + s + 2, u, MIX_W[nb] if nb < 4 else W8)
                    dve.drain()
                    dve.wait_ge(gate_made, g + 1)
                    dst = merged[:, n, :] if b == CONV else gate[:, u, :]
                    dve.tensor_tensor(dst, gate[:, u, :], acc[u][1][:], ALU.mult).then_inc(gated, 1)
                    dve.wait_ge(gated, g + 1)
                    dve.sem_inc(acc_free, 1)
                    side_work(N_IN + s)
                    if b == SSM and n:
                        merged_lower(n - 1)
                merged_lower(KD - 1)
                for n in range(KD - 1):
                    out_tile(l, 1, n, l * CHUNKS + C_OUT + n, n % 2)
                    lower(l * CHUNKS + C_OUT + n + 2, n % 2, W8)
                last_tile(l, 1, l * CHUNKS + C_OUT + KD - 1, l * CHUNKS + C_UP[1])
                ffn(l, 1)


def _tiles(w, k):
    lead = w.shape[:-2]
    n = w.shape[-1] // P
    w = w.reshape(*lead, k, P, n, P)
    m = len(lead)
    w = w.transpose(*range(m), m + 2, m + 1, m, m + 3)
    return np.ascontiguousarray(w).reshape(*lead, n, P, k * P)


def _columns(v):
    v = v.reshape(*v.shape[:-1], v.shape[-1] // P, P)
    return np.moveaxis(v, -1, 0)


def _layout(x, positions, norm_gains, ffn_w1, ffn_w3, ffn_w2, w_in, attn_sinks, ssm_a_re, ssm_a_im, ssm_log_dt,
            ssm_b_re, ssm_b_im, ssm_c_re, ssm_c_im, ssm_d, ssm_glu_w, sgu_ln_g, sgu_ln_b, sgu_w, sgu_b, conv_w,
            w_branch, w_gate, b_gate, w_out):
    L = DEPTH
    head_order = np.array([64 * (4 * kv + t) + d for t in range(4) for kv in range(2) for d in range(64)])
    cols = []
    for name, tile in W_IN_TILES:
        base = W_IN_COLS[name]
        own = head_order if name == "q" else np.arange(2 * P)
        cols.append(base + own[tile * P:(tile + 1) * P])
    win = _tiles(w_in[:, :, np.concatenate(cols)], KD).reshape(L * N_IN, P, W8)
    up = np.stack([_tiles(ffn_w1, KD), _tiles(ffn_w3, KD)], axis=3).reshape(L * 2 * UP_CH, P, W8)
    down = _tiles(ffn_w2, KF).reshape(L, 2, KD, P, 2, W11).transpose(0, 1, 2, 4, 3, 5)
    down = np.ascontiguousarray(down).reshape(L * 2 * DOWN_CH, P, W11)
    mix = []
    for b in range(4):
        rows = BRANCH_ROW0[b] + (head_order if b == ATT else np.arange(BRANCH_K[b] * P))
        g = _tiles(w_gate[:, :, REF_BRANCH[b], :], KD)
        w = _tiles(w_branch[:, rows, :], BRANCH_K[b])
        mix.append(np.concatenate([g, w], axis=-1).reshape(L * KD, P, MIX_W[b]))
    prm = np.zeros((P, L, PC_N), np.float32)
    prm[:, :, PC_GAIN:PC_GAIN + 48] = _columns(norm_gains).reshape(P, L, 48)
    prm[:, :, PC_BGATE:PC_BGATE + 32] = _columns(b_gate[:, list(REF_BRANCH), :]).reshape(P, L, 32)
    for col, a in ((PC_ARE, ssm_a_re), (PC_AIM, ssm_a_im), (PC_LDT, np.repeat(ssm_log_dt[:, :, None], 64, axis=2))):
        prm[:, :, col:col + 8] = _columns(a.reshape(L, 1024))
    prm[:, :, PC_D:PC_D + 2] = _columns(ssm_d)
    prm[:, :, PC_CONV:PC_CONV + 6] = _columns(conv_w).reshape(P, L, 6)
    sink = attn_sinks.reshape(L, 2, 2, 2).transpose(3, 0, 1, 2).reshape(2, L, 4)
    prm[:, :, PC_SINK:PC_SINK + 4] = np.repeat(sink, 64, axis=0)
    sb = np.zeros((L, P, 2, 2, P), np.float32)
    sc = np.zeros((L, P, 2, N_STATE_TILES, 32), np.float32)
    for g in range(16):
        j, h = g // 2, g % 2
        r = 32 * (j % 4) + 16 * h
        for part, (b, c) in enumerate(((ssm_b_re, ssm_c_re), (ssm_b_im, ssm_c_im))):
            sb[:, r:r + 16, j // 4, part, 64 * h:64 * h + 64] = b[:, g].transpose(0, 2, 1)
            sc[:, 64 * h:64 * h + 64, part, j, 16 * h:16 * h + 16] = c[:, g].transpose(0, 2, 1)
    glu = np.ascontiguousarray(ssm_glu_w.reshape(L, 2, P, 2 * P).transpose(0, 2, 1, 3))
    sgw = np.ascontiguousarray(sgu_w.transpose(0, 3, 1, 2))
    sgb = np.repeat(sgu_b.reshape(L, 2, 2, P).transpose(0, 2, 1, 3), 64, axis=1)
    rot = np.zeros((P, P), np.float32)
    invf = np.zeros((P, 1), np.float32)
    freq = np.float32(ROPE_THETA) ** (-np.arange(0, ROT_DIM, 2, dtype=np.float32) / ROT_DIM)
    half = ROT_DIM // 2
    for h0 in (0, HEAD_DIM):
        for i in range(half):
            rot[h0 + half + i, h0 + i] = -1.0
            rot[h0 + i, h0 + half + i] = 1.0
            invf[h0 + i] = invf[h0 + half + i] = freq[i]
    return {
        "x_in": np.ascontiguousarray(x[0].T.reshape(KD, P, SEQ).transpose(1, 0, 2)),
        "pos_in": positions,
        "params_in": prm, "w_up": up, "w_down": down, "w_in": win,
        "w_conv": mix[0], "w_sgu": mix[1], "w_att": mix[2], "w_ssm": mix[3],
        "w_out": _tiles(w_out, KD).reshape(L * OUT_CH, P, W8),
        "ssm_b": sb, "ssm_c": sc, "glu_w": glu, "sgu_w": sgw, "sgu_bias": np.ascontiguousarray(sgb),
        "ln_rows": np.stack([sgu_ln_g, sgu_ln_b], axis=1),
        "consts_in": np.concatenate([np.eye(P, dtype=np.float32), rot, invf], axis=1),
        "time_in": np.tile(np.arange(SEQ, dtype=np.float32), (P, 1)),
    }


def kernel(**inputs):
    import concourse.bacc as _bacc
    from concourse.bass_utils import run_bass_kernel_spmd as _run

    arrays = _layout(**{n: np.asarray(a) for n, a in inputs.items()})
    nc = _bacc.Bacc("TRN2", target_bir_lowering=False, num_devices=1)
    aps = {n: nc.dram_tensor(n, a.shape, mybir.dt.from_np(a.dtype), kind="ExternalInput").ap()
           for n, a in arrays.items()}
    out = nc.dram_tensor("out", (P, KD, SEQ), F32, kind="ExternalOutput").ap()
    build_encoder(nc, **aps, out=out)
    got = _run(nc, [arrays], core_ids=[0]).results[0]["out"]
    return np.ascontiguousarray(got.transpose(1, 0, 2).reshape(D_MODEL, SEQ).T)[None]
```
